# Optimizing a Trainium2 kernel written in Bass

```python
import jax, jax.numpy as jnp
from jax import lax
import numpy as np
import math

D_MODEL = 1024
BATCH = 1
SEQ = 512
DEPTH = 1

CHUNK = 64
Q_BLOCK = 128
ATTN_HEADS = 8
HEAD_DIM = 64
ATTN_WIDTH = ATTN_HEADS * HEAD_DIM
CONV_WIDTH = D_MODEL - ATTN_WIDTH
CONV_GROUPS = 8
CONV_KERNEL = 31
IDX_HEADS = 8
IDX_DIM = 64
TOPK_MAX = 256
ROT_DIM = HEAD_DIM // 4
ROPE_THETA = 500000.0
D_FF = 4 * D_MODEL
N_MOD = 6
EPS = 1e-6
IN_SIZES = (ATTN_WIDTH, ATTN_WIDTH, ATTN_WIDTH, IDX_HEADS * IDX_DIM, IDX_DIM, IDX_HEADS, CONV_WIDTH, CONV_WIDTH)
IN_COLS = 3 * ATTN_WIDTH + IDX_HEADS * IDX_DIM + IDX_DIM + IDX_HEADS + 2 * CONV_WIDTH


def _split_points():
    pts, acc = [], 0
    for s in IN_SIZES[:-1]:
        acc += s
        pts.append(acc)
    return pts

def rms_norm(x, g):
    xf = x.astype(jnp.float32)
    y = xf * lax.rsqrt(jnp.mean(xf * xf, axis=-1, keepdims=True) + EPS)
    return (y * g.astype(jnp.float32)).astype(x.dtype)

def layer_norm(x, g, b):
    xf = x.astype(jnp.float32)
    mu = jnp.mean(xf, axis=-1, keepdims=True)
    var = jnp.mean(jnp.square(xf - mu), axis=-1, keepdims=True)
    y = (xf - mu) * lax.rsqrt(var + EPS)
    return (y * g.astype(jnp.float32) + b.astype(jnp.float32)).astype(x.dtype)

def rope_tables(seq_len, dtype):
    pos = jnp.arange(seq_len, dtype=jnp.float32)
    inv_freq = ROPE_THETA ** (-jnp.arange(0, ROT_DIM, 2, dtype=jnp.float32) / ROT_DIM)
    ang = pos[:, None] * inv_freq[None, :]
    return jnp.cos(ang).astype(dtype), jnp.sin(ang).astype(dtype)

def partial_rope(x, cos, sin):
    half = ROT_DIM // 2
    x1 = x[..., :half]
    x2 = x[..., half:ROT_DIM]
    c = cos[None, :, None, :]
    s = sin[None, :, None, :]
    return jnp.concatenate([x1 * c - x2 * s, x2 * c + x1 * s, x[..., ROT_DIM:]], axis=-1)

def dsa_sparse_attention(q, k, v, iq, ik, iw):
    B, S, H, dh = q.shape
    n_blk = S // Q_BLOCK
    top_k = min(TOPK_MAX, S // 4)
    key_chunk = jnp.arange(S) // CHUNK
    ik_f = ik.astype(jnp.float32)

    def block(i):
        start = i * Q_BLOCK
        q_b = lax.dynamic_slice_in_dim(q, start, Q_BLOCK, axis=1)
        iq_b = lax.dynamic_slice_in_dim(iq, start, Q_BLOCK, axis=1).astype(jnp.float32)
        iw_b = lax.dynamic_slice_in_dim(iw, start, Q_BLOCK, axis=1).astype(jnp.float32)
        q_chunk = (start + jnp.arange(Q_BLOCK)) // CHUNK
        admissible = key_chunk[None, :] <= q_chunk[:, None]
        rel = jax.nn.relu(jnp.einsum('bthd,bsd->bths', iq_b, ik_f) * (IDX_DIM ** -0.5))
        score = jnp.einsum('bths,bth->bts', rel, iw_b)
        score = jnp.where(admissible[None], score, -jnp.inf)
        _, idx = lax.top_k(score, top_k)
        valid = key_chunk[idx] <= q_chunk[None, :, None]
        k_sel = jax.vmap(lambda kb, ib: kb[ib])(k, idx)
        v_sel = jax.vmap(lambda vb, ib: vb[ib])(v, idx)
        logits = jnp.einsum('bthd,btkhd->bthk', q_b, k_sel).astype(jnp.float32) * (dh ** -0.5)
        logits = jnp.where(valid[:, :, None, :], logits, -jnp.inf)
        p = jax.nn.softmax(logits, axis=-1).astype(v.dtype)
        return jnp.einsum('bthk,btkhd->bthd', p, v_sel)

    out = lax.map(block, jnp.arange(n_blk))
    return jnp.transpose(out, (1, 0, 2, 3, 4)).reshape(B, S, H * dh)

def conformer_conv(a, g, w_dw, b_dw, ln_g, ln_b):
    u = a * jax.nn.sigmoid(g)
    u = jnp.pad(u, ((0, 0), (CONV_KERNEL - 1, 0), (0, 0)))
    y = lax.conv_general_dilated(u, w_dw[:, None, :], window_strides=(1,), padding='VALID',
                                 dimension_numbers=('NWC', 'WIO', 'NWC'),
                                 feature_group_count=CONV_WIDTH) + b_dw
    y = layer_norm(y, ln_g, ln_b)
    return jax.nn.silu(y)

def first_inputs(seed: int = 0) -> dict:
    key = jax.random.key(seed)
    ks = jax.random.split(key, 20)

    def nrm(k, shape, scale):
        return jax.random.normal(k, shape, jnp.float32) * scale

    L = DEPTH
    return {
        "x": nrm(ks[0], (BATCH, SEQ, D_MODEL), 1.0),
        "c": nrm(ks[1], (BATCH, D_MODEL), 1.0),
        "w_ada": nrm(ks[2], (L, D_MODEL, N_MOD * D_MODEL), 0.5 * D_MODEL ** -0.5),
        "b_ada": nrm(ks[3], (L, N_MOD * D_MODEL), 0.02),
        "g_norm1": 1.0 + nrm(ks[4], (L, D_MODEL), 0.02),
        "w_in": nrm(ks[5], (L, D_MODEL, IN_COLS), D_MODEL ** -0.5),
        "g_q": 1.0 + nrm(ks[6], (L, HEAD_DIM), 0.02),
        "g_k": 1.0 + nrm(ks[7], (L, HEAD_DIM), 0.02),
        "w_dw": nrm(ks[8], (L, CONV_KERNEL, CONV_WIDTH), CONV_KERNEL ** -0.5),
        "b_dw": nrm(ks[9], (L, CONV_WIDTH), 0.02),
        "g_conv_ln": 1.0 + nrm(ks[10], (L, CONV_WIDTH), 0.02),
        "b_conv_ln": nrm(ks[11], (L, CONV_WIDTH), 0.02),
        "g_out_attn": 1.0 + nrm(ks[12], (L, ATTN_WIDTH), 0.02),
        "g_out_conv": 1.0 + nrm(ks[13], (L, CONV_WIDTH), 0.02),
        "w_out": nrm(ks[14], (L, D_MODEL, D_MODEL), D_MODEL ** -0.5),
        "g_norm2": 1.0 + nrm(ks[15], (L, D_MODEL), 0.02),
        "w_ff1": nrm(ks[16], (L, D_MODEL, D_FF), D_MODEL ** -0.5),
        "w_ff2": nrm(ks[17], (L, D_FF, D_MODEL), D_FF ** -0.5),
    }

def first_block(x, c, w_ada, b_ada, g_norm1, w_in, g_q, g_k, w_dw, b_dw, g_conv_ln, b_conv_ln,
              g_out_attn, g_out_conv, w_out, g_norm2, w_ff1, w_ff2):
    B, S, _ = x.shape
    cos, sin = rope_tables(S, x.dtype)
    c_act = jax.nn.silu(c)
    split_pts = _split_points()
    for l in range(DEPTH):
        mod = (c_act @ w_ada[l] + b_ada[l])[:, None, :]
        sh1, sc1, gt1, sh2, sc2, gt2 = jnp.split(mod, N_MOD, axis=-1)

        h = rms_norm(x, g_norm1[l]) * (1.0 + sc1) + sh1
        u = h @ w_in[l]
        q, k, v, iq, ik, iw, ca, cg = jnp.split(u, split_pts, axis=-1)
        q = partial_rope(rms_norm(q.reshape(B, S, ATTN_HEADS, HEAD_DIM), g_q[l]), cos, sin)
        k = partial_rope(rms_norm(k.reshape(B, S, ATTN_HEADS, HEAD_DIM), g_k[l]), cos, sin)
        v = v.reshape(B, S, ATTN_HEADS, HEAD_DIM)
        iq = partial_rope(iq.reshape(B, S, IDX_HEADS, IDX_DIM), cos, sin)
        ik = partial_rope(ik.reshape(B, S, 1, IDX_DIM), cos, sin)[:, :, 0, :]
        iw = iw * (IDX_HEADS ** -0.5)
        attn = dsa_sparse_attention(q, k, v, iq, ik, iw)
        conv = conformer_conv(ca, cg, w_dw[l], b_dw[l], g_conv_ln[l], b_conv_ln[l])
        mixed = jnp.concatenate([rms_norm(attn, g_out_attn[l]), rms_norm(conv, g_out_conv[l])], axis=-1)
        x = x + gt1 * (mixed @ w_out[l])

        h2 = rms_norm(x, g_norm2[l]) * (1.0 + sc2) + sh2
        f = jnp.square(jax.nn.relu(h2 @ w_ff1[l])) @ w_ff2[l]
        x = x + gt2 * f
    return x


_first_inputs = first_inputs


def first_inputs(seed=0):
    import zlib

    import numpy as np

    out = dict(_first_inputs(seed))
    spreads = {}
    factors = {'g_norm1': 4.627,
     'g_q': 8.0,
     'g_k': 8.0,
     'b_dw': 7.529,
     'g_conv_ln': 8.0,
     'b_conv_ln': 8.0,
     'g_out_attn': 8.0,
     'g_out_conv': 8.0,
     'g_norm2': 6.851}
    for name, (base, spread) in spreads.items():
        noise = np.random.default_rng([zlib.crc32(name.encode()), seed]).standard_normal(out[name].shape)
        drawn = base * np.exp(spread * noise) if base else spread * noise
        out[name] = __import__('jax').numpy.asarray(drawn.astype(out[name].dtype))
    for name, factor in factors.items():
        out[name] = (out[name] * factor).astype(out[name].dtype)
    return out


_narrow_inputs = first_inputs


def first_inputs(seed=0):

    out = dict(_narrow_inputs(seed))
    wider = {'g_conv_ln': 4.02, 'b_conv_ln': 4.08, 'g_out_attn': 4.34, 'g_out_conv': 4.28}
    for name, times in wider.items():
        mean = out[name].mean()
        out[name] = (mean + times * (out[name] - mean)).astype(out[name].dtype)
    return out


FOX_HEADS = 8
FOX_HEAD_DIM = 64
FOX_WIDTH = FOX_HEADS * FOX_HEAD_DIM
MLSTM_HEADS = 4
MLSTM_INNER = D_MODEL
MLSTM_V_DIM = MLSTM_INNER // MLSTM_HEADS
MLSTM_QK_DIM = MLSTM_V_DIM // 2
CONV_WIDTH_2 = 4
D_FF_2 = -(-(8 * D_MODEL) // (3 * 256)) * 256
FOX_FORGET_BIAS = 3.0
MLSTM_FORGET_BIAS = 3.0
LN_EPS = 1e-5
IN_SPLITS = (FOX_WIDTH, FOX_WIDTH, FOX_WIDTH, FOX_HEADS,
             MLSTM_INNER, MLSTM_INNER, MLSTM_HEADS, MLSTM_HEADS, MLSTM_INNER,
             D_MODEL, D_MODEL)
D_IN = sum(IN_SPLITS)


def _ln(x, g=None, b=None):
    xf = x.astype(jnp.float32)
    mu = jnp.mean(xf, axis=-1, keepdims=True)
    var = jnp.mean(jnp.square(xf - mu), axis=-1, keepdims=True)
    y = ((xf - mu) * lax.rsqrt(var + LN_EPS)).astype(x.dtype)
    if g is not None:
        y = y * g + b
    return y

def _forgetting_attention(q, k, v, f_logit):
    B, S, H, d = q.shape
    log_f = jax.nn.log_sigmoid(f_logit.astype(jnp.float32))
    F = jnp.cumsum(log_f, axis=1).transpose(0, 2, 1)
    q = q.transpose(0, 2, 1, 3)
    k = k.transpose(0, 2, 1, 3)
    v = v.transpose(0, 2, 1, 3)
    scale = d ** -0.5
    outs = []
    for start in range(0, S, Q_BLOCK):
        end = start + Q_BLOCK
        logits = jnp.einsum('bhqd,bhkd->bhqk', q[:, :, start:end], k[:, :, :end]).astype(jnp.float32) * scale
        logits = logits + F[:, :, start:end, None] - F[:, :, None, :end]
        q_pos = jnp.arange(start, end)[:, None]
        k_pos = jnp.arange(end)[None, :]
        logits = jnp.where(k_pos <= q_pos, logits, -jnp.inf)
        p = jax.nn.softmax(logits, axis=-1).astype(v.dtype)
        outs.append(jnp.einsum('bhqk,bhkd->bhqd', p, v[:, :, :end]))
    o = jnp.concatenate(outs, axis=2)
    return o.transpose(0, 2, 1, 3).reshape(B, S, H * d)

def _mlstm_chunkwise(q, k, v, i_pre, f_pre):
    out_dtype = v.dtype
    B, S, H, dk = q.shape
    dv = v.shape[-1]
    NC, L = S // CHUNK, CHUNK
    f32 = jnp.float32
    q = (q.astype(f32) * dk ** -0.5).reshape(B, NC, L, H, dk).transpose(0, 3, 1, 2, 4)
    k = k.astype(f32).reshape(B, NC, L, H, dk).transpose(0, 3, 1, 2, 4)
    v = v.astype(f32).reshape(B, NC, L, H, dv).transpose(0, 3, 1, 2, 4)
    ig = i_pre.astype(f32).reshape(B, NC, L, H).transpose(0, 3, 1, 2)
    lf = jax.nn.log_sigmoid(f_pre.astype(f32)).reshape(B, NC, L, H).transpose(0, 3, 1, 2)
    b = jnp.cumsum(lf, axis=-1)
    g = b[..., -1]
    a = g[..., None] - b + ig

    def step(carry, xs):
        C, n, m = carry
        k_c, v_c, a_c, g_c = xs
        m_new = jnp.maximum(g_c + m, jnp.max(a_c, axis=-1))
        decay = jnp.exp(g_c + m - m_new)
        w = jnp.exp(a_c - m_new[..., None])
        C_new = decay[..., None, None] * C + jnp.einsum('bhl,bhlk,bhlv->bhkv', w, k_c, v_c)
        n_new = decay[..., None] * n + jnp.einsum('bhl,bhlk->bhk', w, k_c)
        return (C_new, n_new, m_new), (C, n, m)

    init = (jnp.zeros((B, H, dk, dv), f32), jnp.zeros((B, H, dk), f32), jnp.zeros((B, H), f32))
    xs = (k.transpose(2, 0, 1, 3, 4), v.transpose(2, 0, 1, 3, 4),
          a.transpose(2, 0, 1, 3), g.transpose(2, 0, 1))
    _, (C_prev, n_prev, m_prev) = lax.scan(step, init, xs)
    C_prev = C_prev.transpose(1, 2, 0, 3, 4)
    n_prev = n_prev.transpose(1, 2, 0, 3)
    m_prev = m_prev.transpose(1, 2, 0)

    causal = jnp.tril(jnp.ones((L, L), dtype=bool))
    D = jnp.where(causal, b[..., :, None] - b[..., None, :] + ig[..., None, :], -jnp.inf)
    inter = b + m_prev[..., None]
    m_t = jnp.maximum(inter, jnp.max(D, axis=-1))
    scores = jnp.einsum('bhcld,bhcsd->bhcls', q, k) * jnp.exp(D - m_t[..., None])
    w_inter = jnp.exp(inter - m_t)
    num = (w_inter[..., None] * jnp.einsum('bhcld,bhcdv->bhclv', q, C_prev)
           + jnp.einsum('bhcls,bhcsv->bhclv', scores, v))
    den = w_inter * jnp.einsum('bhcld,bhcd->bhcl', q, n_prev) + jnp.sum(scores, axis=-1)
    h = num / jnp.maximum(jnp.abs(den), jnp.exp(-m_t))[..., None]
    return h.transpose(0, 2, 3, 1, 4).reshape(B, S, H * dv).astype(out_dtype)

def _causal_depthwise_conv(u, w, b):
    out = lax.conv_general_dilated(u, w[:, None, :], window_strides=(1,),
                                   padding=[(CONV_WIDTH_2 - 1, 0)],
                                   dimension_numbers=('NWC', 'WIO', 'NWC'),
                                   feature_group_count=u.shape[-1])
    return out + b

def _head_norm(h, g, n_heads):
    B, S, W = h.shape
    return _ln(h.reshape(B, S, n_heads, W // n_heads)).reshape(B, S, W) * g

def _hybrid_mixer(h, w_in, b_in, conv_w, conv_b, w_mq, w_mk, mh_norm_g, w_pa, w_pb, w_out):
    B, S, _ = h.shape
    proj = jnp.einsum('bsd,de->bse', h, w_in) + b_in
    fq, fk, fv, ff, mu, mv, mi, mf, mo, ga, gb = jnp.split(
        proj, np.cumsum(IN_SPLITS)[:-1].tolist(), axis=-1)
    shp = (B, S, FOX_HEADS, FOX_HEAD_DIM)
    att = _forgetting_attention(fq.reshape(shp), fk.reshape(shp), fv.reshape(shp), ff)
    u = jax.nn.silu(_causal_depthwise_conv(mu, conv_w, conv_b))
    uh = u.reshape(B, S, MLSTM_HEADS, MLSTM_V_DIM)
    mq = jnp.einsum('bshi,hik->bshk', uh, w_mq)
    mk = jnp.einsum('bshi,hik->bshk', uh, w_mk)
    hm = _mlstm_chunkwise(mq, mk, mv.reshape(B, S, MLSTM_HEADS, MLSTM_V_DIM), mi, mf)
    hm = _head_norm(hm, mh_norm_g, MLSTM_HEADS) * jax.nn.sigmoid(mo)
    y = (jax.nn.sigmoid(ga) * jnp.einsum('bsi,id->bsd', att, w_pa)
         + jax.nn.sigmoid(gb) * jnp.einsum('bsi,id->bsd', hm, w_pb))
    return jnp.einsum('bsd,de->bse', y, w_out)

def _swiglu(h, w_ffn_in, w_ffn_down):
    gate, up = jnp.split(jnp.einsum('bsd,df->bsf', h, w_ffn_in), 2, axis=-1)
    return jnp.einsum('bsf,fd->bsd', jax.nn.silu(gate) * up, w_ffn_down)

def second_inputs(seed: int = 0) -> dict:
    key = jax.random.key(seed)
    ks = jax.random.split(key, 24)
    f32 = jnp.float32
    beta = (8.0 * DEPTH) ** -0.25
    nrm = lambda k, shape, s: jax.random.normal(k, shape, f32) * s
    ada_offset = jnp.concatenate([jnp.zeros((2 * D_MODEL,), f32), jnp.ones((D_MODEL,), f32),
                                  jnp.zeros((2 * D_MODEL,), f32), jnp.ones((D_MODEL,), f32)])
    parts = [jnp.zeros((n,), f32) for n in IN_SPLITS]
    parts[3] = jnp.full((FOX_HEADS,), FOX_FORGET_BIAS, f32)
    parts[7] = jnp.full((MLSTM_HEADS,), MLSTM_FORGET_BIAS, f32)
    in_offset = jnp.concatenate(parts)
    return {
        "x": nrm(ks[0], (BATCH, SEQ, D_MODEL), 1.0),
        "c": nrm(ks[1], (BATCH, D_MODEL), 1.0),
        "w_ada": nrm(ks[2], (DEPTH, D_MODEL, 6 * D_MODEL), 0.3 * D_MODEL ** -0.5),
        "b_ada": nrm(ks[3], (DEPTH, 6 * D_MODEL), 0.02) + ada_offset,
        "w_in": nrm(ks[4], (DEPTH, D_MODEL, D_IN), D_MODEL ** -0.5),
        "b_in": nrm(ks[5], (DEPTH, D_IN), 0.02) + in_offset,
        "conv_w": nrm(ks[6], (DEPTH, CONV_WIDTH_2, MLSTM_INNER), CONV_WIDTH_2 ** -0.5),
        "conv_b": nrm(ks[7], (DEPTH, MLSTM_INNER), 0.02),
        "w_mq": nrm(ks[8], (DEPTH, MLSTM_HEADS, MLSTM_V_DIM, MLSTM_QK_DIM), MLSTM_V_DIM ** -0.5),
        "w_mk": nrm(ks[9], (DEPTH, MLSTM_HEADS, MLSTM_V_DIM, MLSTM_QK_DIM), MLSTM_V_DIM ** -0.5),
        "mh_norm_g": 1.0 + nrm(ks[10], (DEPTH, MLSTM_INNER), 0.02),
        "w_pa": nrm(ks[11], (DEPTH, FOX_WIDTH, D_MODEL), FOX_WIDTH ** -0.5),
        "w_pb": nrm(ks[12], (DEPTH, MLSTM_INNER, D_MODEL), MLSTM_INNER ** -0.5),
        "w_out": nrm(ks[13], (DEPTH, D_MODEL, D_MODEL), beta * D_MODEL ** -0.5),
        "ln1_g": 1.0 + nrm(ks[14], (DEPTH, D_MODEL), 0.02),
        "ln1_b": nrm(ks[15], (DEPTH, D_MODEL), 0.02),
        "w_ffn_in": nrm(ks[16], (DEPTH, D_MODEL, 2 * D_FF_2), D_MODEL ** -0.5),
        "w_ffn_down": nrm(ks[17], (DEPTH, D_FF_2, D_MODEL), beta * D_FF_2 ** -0.5),
        "ln2_g": 1.0 + nrm(ks[18], (DEPTH, D_MODEL), 0.02),
        "ln2_b": nrm(ks[19], (DEPTH, D_MODEL), 0.02),
    }

def second_block(x, c, w_ada, b_ada, w_in, b_in, conv_w, conv_b, w_mq, w_mk, mh_norm_g,
              w_pa, w_pb, w_out, ln1_g, ln1_b, w_ffn_in, w_ffn_down, ln2_g, ln2_b):
    alpha = (2.0 * DEPTH) ** 0.25
    for l in range(DEPTH):
        mod = jnp.einsum('bd,de->be', jax.nn.silu(c), w_ada[l]) + b_ada[l]
        sh1, sc1, g1, sh2, sc2, g2 = [m[:, None, :] for m in jnp.split(mod, 6, axis=-1)]
        h = _ln(x) * (1.0 + sc1) + sh1
        y = _hybrid_mixer(h, w_in[l], b_in[l], conv_w[l], conv_b[l], w_mq[l], w_mk[l],
                          mh_norm_g[l], w_pa[l], w_pb[l], w_out[l])
        x = _ln(alpha * x + g1 * y, ln1_g[l], ln1_b[l])
        h = _ln(x) * (1.0 + sc2) + sh2
        x = _ln(alpha * x + g2 * _swiglu(h, w_ffn_in[l], w_ffn_down[l]), ln2_g[l], ln2_b[l])
    return x


_first_inputs_2 = second_inputs


def second_inputs(seed=0):
    import zlib

    import numpy as np

    out = dict(_first_inputs_2(seed))
    spreads = {}
    factors = {'conv_b': 8.0,
     'mh_norm_g': 8.0,
     'ln1_g': 2.766,
     'ln1_b': 2.736,
     'ln2_g': 2.911,
     'ln2_b': 2.842}
    for name, (base, spread) in spreads.items():
        noise = np.random.default_rng([zlib.crc32(name.encode()), seed]).standard_normal(out[name].shape)
        drawn = base * np.exp(spread * noise) if base else spread * noise
        out[name] = __import__('jax').numpy.asarray(drawn.astype(out[name].dtype))
    for name, factor in factors.items():
        out[name] = (out[name] * factor).astype(out[name].dtype)
    return out


_narrow_inputs_2 = second_inputs


def second_inputs(seed=0):

    out = dict(_narrow_inputs_2(seed))
    wider = {'mh_norm_g': 4.29, 'ln1_g': 3.23, 'ln1_b': 3.24, 'ln2_g': 3.25, 'ln2_b': 3.27}
    for name, times in wider.items():
        mean = out[name].mean()
        out[name] = (mean + times * (out[name] - mean)).astype(out[name].dtype)
    return out


D_CONV = D_MODEL // 2
CONV_W = 3
D_RWKV = D_MODEL // 2
HEAD_SIZE = 64
N_HEADS = D_RWKV // HEAD_SIZE
DECAY_LORA = 64
ICLR_LORA = 64
GATE_LORA = 128
GN_EPS = 64e-5
D_FF_3 = 2816
RMS_EPS = 1e-6

COLS_A = 3 * D_CONV
COLS_B = 3 * D_RWKV + DECAY_LORA + ICLR_LORA + GATE_LORA
COLS_G = 2 * D_MODEL
COLS_IN = COLS_A + COLS_B + COLS_G
SPLIT_B = [D_RWKV, 2 * D_RWKV, 3 * D_RWKV, 3 * D_RWKV + DECAY_LORA, 3 * D_RWKV + DECAY_LORA + ICLR_LORA]


def rms_norm_3(x, g):
    xf = x.astype(jnp.float32)
    y = xf * lax.rsqrt(jnp.mean(xf * xf, axis=-1, keepdims=True) + RMS_EPS)
    return (y * g.astype(jnp.float32)).astype(x.dtype)

def swiglu(x, w_gate, w_up, w_down):
    return (jax.nn.silu(x @ w_gate) * (x @ w_up)) @ w_down

def token_shift(p):
    return jnp.pad(p, ((0, 0), (1, 0), (0, 0)))[:, :-1]

def causal_dwconv(u, w):
    return lax.conv_general_dilated(
        u, w[:, None, :].astype(u.dtype), window_strides=(1,),
        padding=[(CONV_W - 1, 0)], dimension_numbers=("NWC", "WIO", "NWC"),
        feature_group_count=u.shape[-1])

def wkv7_scan(r, w, k, v, a, b):
    bsz, _, h, n = r.shape

    def step(S, inp):
        r_t, w_t, k_t, v_t, a_t, b_t = inp
        sa = jnp.einsum("bhvk,bhk->bhv", S, a_t)
        S = S * w_t[:, :, None, :] + sa[..., None] * b_t[:, :, None, :] + v_t[..., None] * k_t[:, :, None, :]
        y = jnp.einsum("bhvk,bhk->bhv", S, r_t)
        return S, y

    xs = tuple(jnp.moveaxis(t, 1, 0) for t in (r, w, k, v, a, b))
    S0 = jnp.zeros((bsz, h, n, n), jnp.float32)
    _, ys = lax.scan(step, S0, xs)
    return jnp.moveaxis(ys, 0, 1)

def third_inputs(seed: int = 0) -> dict:
    key = jax.random.key(seed)
    ks = iter(jax.random.split(key, 40))
    f32 = jnp.float32

    def nrm(shape, scale):
        return jax.random.normal(next(ks), shape, f32) * scale

    def gain(shape):
        return 1.0 + 0.01 * jax.random.normal(next(ks), shape, f32)

    L = DEPTH
    return {
        "x": jax.random.normal(next(ks), (BATCH, SEQ, D_MODEL), f32),
        "ffn1_norm": gain((L, D_MODEL)),
        "ffn1_w_gate": nrm((L, D_MODEL, D_FF_3), D_MODEL ** -0.5),
        "ffn1_w_up": nrm((L, D_MODEL, D_FF_3), D_MODEL ** -0.5),
        "ffn1_w_down": nrm((L, D_FF_3, D_MODEL), D_FF_3 ** -0.5),
        "mix_norm": gain((L, D_MODEL)),
        "w_in": nrm((L, D_MODEL, COLS_IN), D_MODEL ** -0.5),
        "conv_w": nrm((L, CONV_W, D_CONV), CONV_W ** -0.5),
        "w_out_a": nrm((L, D_CONV, D_MODEL), D_CONV ** -0.5),
        "mu_b": jax.random.uniform(next(ks), (L, COLS_B), f32),
        "w0": nrm((L, D_RWKV), 0.5) - 0.5,
        "w_decay_up": nrm((L, DECAY_LORA, D_RWKV), 0.5 * DECAY_LORA ** -0.5),
        "a0": nrm((L, D_RWKV), 0.1),
        "w_iclr_up": nrm((L, ICLR_LORA, D_RWKV), ICLR_LORA ** -0.5),
        "w_gate_up": nrm((L, GATE_LORA, D_RWKV), GATE_LORA ** -0.5),
        "k_k": 0.85 + nrm((L, D_RWKV), 0.05),
        "k_a": 1.0 + nrm((L, D_RWKV), 0.05),
        "r_k": nrm((L, N_HEADS, HEAD_SIZE), 0.1),
        "ln_x_w": gain((L, D_RWKV)),
        "ln_x_b": nrm((L, D_RWKV), 0.01),
        "w_out_b": nrm((L, D_RWKV, D_MODEL), D_RWKV ** -0.5),
        "w_o": nrm((L, D_MODEL, D_MODEL), D_MODEL ** -0.5),
        "ffn2_norm": gain((L, D_MODEL)),
        "ffn2_w_gate": nrm((L, D_MODEL, D_FF_3), D_MODEL ** -0.5),
        "ffn2_w_up": nrm((L, D_MODEL, D_FF_3), D_MODEL ** -0.5),
        "ffn2_w_down": nrm((L, D_FF_3, D_MODEL), D_FF_3 ** -0.5),
        "final_norm": gain((D_MODEL,)),
    }

def token_mixer(h, w_in, conv_w, w_out_a, mu_b, w0, w_decay_up, a0, w_iclr_up,
                w_gate_up, k_k, k_a, r_k, ln_x_w, ln_x_b, w_out_b, w_o):
    bsz, t, _ = h.shape
    f32 = jnp.float32
    p = h @ w_in
    pa, pb, pg = jnp.split(p, [COLS_A, COLS_A + COLS_B], axis=-1)

    b_gate, c_gate, u = jnp.split(pa, 3, axis=-1)
    y_a = (b_gate * causal_dwconv(c_gate * u, conv_w)) @ w_out_a

    pb = pb + (token_shift(pb) - pb) * mu_b
    r, k, v, xw, xa, xg = jnp.split(pb, SPLIT_B, axis=-1)
    w_log = -jax.nn.softplus(-(w0 + jnp.tanh(xw) @ w_decay_up)) - 0.5
    decay = jnp.exp(-jnp.exp(w_log.astype(f32)))
    iclr = jax.nn.sigmoid(a0 + xa @ w_iclr_up)
    g = jax.nn.sigmoid(xg) @ w_gate_up

    def heads(z):
        return z.astype(f32).reshape(bsz, t, N_HEADS, HEAD_SIZE)

    kk = heads(k * k_k)
    kk = kk / jnp.maximum(jnp.sqrt(jnp.sum(kk * kk, axis=-1, keepdims=True)), 1e-12)
    k = k * (1.0 + (iclr - 1.0) * k_a)
    rh, kh, vh, ah = heads(r), heads(k), heads(v), heads(iclr)
    y = wkv7_scan(rh, heads(decay), kh, vh, -kk, kk * ah)

    mu = jnp.mean(y, axis=-1, keepdims=True)
    var = jnp.mean(jnp.square(y - mu), axis=-1, keepdims=True)
    y = (y - mu) * lax.rsqrt(var + GN_EPS)
    y = (y * ln_x_w.astype(f32).reshape(N_HEADS, HEAD_SIZE)
         + ln_x_b.astype(f32).reshape(N_HEADS, HEAD_SIZE))
    y = y + jnp.sum(rh * kh * r_k.astype(f32), axis=-1, keepdims=True) * vh
    y = y.reshape(bsz, t, D_RWKV).astype(h.dtype)
    y_b = (y * g) @ w_out_b

    g_a, g_b = jnp.split(pg, 2, axis=-1)
    merged = jax.nn.sigmoid(g_a) * y_a + jax.nn.sigmoid(g_b) * y_b
    return merged @ w_o

def third_block(x, ffn1_norm, ffn1_w_gate, ffn1_w_up, ffn1_w_down, mix_norm, w_in,
              conv_w, w_out_a, mu_b, w0, w_decay_up, a0, w_iclr_up, w_gate_up,
              k_k, k_a, r_k, ln_x_w, ln_x_b, w_out_b, w_o, ffn2_norm,
              ffn2_w_gate, ffn2_w_up, ffn2_w_down, final_norm):
    for l in range(DEPTH):
        x = x + 0.5 * swiglu(rms_norm_3(x, ffn1_norm[l]), ffn1_w_gate[l], ffn1_w_up[l], ffn1_w_down[l])
        x = x + token_mixer(rms_norm_3(x, mix_norm[l]), w_in[l], conv_w[l], w_out_a[l], mu_b[l],
                            w0[l], w_decay_up[l], a0[l], w_iclr_up[l], w_gate_up[l],
                            k_k[l], k_a[l], r_k[l], ln_x_w[l], ln_x_b[l], w_out_b[l], w_o[l])
        x = x + 0.5 * swiglu(rms_norm_3(x, ffn2_norm[l]), ffn2_w_gate[l], ffn2_w_up[l], ffn2_w_down[l])
    return rms_norm_3(x, final_norm)


_first_inputs_3 = third_inputs


def third_inputs(seed=0):
    import zlib

    import numpy as np

    out = dict(_first_inputs_3(seed))
    spreads = {}
    factors = {'ffn1_norm': 8.0,
     'mix_norm': 5.644,
     'w_decay_up': 27.656,
     'a0': 5.055,
     'k_k': 64.0,
     'k_a': 3.816,
     'ln_x_w': 64.0,
     'ln_x_b': 64.0,
     'ffn2_norm': 64.0,
     'final_norm': 31.304,
     'w0': 8.0}
    for name, (base, spread) in spreads.items():
        noise = np.random.default_rng([zlib.crc32(name.encode()), seed]).standard_normal(out[name].shape)
        drawn = base * np.exp(spread * noise) if base else spread * noise
        out[name] = __import__('jax').numpy.asarray(drawn.astype(out[name].dtype))
    for name, factor in factors.items():
        out[name] = (out[name] * factor).astype(out[name].dtype)
    return out


_narrow_inputs_3 = third_inputs


def third_inputs(seed=0):

    out = dict(_narrow_inputs_3(seed))
    wider = {'k_k': 12.0, 'ln_x_w': 12.0, 'ln_x_b': 12.0, 'ffn2_norm': 4.5, 'final_norm': 6.3}
    for name, times in wider.items():
        mean = out[name].mean()
        out[name] = (mean + times * (out[name] - mean)).astype(out[name].dtype)
    return out


def setup_inputs(seed=0):
    out = dict(first_inputs(seed))
    for name, value in second_inputs(seed + 1).items():
        if name != "x":
            out[name + "_2"] = value
    for name, value in third_inputs(seed + 2).items():
        if name != "x":
            out[name + "_3"] = value
    return out


def reference(
    x, c, w_ada, b_ada, g_norm1, w_in, g_q, g_k, w_dw, b_dw, g_conv_ln, b_conv_ln, g_out_attn,
    g_out_conv, w_out, g_norm2, w_ff1, w_ff2, c_2, w_ada_2, b_ada_2, w_in_2, b_in_2, conv_w_2,
    conv_b_2, w_mq_2, w_mk_2, mh_norm_g_2, w_pa_2, w_pb_2, w_out_2, ln1_g_2, ln1_b_2,
    w_ffn_in_2, w_ffn_down_2, ln2_g_2, ln2_b_2, ffn1_norm_3, ffn1_w_gate_3, ffn1_w_up_3,
    ffn1_w_down_3, mix_norm_3, w_in_3, conv_w_3, w_out_a_3, mu_b_3, w0_3, w_decay_up_3, a0_3,
    w_iclr_up_3, w_gate_up_3, k_k_3, k_a_3, r_k_3, ln_x_w_3, ln_x_b_3, w_out_b_3, w_o_3,
    ffn2_norm_3, ffn2_w_gate_3, ffn2_w_up_3, ffn2_w_down_3, final_norm_3,
):
    x = first_block(
        x, c, w_ada, b_ada, g_norm1, w_in, g_q, g_k, w_dw, b_dw, g_conv_ln, b_conv_ln,
        g_out_attn, g_out_conv, w_out, g_norm2, w_ff1, w_ff2,
    )
    x = second_block(
        x, c_2, w_ada_2, b_ada_2, w_in_2, b_in_2, conv_w_2, conv_b_2, w_mq_2, w_mk_2,
        mh_norm_g_2, w_pa_2, w_pb_2, w_out_2, ln1_g_2, ln1_b_2, w_ffn_in_2, w_ffn_down_2,
        ln2_g_2, ln2_b_2,
    )
    return third_block(
        x, ffn1_norm_3, ffn1_w_gate_3, ffn1_w_up_3, ffn1_w_down_3, mix_norm_3, w_in_3, conv_w_3,
        w_out_a_3, mu_b_3, w0_3, w_decay_up_3, a0_3, w_iclr_up_3, w_gate_up_3, k_k_3, k_a_3,
        r_k_3, ln_x_w_3, ln_x_b_3, w_out_b_3, w_o_3, ffn2_norm_3, ffn2_w_gate_3, ffn2_w_up_3,
        ffn2_w_down_3, final_norm_3,
    )


_drawn_inputs = setup_inputs


def setup_inputs(seed=0):
    import zlib

    import numpy as np

    out = dict(_drawn_inputs(seed))
    spreads = {}
    factors = {}
    for name, (base, spread) in spreads.items():
        noise = np.random.default_rng([zlib.crc32(name.encode()), seed]).standard_normal(out[name].shape)
        drawn = base * np.exp(spread * noise) if base else spread * noise
        out[name] = __import__('jax').numpy.asarray(drawn.astype(out[name].dtype))
    for name, factor in factors.items():
        out[name] = (out[name] * factor).astype(out[name].dtype)
    return out
```

```python
from contextlib import ExitStack

import numpy as np

import concourse.bass as bass
from concourse import mybir

ALU = mybir.AluOpType
ACT = mybir.ActivationFunctionType
F32 = mybir.dt.float32
F32R = mybir.dt.float32r
BF16 = mybir.dt.bfloat16
AX = mybir.AxisListType.X
MUL, ADD, SUB, MAX, MIN = ALU.mult, ALU.add, ALU.subtract, ALU.max, ALU.min

S = 512
NT = 4
SLOT = 2048
RAW = 2
RING = 2
NEG = -3.0e38
ALL = ("pe", "blk", "act", "dve", "pool", "ev0", "ev1", "ev2", "ev3")
BIG = 2.0 ** 100


def plan():
    slots = []

    def put(kind, blocks):
        cur, used = [], 0
        for b in blocks:
            n = b[2] * b[4]
            if used + n > SLOT:
                slots.append((kind, cur))
                cur, used = [], 0
            cur.append(b)
            used += n
        if cur:
            slots.append((kind, cur))

    def fm(name, nk, col0, ntiles, row0=0):
        return [(name, row0, nk, col0 + 128 * j, 128) for j in range(ntiles)]

    def tm(name, col0, ncol=512):
        return [(name, 0, 4, col0, ncol), (name, 512, 4, col0, ncol)]

    put("raw", fm("w_ada", 8, 0, 48))
    put("mm", fm("w_in", 8, 2120, 4) + fm("w_in", 8, 2632, 4))
    put("mm", tm("w_in", 0) + tm("w_in", 512) + tm("w_in", 1536) + tm("w_in", 1024))
    put("mm", [("w_in", 0, 8, 2048, 72)])
    put("mm", fm("w_out", 8, 0, 8))
    for q in range(4):
        put("mm", fm("w_ff1", 8, q * 1024, 8))
        put("mm", fm("w_ff2", 8, 0, 8, row0=q * 1024))
    put("raw", fm("w_ada_2", 8, 0, 48))
    put("mm", fm("w_gates_2", 8, 0, 2))
    put("mm", fm("w_in_2", 8, 0, 8))
    put("mm", tm("w_in_2", 1024))
    put("mm", fm("w_in_2", 8, 1544, 8))
    put("mm", tm("w_in_2", 2568) + tm("w_in_2", 3080))
    put("mm", [(n, h, 2, 0, 128) for h in range(4) for n in ("w_mq_2", "w_mk_2")])
    put("mm", fm("w_in_2", 8, 3600, 8))
    blocks = []
    for j in range(8):
        blocks += [("w_in_2", 0, 8, 4624 + 128 * j, 128), ("w_pa_2", 0, 4, 128 * j, 128)]
    put("mm", blocks)
    blocks = []
    for j in range(8):
        blocks += [("w_in_2", 0, 8, 5648 + 128 * j, 128), ("w_pb_2", 0, 8, 128 * j, 128)]
    put("mm", blocks)
    put("mm", fm("w_out_2", 8, 0, 8))

    def ffn(gate, gcol, up, ucol, down):
        j0 = 0
        for n in (8, 7, 7):
            blocks = []
            for j in range(j0, j0 + n):
                blocks += [(gate, 0, 8, gcol + 128 * j, 128), (up, 0, 8, ucol + 128 * j, 128)]
            put("mm", blocks)
            put("mm", fm(down, n, 0, 8, row0=128 * j0))
            j0 += n

    ffn("w_ffn_in_2", 0, "w_ffn_in_2", 2816, "w_ffn_down_2")
    ffn("ffn1_w_gate_3", 0, "ffn1_w_up_3", 0, "ffn1_w_down_3")
    put("mm", fm("w_in_3", 8, 512, 8))
    put("mm", fm("w_in_3", 8, 0, 4))
    put("mm", fm("w_in_3", 8, 1536, 14))
    put("raw", [("w_lora_3", 0, 1, 0, 512), ("w_gate_up_3", 0, 1, 0, 512)])
    blocks = []
    for j in range(8):
        blocks += [("w_in_3", 0, 8, 3328 + 128 * j, 128), ("w_out_a_3", 0, 4, 128 * j, 128)]
    put("mm", blocks)
    blocks = []
    for j in range(8):
        blocks += [("w_in_3", 0, 8, 4352 + 128 * j, 128), ("w_out_b_3", 0, 4, 128 * j, 128)]
    put("mm", blocks)
    put("mm", fm("w_o_3", 8, 0, 8))
    ffn("ffn2_w_gate_3", 0, "ffn2_w_up_3", 0, "ffn2_w_down_3")
    return slots


def counted(block):
    _, row0, _, _, ncol = block
    return 4 if (ncol == 512 and row0 == 512) or ncol == 72 else 1


VECS = [
    ("c", 8), ("b_ada", 48), ("g_norm1", 8), ("w_dw", 124), ("b_dw", 4), ("g_conv_ln", 4), ("b_conv_ln", 4),
    ("g_out_attn", 4), ("g_out_conv", 4), ("g_norm2", 8), ("c_2", 8), ("b_ada_2", 48), ("b_fq", 4), ("b_fk", 4),
    ("b_mu", 8), ("b_mo", 8), ("b_ga", 8), ("b_gb", 8), ("b_gates", 2), ("conv_w_2", 32), ("conv_b_2", 8),
    ("mh_norm_g_2", 8), ("ln1_g_2", 8), ("ln1_b_2", 8), ("ln2_g_2", 8), ("ln2_b_2", 8), ("ffn1_norm_3", 8),
    ("mix_norm_3", 8), ("conv_w_3", 12), ("mu_b_3", 14), ("w0_3", 4), ("a0_3", 4), ("k_k_3", 4), ("k_a_3", 4),
    ("r_k_3", 4), ("ln_x_w_3", 4), ("ln_x_b_3", 4), ("ffn2_norm_3", 8), ("final_norm_3", 8), ("g_q", 64), ("g_k", 64),
]
VOFF = {}
_o = 0
for _n, _k in VECS:
    VOFF[_n] = (_o, _k)
    _o += _k
NVEC = _o

CONSTS = ["ident", "ones", "bd", "SLT", "LET", "SL", "m16", "m16T", "L32", "L64", "tri", "triT"]
NCONST = 128 * len(CONSTS) + 64 + 512


def const_array():
    i = np.arange(128)
    r, c = i[:, None], i[None, :]
    c64, c32, c16 = (r // 64 == c // 64), (r // 32 == c // 32), (r // 16 == c // 16)
    m = {
        "ident": r == c, "ones": r + c >= 0, "bd": c64, "SLT": (r < c) & c64, "LET": (r <= c) & c64,
        "SL": (r > c) & c64, "m16": (r > c) & c16, "m16T": (r < c) & c16, "L32": (r > c) & c32 & ~c16,
        "L64": (r > c) & c64 & ~c32,
    }
    m = {k: v.astype(np.float32) for k, v in m.items()}
    m["tri"] = np.where(c > r, np.float32(-BIG), np.float32(0))
    m["triT"] = np.where(r > c, np.float32(BIG), np.float32(0))
    pos = np.arange(S, dtype=np.float32)
    inv = np.float32(500000.0) ** (-np.arange(0, 16, 2, dtype=np.float32) / np.float32(16))
    ang = (pos[:, None] * inv[None, :]).astype(np.float32)
    rope = np.concatenate([np.cos(ang).reshape(4, 128, 8), np.sin(ang).reshape(4, 128, 8)], 0)
    rope = rope.transpose(1, 0, 2).reshape(128, 64).astype(np.float32)
    reset = np.ones((128, S), np.float32)
    reset[:, ::64] = 0
    return np.ascontiguousarray(np.concatenate([m[k] for k in CONSTS] + [rope, reset], 1).astype(np.float32))


class Queues:

    def __init__(self):
        self.q = {e: [] for e in ("pe", "act", "dve", "pool", "sp")}
        self.n = {}

    def op(self, e, fn, waits=(), sem=None, inc=True, by=1):
        sem = (sem or e) if inc else None
        self.q[e].append((list(waits), fn, sem, by))
        if inc:
            self.n[sem] = self.n.get(sem, 0) + by
            return (sem, self.n[sem])

    def dma(self, sem, fn, waits=()):
        return self.op("sp", fn, waits, sem, by=16)

    def now(self, *sems):
        return [(s, self.n[s]) for s in sems if s in self.n]

    def play(self, e, eng, sems):
        seen = {}
        for waits, fn, sem, by in self.q[e]:
            for s, v in waits:
                if v > seen.get(s, 0):
                    eng.wait_ge(sems[s], v)
                    seen[s] = v
            if fn:
                ins = fn()
                if sem:
                    ins.then_inc(sems[sem], by)


class Instructions:

    def act(self, out, in_, f=ACT.Copy, **kw):
        return lambda: self.nc.scalar.activation(out, in_, f, **kw)

    def tt(self, out, a, b, o, e="vector"):
        eng = self.nc.vector if e == "vector" else self.nc.gpsimd
        return lambda: eng.tensor_tensor(out, a, b, o)

    def ts(self, out, a, s1, s2=None, o0=MUL, o1=None):
        if o1 is None:
            return lambda: self.nc.vector.tensor_scalar(out, a, s1, None, o0)
        return lambda: self.nc.vector.tensor_scalar(out, a, s1, s2, o0, o1)

    def stt(self, out, a, s, b, o0, o1):
        return lambda: self.nc.vector.scalar_tensor_tensor(out=out, in0=a, scalar=s, in1=b, op0=o0, op1=o1)

    def cp(self, out, a):
        return lambda: self.nc.vector.tensor_copy(out, a)

    def mm(self, out, l, r, start=True, stop=True):
        return lambda: self.nc.tensor.matmul(out, l, r, start=start, stop=stop)

    def tr(self, out, in_):
        return lambda: self.nc.tensor.transpose(out, in_, self.C("ident"))


class Program(Instructions):

    def __init__(self, nc, ctx, xin, wst, vec, cst, fvb, out):
        self.xs = nc.dram_tensor("x_spill", (1024, S), F32, kind="Internal").ap()
        self.nc, self.Q = nc, Queues()
        self.xin, self.wst, self.vec_d, self.cst_d, self.fvb, self.out = xin, wst, vec, cst, fvb, out
        self.slots = plan()
        sb = lambda n, s, d=F32: ctx.enter_context(nc.sbuf_tensor(n, s, d))
        self.RAWT = sb("wraw", [128, RAW, SLOT])
        self.WH = sb("wh", [128, RING, SLOT], F32R)
        self.WL = sb("wl", [128, RING, SLOT], F32R)
        self.AH = sb("ah", [128, 8, S], F32R)
        self.AL = sb("al", [128, 8, S], F32R)
        self.HH = sb("hh", [128, 8, S], F32R)
        self.HL = sb("hl", [128, 8, S], F32R)
        self.VEC = sb("vecs", [128, NVEC])
        self.CST = sb("csts", [128, NCONST])
        self.MOD = sb("mod", [128, 48])
        self.CA = sb("cact", [128, 8])
        self.SC = sb("scr", [128, 64])
        self.IDB = sb("identb", [128, 128], BF16)
        self.TRB = sb("trib", [128, 2, 128], BF16)
        self.XT = sb("xt", [128, 8, S])
        self.AR = sb("arena", [128, ARENA])
        self.PS = [ctx.enter_context(nc.psum_tensor(f"ps{i}", [128, 512], F32)) for i in range(8)]
        self.slot = -1
        if START > 1:
            pre = {2: "w_ada_2", 3: "ffn1_w_gate_3"}[START]
            self.slot = [i for i, x in enumerate(self.slots) if x[1][0][0] == pre][0] - 1
        self.slot0 = self.slot + 1
        self.blk = 0
        self.mm_slots = [i for i, x in enumerate(self.slots) if x[0] == "mm" and i >= self.slot0]
        self.mth = {n: m for m, n in enumerate(self.mm_slots)}
        self.through, c = {}, 0
        for i in range(self.slot0, len(self.slots)):
            c += sum(counted(b) for b in self.slots[i][1])
            self.through[i] = c
        self.g = 0

    def C(self, name):
        i = CONSTS.index(name)
        return self.CST[:, 128 * i:128 * i + 128]

    def V(self, name, j=0, n=1):
        o = VOFF[name][0]
        return self.VEC[:, o + j:o + j + n]

    def arena(self, off, *shape):
        n = 1
        for s in shape:
            n *= s
        assert off + n <= ARENA, (off, n)
        ap = self.AR[:, off:off + n]
        if len(shape) == 2:
            ap = ap.rearrange("p (a b) -> p a b", a=shape[0])
        if len(shape) == 3:
            ap = ap.rearrange("p (a b c) -> p a b c", a=shape[0], b=shape[1])
        return ap

    def load(self, n):
        if n >= len(self.slots):
            return
        waits = []
        o = n - RAW
        if o >= self.slot0:
            if self.slots[o][0] == "mm":
                waits = [("hi", self.mth[o] + 1), ("lo", self.mth[o] + 1)]
            else:
                waits = [("blk", self.through[o])]
        w = sum(b[2] * b[4] for b in self.slots[n][1])
        dst, src = self.RAWT[:, n % RAW, 0:w], self.wst[n][:, 0:w]
        self.Q.dma(f"w{n % RAW}", lambda: self.nc.sync.dma_start(dst, src), waits)

    def arrived(self, n):
        return (f"w{n % RAW}", 16 * ((n - self.slot0) // RAW + 1))

    def split_slot(self, n):
        if n >= len(self.slots) or self.slots[n][0] == "raw":
            return
        m = self.mth[n]
        w = sum(b[2] * b[4] for b in self.slots[n][1])
        src = self.RAWT[:, n % RAW, 0:w]
        hi, lo = self.WH[:, m % RING, 0:w], self.WL[:, m % RING, 0:w]
        waits = [self.arrived(n)]
        if m >= RING:
            waits.append(("blk", self.through[self.mm_slots[m - RING]]))
        self.Q.op("act", self.act(hi, src), waits, sem="hi")
        self.Q.op("dve", self.tt(lo, src, hi.bitcast(F32), SUB), [*waits, ("hi", m + 1)], sem="lo")
        self.load(n + RAW)

    def next_block(self, name):
        if self.slot < self.slot0 or self.blk == len(self.slots[self.slot][1]):
            n = self.slot
            if n < self.slot0:
                self.split_slot(n + 1)
            elif self.slots[n][0] == "raw":
                self.load(n + RAW)
            self.slot, self.blk = n + 1, 0
            self.split_slot(n + 2)
        kind, blocks = self.slots[self.slot]
        b = blocks[self.blk]
        assert b[0] == name, (b, name)
        off = sum(x[2] * x[4] for x in blocks[:self.blk])
        self.blk += 1
        view = lambda t, i: t[:, i, off:off + b[2] * b[4]].rearrange("p (k c) -> p k c", k=b[2])
        if kind == "raw":
            return view(self.RAWT, self.slot % RAW), None, [self.arrived(self.slot)]
        m = self.mth[self.slot]
        return view(self.WH, m % RING), view(self.WL, m % RING), [("hi", m + 1), ("lo", m + 1)]

    def triple(self, out, wh, wl, xh, xl, first, last, waits, moving_w=False, count=False):
        Q = self.Q
        if moving_w:
            pairs = [(xh, wh), (xh, wl), (xl, wh)]
        else:
            pairs = [(wh, xh), (wh, xl), (wl, xh)]
        for i, (l, r) in enumerate(pairs):
            t = Q.op("pe", self.mm(out, l, r, first and i == 0, last and i == 2), waits if i == 0 else (),
                     sem="blk", inc=i == 2 and (last or count))
        return t

    def gemm(self, name, ntiles, xh, xl, evac, deps=(), x0=0):
        for j in range(ntiles):
            wh, wl, wt = self.next_block(name)
            bank, g4 = self.g % 4, self.g // 4
            ps = self.PS[bank]
            nk = wh.shape[1]
            for k in range(nk):
                t = self.triple(ps[:], wh[:, k, :], wl[:, k, :], xh[:, x0 + k, :], xl[:, x0 + k, :], k == 0,
                                k == nk - 1, [*wt, (f"ev{bank}", g4), *deps] if k == 0 else ())
            evac(j, ps[:], t, f"ev{bank}")
            self.g += 1

    def gemm_tm(self, name, ncol, evac, deps=()):
        rows = 0
        toks = []
        while rows < 8:
            wh, wl, wt = self.next_block(name)
            nk = wh.shape[1]
            for t4 in range(NT):
                bank, g4 = (self.g + t4) % 4, (self.g + t4) // 4
                for k in range(nk):
                    kk = rows + k
                    c = slice(t4 * 128, t4 * 128 + 128)
                    t = self.triple(self.PS[bank][:, 0:ncol], wh[:, k, :], wl[:, k, :], self.AH[:, kk, c],
                                    self.AL[:, kk, c], kk == 0, kk == 7,
                                    [*wt, (f"ev{bank}", g4), *deps] if k == 0 else (), moving_w=True,
                                    count=t4 == 3 and k == nk - 1)
                toks.append(t)
            rows += nk
        for t4 in range(NT):
            bank = (self.g + t4) % 4
            evac(t4, self.PS[bank][:, 0:ncol], toks[t4 - 4], f"ev{bank}")
        self.g += 4

    def split(self, v, hi, lo, deps):
        a = self.Q.op("act", self.act(hi, v), deps)
        d = self.Q.op("dve", self.tt(lo, v, hi.bitcast(F32), SUB), [*deps, a])
        return [a, d]

    def stat(self, after, src, n, scale_mat, bank, square, tmp):
        Q, ps = self.Q, self.PS[bank]
        last = [None, None]
        for t in range(n):
            if square:
                a = Q.op("act", self.act(tmp[:, t % 2, :], src[:, t, :], ACT.Square), [*after, *( [last[t % 2]] if last[t % 2] else [])])
                r = tmp[:, t % 2, :]
                w = [a]
            else:
                r, w = src[:, t, :], []
            m = Q.op("pe", self.mm(ps[:], scale_mat, r, t == 0, t == n - 1), [*after, *w])
            last[t % 2] = m
        return ps, [m]

    def rstd(self, after, out, ps, inv, eps, refine=None):
        Q, v = self.Q, out if refine is None else refine[0]
        t = Q.op("dve", self.ts(v, ps, inv, eps, MUL, ADD), after)
        t = Q.op("dve", lambda: self.nc.vector.reciprocal(out, v), [t])
        t = Q.op("act", self.act(out, out, ACT.Sqrt), [t])
        if refine is not None:
            w = refine[1]
            t = Q.op("dve", self.tt(w, v, out, MUL), [t])
            t = Q.op("dve", self.tt(w, w, out, MUL), [t])
            t = Q.op("dve", self.ts(w, w, -0.5, 1.5, MUL, ADD), [t])
            t = Q.op("dve", self.tt(out, out, w, MUL), [t])
        return [t]

    def rms(self, src, n, width, eps, off, scale, bias, hi, lo, dst0=0):
        after = self.Q.now(*ALL)
        tmp, rs, v = self.arena(off, 2, S), self.arena(off + 1024, S), self.arena(off + 1536, 2, S)
        ps, after = self.stat(after, src, n, self.C("ones"), 4, True, tmp)
        after = self.rstd(after, rs, ps[:], 1.0 / width, eps, (v[:, 0, :], v[:, 1, :]))
        return self.affine(after, src, n, rs, scale, bias, hi, lo, dst0, tmp, v)

    def affine(self, after, src, n, rs, scale, bias, hi, lo, dst0, tmp, v):
        Q = self.Q
        parts = [[], []]
        for t in range(n):
            y = tmp[:, t % 2, :]
            z = v[:, t % 2, :]
            a = Q.op("dve", self.tt(y, src[:, t, :], rs, MUL), [*after, *parts[-2]])
            if bias is None:
                b = Q.op("dve", self.ts(z, y, scale(t)), [a])
            else:
                b = Q.op("dve", self.ts(z, y, scale(t), bias(t), MUL, ADD), [a])
            parts.append(self.split(z, hi[:, dst0 + t, :], lo[:, dst0 + t, :], [b]))
        return parts[-1]

    def ln_center(self, after, src, n, width, dst, tmp, rs, eps):
        Q = self.Q
        ps, summed = self.stat(after, src, n, self.C("ones"), 4, False, None)
        mean = Q.op("act", self.act(rs, ps[:], ACT.Copy, scale=1.0 / width), summed)
        centred = [Q.op("dve", self.tt(dst[:, t, :], src[:, t, :], rs, SUB), [mean]) for t in range(n)]
        ps, summed = self.stat(centred, dst, n, self.C("ones"), 4, True, tmp)
        return self.rstd(summed, rs, ps[:], 1.0 / width, eps)

    def ada(self, name, vec, bvec, c):
        Q = self.Q
        start = Q.now(*ALL) + [self.vtok]
        half = self.SC[:, 44:52]
        th = Q.op("act", self.act(self.CA[:], self.V(c, 0, 8), ACT.Tanh, scale=0.5), start)
        hf = Q.op("dve", self.ts(half, self.V(c, 0, 8), 0.5), start)
        silu = Q.op("dve", self.stt(self.CA[:], self.CA[:], 1.0, half, ADD, MUL), [th, hf])
        ps = self.PS[5]
        for j in range(48):
            w, _, wt = self.next_block(name)
            for k in range(8):
                t = Q.op("pe", self.mm(ps[:, j:j + 1], w[:, k, :], self.CA[:, k:k + 1], k == 0, k == 7),
                         [*wt, silu] if k == 0 else (), sem="blk", inc=k == 7)
        Q.op("dve", self.tt(self.MOD[:], ps[:, 0:48], self.V(bvec, 0, 48), ADD), [t])

    def scaled(self, g, part):
        start = self.Q.now(*ALL)
        m = self.MOD[:, 8 * part:8 * part + 8]
        if g is None:
            self.Q.op("dve", self.ts(self.SC[:, 0:8], m, 1.0, None, ADD), start)
        else:
            self.Q.op("dve", self.stt(self.SC[:, 0:8], m, 1.0, self.V(g, 0, 8), ADD, MUL), start)

    def attention(self, qT, kT, v, add, out, p, pT, st, deps, scale):
        Q, PS = self.Q, self.PS
        N = [(i, h) for i in range(NT) for h in range(8)]
        tmax, texp, ttr, tcp, tpv = {}, {}, {}, {}, {}
        for n in range(len(N) + 2):
            if n < len(N):
                i, h = N[n]
                w = 128 * (i + 1)
                ps = PS[4 + n % 2]
                q0 = 64 * (h % 2)
                Q.op("pe", self.mm(ps[:, 0:w], qT[q0:q0 + 64, h // 2, 128 * i:128 * i + 128],
                                   kT[q0:q0 + 64, h // 2, 0:w], True, False),
                     [*deps, *([texp[n - 2]] if n >= 2 else [])], inc=False)
                tl = add(i, h, ps, w)
                mx, nb, rs = st[:, 0, n:n + 1], st[:, 1, n:n + 1], st[:, 2, n:n + 1]
                psw = ps[:, 0:w]
                tm_ = Q.op("dve", lambda mx=mx, psw=psw: self.nc.vector.reduce_max(mx, psw, AX), [tl])
                tmax[n] = Q.op("dve", self.ts(nb, mx, -scale), [tm_])
                texp[n] = Q.op("act", self.act(p[:, n % 2, 0:w], psw, ACT.Exp, bias=nb, scale=scale, accum_out=rs),
                               [tmax[n], *([ttr[n - 2]] if n >= 2 else [])])
            m = n - 1
            if 0 <= m < len(N):
                i, h = N[m]
                ps = PS[6 + m % 2]
                for j in range(i + 1):
                    t = Q.op("pe", self.tr(ps[:, 128 * j:128 * j + 128], p[:, m % 2, 128 * j:128 * j + 128]),
                             [texp[m], *([tcp[m - 2]] if m >= 2 else [])], inc=j == i)
                ttr[m] = t
                w = 128 * (i + 1)
                dst, src = pT[:, m % 2, 0:w], ps[:, 0:w]
                wt = [t, *([tpv[m - 2]] if m >= 2 else [])]
                tcp[m] = Q.op("act", self.act(dst, src), wt) if m % 2 else Q.op("dve", self.cp(dst, src), wt)
            m = n - 2
            if 0 <= m < len(N):
                i, h = N[m]
                bank, g4 = (self.g + i) % 4, (self.g + i) // 4
                ob = PS[bank]
                for j in range(i + 1):
                    t = Q.op("pe", self.mm(ob[:, 64 * h:64 * h + 64], pT[:, m % 2, 128 * j:128 * j + 128],
                                           v(j, h), j == 0, j == i),
                             [tcp[m], (f"ev{bank}", g4)], inc=j == i)
                tpv[m] = t
                if h == 7:
                    rs8 = st[:, 2, 8 * i:8 * i + 8]
                    ri8 = st[:, 3, 8 * i:8 * i + 8]
                    a = Q.op("dve", lambda ri8=ri8, rs8=rs8: self.nc.vector.reciprocal(ri8, rs8), [texp[m]])
                    o3 = out[:, i, :].rearrange("p (h d) -> p h d", h=8)
                    s3 = ob[:].rearrange("p (h d) -> p h d", h=8)
                    Q.op("dve", self.tt(o3, s3, ri8.unsqueeze(2).to_broadcast([128, 8, 64]), MUL), [a, t], sem=f"ev{bank}")
        self.g += NT

    def transpose_to(self, src, ntiles, evac):
        base = self.Q.now(*ALL)
        emptied = [[], [], [], []]
        for j in range(ntiles):
            b = 4 + j % 4
            for t in range(NT):
                tok = self.Q.op("pe", self.tr(self.PS[b][:, 128 * t:128 * t + 128], src(t, j)),
                                [*base, *emptied[j]], inc=t == 3)
            emptied.append(evac(j, self.PS[b][:], tok, None))

    def residual_evac(self, gate, extra=None):
        def ev(j, ps, t, ev):
            x = self.XT[:, j, :]
            g = gate if isinstance(gate, float) else gate(j)
            return [self.Q.op("dve", self.stt(x, ps, g, x, MUL, ADD), [t, *self.Q.now("dve", "ev0", "ev1", "ev2", "ev3")], sem=ev)]
        return ev

    def swiglu(self, gname, uname, dname, gate, off, atok):
        Q = self.Q
        v = self.arena(off, 2, 2, S)
        act, parts = [], [[], []]
        read = []
        for n in (8, 7, 7):
            for j in range(n):
                g, z = v[:, j % 2, 0, :], v[:, j % 2, 1, :]

                def evg(_, ps, t, ev, g=g):
                    act.append(Q.op("act", self.act(g, ps, ACT.Silu), [t, *parts[-2]], sem=ev))

                def evu(_, ps, t, ev, j=j, g=g, z=z):
                    b = Q.op("dve", self.tt(z, ps, g, MUL), [t, act[-1], *parts[-2]], sem=ev)
                    parts.append(self.split(z, self.HH[:, j, :], self.HL[:, j, :], [b, *read]))

                self.gemm(gname, 1, self.AH, self.AL, evg, deps=atok)
                self.gemm(uname, 1, self.AH, self.AL, evu, deps=atok)
            self.gemm(dname, 8, self.HH, self.HL, self.residual_evac(gate), deps=parts[-1])
            read = Q.now("blk")

    def build(self):
        nc, Q = self.nc, self.Q
        t1 = Q.dma("v", lambda: nc.sync.dma_start(self.VEC[:], self.vec_d))
        t2 = Q.dma("c", lambda: nc.sync.dma_start(self.CST[:], self.cst_d))
        t3 = Q.dma("x", lambda: nc.sync.dma_start(self.XT[:], self.xin.rearrange("(k p) t -> p k t", p=128)))
        for i in range(RAW):
            self.load(self.slot0 + i)
        self.vtok = t1
        a = Q.op("dve", self.cp(self.IDB[:], self.C("ident")), [t1, t2])
        Q.op("dve", self.cp(self.TRB[:, 0, :], self.C("tri")), [a])
        Q.op("act", self.act(self.TRB[:, 1, :], self.C("triT")), [t2, t3, t1])
        Q.op("pool", lambda: nc.gpsimd.memset(self.SC[:], 0.0), [t3, t1, t2])
        Q.op("pe", self.tr(self.PS[7][:, 0:128], self.C("ident")), [t1, t2, t3])
        if START <= 1:
            self.block1()
        if STOP == 1:
            return self.finish()
        if START <= 2:
            self.block2()
        if STOP == 2:
            return self.finish()
        self.block3()
        self.finish()

    def finish(self):
        f = self.Q.now(*ALL)
        o = self.out.rearrange("(k p) t -> p k t", p=128)
        t = self.Q.dma("out", lambda: self.nc.sync.dma_start(o, self.XT[:]), f)
        self.Q.op("sp", None, [t], inc=False)

    def block1(self):
        nc, Q, M = self.nc, self.Q, self.MOD
        self.ada("w_ada", None, "b_ada", "c")
        self.scaled("g_norm1", 1)
        at = self.rms(self.XT, 8, 1024, 1e-6, 0, lambda t: self.SC[:, t:t + 1], lambda t: M[:, t:t + 1], self.AH, self.AL)
        U = self.arena(8480, 4, 542)
        Y = self.arena(8480 + 2168, 4, S)
        z = Q.op("pool", lambda: nc.gpsimd.memset(U[:, :, 0:30], 0.0), Q.now(*ALL))
        f0 = Q.now(*ALL)
        ut = {}
        self.gemm("w_in", 4, self.AH, self.AL,
                  lambda j, ps, t, ev: [Q.op("act", self.act(Y[:, j, :], ps), [t, *f0], sem=ev)], deps=at)
        ytok = [("act", Q.n["act"])]
        SG = self.arena(0, 4, S)

        def evg(j, ps, t, ev):
            a = Q.op("act", self.act(SG[:, j, :], ps, ACT.Sigmoid), [t, *f0], sem=ev)
            ut[j] = Q.op("dve", self.tt(U[:, j, 30:542], Y[:, j, :], SG[:, j, :], MUL), [a, *ytok])
            return [a]

        self.gemm("w_in", 4, self.AH, self.AL, evg, deps=at)
        prev = {}
        for k in range(31):
            for t in range(4):
                y, u, w = Y[:, t, :], U[:, t, k:k + 512], self.V("w_dw", 31 * t + k)
                if k == 0:
                    prev[t] = Q.op("dve", self.ts(y, u, w, self.V("b_dw", t), MUL, ADD), [ut[t], z])
                else:
                    prev[t] = Q.op("dve", self.stt(y, u, w, y, MUL, ADD), [prev[t]])
        after, done = Q.now(*ALL), []
        tmp, rs = self.arena(0, 2, S), self.arena(1024, S)
        after = self.ln_center(after, Y, 4, 512, Y, tmp, rs, 1e-6)
        for t in range(4):
            done += [Q.op("dve", self.tt(Y[:, t, :], Y[:, t, :], rs, MUL), after)]
        after, done = done, []
        for t in range(4):
            done += [Q.op("act", self.act(Y[:, t, :], Y[:, t, :], ACT.Silu, scale=self.V("g_conv_ln", t), bias=self.V("b_conv_ln", t)), after)]
        after, done = done, []
        self.rms(Y, 4, 512, 1e-6, 0, lambda t: self.V("g_out_conv", t), None, self.HH, self.HL, dst0=4)
        TM = self.arena(0, 4, 2120)
        base = Q.now(*ALL)
        for c in range(4):
            def ev(t, ps, tok, ev, c=c):
                dst = TM[:, t, 512 * c:512 * c + 512]
                if t % 2:
                    return [Q.op("act", self.act(dst, ps), [tok, *base], sem=ev)]
                return [Q.op("dve", self.cp(dst, ps), [tok, *base], sem=ev)]
            self.gemm_tm("w_in", 512, ev, deps=at)
        self.gemm_tm("w_in", 72, lambda t, ps, tok, ev: [Q.op("act", self.act(TM[:, t, 2048:2120], ps), [tok, *base], sem=ev)], deps=at)
        after, done = Q.now(*ALL), []
        SQ = self.arena(8480, 4, 1024)
        for t in range(4):
            done += [Q.op("act", self.act(SQ[:, t, :], TM[:, t, 0:1024], ACT.Square), after)]
        after, done = done, []
        ST = self.arena(8480 + 4096, 64)
        done += [Q.op("dve", lambda: nc.vector.reduce_sum(ST, SQ.rearrange("p t (h d) -> p (t h) d", d=64), AX), after)]
        after, done = done, []
        done += [Q.op("dve", self.ts(ST, ST, 1.0 / 64, 1e-6, MUL, ADD), after)]
        after, done = done, []
        done += [Q.op("dve", lambda: nc.vector.reciprocal(ST, ST), after)]
        after, done = done, []
        done += [Q.op("act", self.act(ST, ST, ACT.Sqrt), after)]
        after, done = done, []
        for t in range(4):
            qk = TM[:, t, 0:1024].rearrange("p (h d) -> p h d", d=64)
            done += [Q.op("dve", self.tt(qk, qk, ST[:, 16 * t:16 * t + 16].unsqueeze(2).to_broadcast([128, 16, 64]), MUL), after)]
        after, done = done, []
        for g, o in (("g_q", 0), ("g_k", 512)):
            for t in range(4):
                x = TM[:, t, o:o + 512].rearrange("p (h d) -> p h d", d=64)
                done += [Q.op("dve", self.tt(x, x, self.V(g, 0, 64).unsqueeze(1).to_broadcast([128, 8, 64]), MUL), after)]
        after, done = done, []
        RO = self.CST[:, 128 * len(CONSTS):128 * len(CONSTS) + 64].rearrange("p (s t f) -> p s t f", s=2, t=4)
        R4 = self.arena(8480, 4, 24 * 8)
        for t in range(4):
            for x, nh in ((TM[:, t, 0:1536].rearrange("p (h d) -> p h d", d=64), 24),
                          (TM[:, t, 2048:2112].rearrange("p (h d) -> p h d", d=64), 1)):
                x1, x2 = x[:, :, 0:8], x[:, :, 8:16]
                c = RO[:, 0, t, :].unsqueeze(1).to_broadcast([128, nh, 8])
                s = RO[:, 1, t, :].unsqueeze(1).to_broadcast([128, nh, 8])
                r = [R4[:, i, 0:nh * 8].rearrange("p (h f) -> p h f", h=nh) for i in range(4)]
                done += [Q.op("dve", self.tt(r[0], x1, c, MUL), after)]
                done += [Q.op("dve", self.tt(r[1], x2, s, MUL), after)]
                done += [Q.op("dve", self.tt(r[2], x2, c, MUL), after)]
                done += [Q.op("dve", self.tt(r[3], x1, s, MUL), after)]
                after, done = done, []
                done += [Q.op("dve", self.tt(x1, r[0], r[1], SUB), after)]
                done += [Q.op("dve", self.tt(x2, r[2], r[3], ADD), after)]
                after, done = done, []
        IK2 = self.arena(8480, 4, 128)
        for t in range(4):
            for r in range(2):
                done += [Q.op("dve", self.cp(IK2[:, t, 64 * r:64 * r + 64], TM[:, t, 2048:2112]), after)]
        IW = self.arena(8480 + 512, 32)
        done += [Q.op("dve", self.ts(IW.rearrange("p (t h) -> p t h", t=4), TM[:, :, 2112:2120], 8.0 ** -0.5), after)]
        after, done = done, []
        QKT = self.arena(8480 + 544, 13, S)

        def evt(j, ps, tok, ev):
            return [Q.op("act", self.act(QKT[:, j, :], ps), [tok], sem=ev)] if j % 2 else [Q.op("dve", self.cp(QKT[:, j, :], ps), [tok], sem=ev)]

        self.transpose_to(lambda t, j: TM[:, t, 128 * j:128 * j + 128] if j < 12 else IK2[:, t, :], 13, evt)
        qT, kT, iqT, ikT = QKT[:, 0:4, :], QKT[:, 4:8, :], QKT[:, 8:12, :], QKT[:, 12, :]
        NM = self.arena(15680, 1024).bitcast(BF16).rearrange("p (i s) -> p i s", i=4)
        SCR = self.arena(0, 4, 2120)
        f = Q.now(*ALL)
        qn = 0
        relu, mac = [], []
        for i in range(4):
            w = 128 * (i + 1)
            acc = SCR[:, 0, 0:w] if i % 2 == 0 else SCR[:, 0, 512:512 + w]
            prev_a = None
            for h in range(8):
                b = 4 + h % 2
                q0 = 64 * (h % 2)
                t = Q.op("pe", self.mm(self.PS[b][:, 0:w], iqT[q0:q0 + 64, h // 2, 128 * i:128 * i + 128],
                                       ikT[q0:q0 + 64, 0:w]), [*f, *relu[-2:-1]])
                rel = SCR[:, 1, 512 * (h % 2):512 * (h % 2) + w]
                a = Q.op("act", self.act(rel, self.PS[b][:, 0:w], ACT.Relu, scale=0.125), [t, *mac[-2:-1]])
                relu.append(a)
                iw = IW[:, 8 * i + h:8 * i + h + 1]
                if h == 0:
                    prev_a = Q.op("dve", self.ts(acc, rel, iw), [a, ("dve", Q.n["dve"])])
                else:
                    prev_a = Q.op("dve", self.stt(acc, rel, iw, acc, MUL, ADD), [a, prev_a])
                mac.append(prev_a)
            after, done = [prev_a], []
            nm = NM[:, i, 0:w]
            if i == 0:
                done += [Q.op("dve", lambda nm=nm: nc.vector.memset(nm, 0.0), after)]
                after, done = done, []
                done += [Q.op("dve", lambda: nc.vector.memset(NM[0:64, 0, 64:128], -BIG), after)]
                after, done = done, []
                continue
            done += [Q.op("dve", lambda acc=acc, i=i: nc.vector.memset(acc[0:64, 128 * i + 64:128 * i + 128], NEG), after)]
            after, done = done, []
            wk = SCR[:, 2, 0:w]
            m8 = SCR[:, 3, 0:8]
            src = acc
            for r in range(16):
                done += [Q.op("dve", lambda src=src, m8=m8: nc.vector.max(m8, src), after)]
                after, done = done, []
                if r < 15:
                    done += [Q.op("dve", lambda src=src, wk=wk, m8=m8: nc.vector.match_replace(wk, m8, src, NEG), after)]
                    after, done = done, []
                src = wk
            th = m8[:, 7:8]
            gt, eq, cum = SCR[:, 2, 512:512 + w], SCR[:, 2, 0:w], SCR[:, 3, 512:512 + w]
            done += [Q.op("dve", self.ts(gt, acc, th, None, ALU.is_gt), after)]
            done += [Q.op("dve", self.ts(eq, acc, th, None, ALU.is_equal), after)]
            after, done = done, []
            cnt = SCR[:, 3, 16:17]
            done += [Q.op("dve", lambda cnt=cnt, gt=gt: nc.vector.reduce_sum(cnt, gt, AX), after)]
            ones = SCR[:, 3, 1024:1024 + w]
            done += [Q.op("dve", lambda ones=ones: nc.vector.memset(ones, 1.0), after)]
            after, done = done, []
            done += [Q.op("dve", lambda ones=ones, eq=eq, cum=cum: nc.vector.tensor_tensor_scan(cum, ones, eq, 0.0, MUL, ADD), after)]
            done += [Q.op("dve", self.ts(cnt, cnt, -1.0, 128.0, MUL, ADD), after)]
            after, done = done, []
            done += [Q.op("dve", self.stt(eq, cum, cnt, eq, ALU.is_le, MUL), after)]
            after, done = done, []
            done += [Q.op("dve", self.tt(eq, eq, gt, ADD), after)]
            after, done = done, []
            done += [Q.op("dve", self.ts(nm, eq, -1.0, BIG, ADD, MUL), after)]
            after, done = done, []
        f = Q.now(*ALL)
        AT = SCR[:, :, 0:512]
        PP = SCR[:, 0:2, 512:1024]
        PT = SCR[:, 2:4, 512:1024]
        ST4 = SCR[:, 0, 1024:1152].rearrange("p (a b) -> p a b", a=4)

        def add(i, h, ps, w):
            return Q.op("pe", self.mm(ps[:, 0:w], self.IDB[:], NM[:, i, 0:w], False, True))

        self.attention(qT, kT, lambda j, h: TM[:, j, 1536 + 64 * h:1600 + 64 * h], add, AT, PP, PT, ST4, f, 0.125)
        after, done = Q.now(*ALL), []
        ss = SCR[:, 0, 1024:1028]
        for t in range(4):
            done += [Q.op("act", self.act(SCR[:, t, 512:1024], AT[:, t, :], ACT.Square, accum_out=ss[:, t:t + 1]), after)]
        after, done = done, []
        after = self.rstd(after, ss, ss, 1.0 / 512, 1e-6)
        for t in range(4):
            done += [Q.op("dve", self.ts(AT[:, t, :], AT[:, t, :], ss[:, t:t + 1]), after)]
        after, done = done, []
        YT = QKT

        def evo(j, ps, tok, ev):
            a = Q.op("dve", self.ts(YT[:, j, :], ps, self.V("g_out_attn", j)), [tok], sem=ev)
            self.split(YT[:, j, :], self.HH[:, j, :], self.HL[:, j, :], [a])
            return [a]

        self.transpose_to(lambda t, j: AT[:, t, 128 * j:128 * j + 128], 4, evo)
        self.gemm("w_out", 8, self.HH, self.HL, self.residual_evac(lambda j: M[:, 16 + j:17 + j]), deps=Q.now(*ALL))
        self.scaled("g_norm2", 4)
        at = self.rms(self.XT, 8, 1024, 1e-6, 0, lambda t: self.SC[:, t:t + 1], lambda t: M[:, 24 + t:25 + t], self.AH, self.AL)
        R = self.arena(0, 2, 2, S)
        parts = [[], []]
        f0 = Q.now(*ALL)
        for q in range(4):
            read = Q.now("blk")

            def evr(j, ps, t, ev):
                r, z = R[:, j % 2, 0, :], R[:, j % 2, 1, :]
                a = Q.op("act", self.act(r, ps, ACT.Relu), [t, *f0, *parts[-2]], sem=ev)
                b = Q.op("dve", self.tt(z, r, r, MUL), [a, *parts[-2]])
                parts.append(self.split(z, self.HH[:, j, :], self.HL[:, j, :], [b, *read]))

            self.gemm("w_ff1", 8, self.AH, self.AL, evr, deps=at)
            self.gemm("w_ff2", 8, self.HH, self.HL, self.residual_evac(lambda j: M[:, 40 + j:41 + j]), deps=parts[-1])

    def block2(self):
        nc, Q, M = self.nc, self.Q, self.MOD
        self.ada("w_ada_2", None, "b_ada_2", "c_2")
        self.ln_mod(1, 0)
        at = Q.now(*ALL)
        GA = self.arena(0, 6, S)
        base = Q.now(*ALL)
        self.gemm("w_gates_2", 2, self.AH, self.AL,
                  lambda j, ps, t, ev: [Q.op("act", self.act(GA[:, j, :], ps, ACT.Identity, bias=self.V("b_gates", j)), [t, *base], sem=ev)],
                  deps=at)
        after, done = Q.now(*ALL), []
        done += [Q.op("act", self.act(GA[:, 2, :], GA[:, 0, :], ACT.Abs), after)]
        done += [Q.op("dve", self.ts(GA[:, 3, :], GA[:, 0, :], 0.0, None, MIN), after)]
        done += [Q.op("pool", lambda: nc.gpsimd.memset(GA[:, 4, :], 1.0), after)]
        after, done = done, []
        done += [Q.op("act", self.act(GA[:, 2, :], GA[:, 2, :], ACT.Exp, scale=-1.0), after)]
        after, done = done, []
        done += [Q.op("act", self.act(GA[:, 2, :], GA[:, 2, :], ACT.Ln, bias=1.0), after)]
        after, done = done, []
        done += [Q.op("dve", self.tt(GA[:, 3, :], GA[:, 3, :], GA[:, 2, :], SUB), after)]
        after, done = done, []
        B_, A_, M_, F8 = GA[:, 0, :], GA[:, 1, :], GA[:, 2, :], GA[:, 5, :]
        done += [Q.op("dve", lambda: nc.vector.tensor_tensor_scan(B_, GA[:, 4, :], GA[:, 3, :], 0.0, MUL, ADD), after)]
        after, done = done, []
        done += [Q.op("dve", self.tt(A_, A_, B_, SUB), after)]
        done += [Q.op("act", self.act(F8, B_, ACT.Copy, scale=-8.0), after)]
        after, done = done, []
        done += [Q.op("dve", lambda: nc.vector.tensor_tensor_scan(M_, A_, A_, 0.0, MAX, MAX), after)]
        after, done = done, []
        done += [Q.op("dve", self.tt(GA[:, 3, :], B_, M_, ADD), after)]
        after, done = done, []
        COL = self.arena(3072, 2, 4, 4)
        for t in range(NT):
            done += [Q.op("pe", self.tr(self.PS[4][:, 128 * t:128 * t + 128], A_[:, 128 * t:128 * t + 128]), after)]
            done += [Q.op("pe", self.tr(self.PS[5][:, 128 * t:128 * t + 128], GA[:, 3, 128 * t:128 * t + 128]), after)]
        after, done = done, []
        p4 = self.PS[4][:].rearrange("p (t r) -> p t r", t=4)[:, :, 64:68]
        p5 = self.PS[5][:].rearrange("p (t r) -> p t r", t=4)[:, :, 64:68]
        done += [Q.op("dve", self.cp(COL[:, 0], p4), after)]
        done += [Q.op("act", self.act(COL[:, 1], p5, ACT.Exp, scale=-1.0), after)]
        after, done = done, []
        QT, VF = self.arena(3104, 8, S), self.arena(7200, 4, S)
        VB = self.arena(9248, 512)
        vb = Q.dma("b", lambda: nc.sync.dma_start(VB, self.fvb[:, 0:512]), Q.now(*ALL))
        base = Q.now(*ALL)

        def evq(j, ps, t, ev):
            b = self.V("b_fq", j) if j < 4 else self.V("b_fk", j - 4)
            return [Q.op("act", self.act(QT[:, j, :], ps, ACT.Identity, bias=b), [t, *base], sem=ev)]

        self.gemm("w_in_2", 8, self.AH, self.AL, evq, deps=at)
        self.gemm_tm("w_in_2", 512, lambda t, ps, tok, ev: [Q.op("dve", self.tt(VF[:, t, :], ps, VB, ADD), [tok, *base, vb], sem=ev)],
                     deps=at)
        ATT, PP, PT = self.arena(9760, 4, S), self.arena(11808, 2, S), self.arena(12832, 2, S)
        ST4 = self.arena(13856, 4, 32)

        def add(i, h, ps, w):
            Q.op("pe", self.mm(ps[:, 0:w], self.C("ident")[:, h:h + 1].to_broadcast([128, 128]), F8[:, 0:w], False, False),
                 inc=False)
            return Q.op("pe", self.mm(ps[:, 128 * i:w], self.IDB[:], self.TRB[:, 0, :], False, True))

        self.attention(QT[:, 0:4, :], QT[:, 4:8, :], lambda j, h: VF[:, j, 64 * h:64 * h + 64], add, ATT, PP, PT, ST4,
                       Q.now(*ALL), 0.125)
        f = Q.now(*ALL)
        AT2 = self.arena(3104, 4, S)

        def eva(j, ps, tok, ev):
            return [Q.op("act", self.act(AT2[:, j, :], ps), [tok, *f], sem=ev)]

        self.transpose_to(lambda t, j: ATT[:, t, 128 * j:128 * j + 128], 4, eva)
        base = Q.now(*ALL)
        MU = self.arena(5152, 8, 515)
        U = self.arena(9272, 2, S)
        z = Q.op("pool", lambda: nc.gpsimd.memset(MU[:, :, 0:3], 0.0), base)
        ut = [[], []]
        prevs = {}

        def evm(j, ps, t, ev):
            a = Q.op("act", self.act(MU[:, j, 3:515], ps, ACT.Identity, bias=self.V("b_mu", j)), [t, *base], sem=ev)
            u = U[:, j % 2, :]
            for k in range(4):
                src, w = MU[:, j, k:k + 512], self.V("conv_w_2", 4 * j + k)
                if k == 0:
                    d = Q.op("dve", self.ts(u, src, w, self.V("conv_b_2", j), MUL, ADD), [a, z, *ut[-2]])
                else:
                    d = Q.op("dve", self.stt(u, src, w, u, MUL, ADD), [d])
            d = Q.op("act", self.act(u, u, ACT.Silu), [d])
            ut.append(self.split(u, self.HH[:, j, :], self.HL[:, j, :], [d, *base]))
            return [a]

        self.gemm("w_in_2", 8, self.AH, self.AL, evm, deps=at)
        VM = self.arena(9272 + 1024, 4, 4 * 257)
        VB2 = self.arena(9272, 1024)
        base = Q.now(*ALL)
        vb = Q.dma("b", lambda: nc.sync.dma_start(VB2, self.fvb[:, 512:1536]), base)
        V4 = VM.rearrange("p t (h e) -> p t h e", h=4)
        on = Q.op("dve", lambda: nc.vector.memset(V4[:, :, :, 256:257], 1.0), base)
        for c in range(2):
            def evv(t, ps, tok, ev, c=c):
                dst = V4[:, t, 2 * c:2 * c + 2, 0:256]
                vv = VB2[:, 512 * c:512 * c + 512].rearrange("p (h e) -> p h e", h=2)
                return [Q.op("dve", self.tt(dst, ps.rearrange("p (h e) -> p h e", h=2), vv, ADD), [tok, *base, vb, on], sem=ev)]
            self.gemm_tm("w_in_2", 512, evv, deps=at)
        MQK = self.arena(5152, 2, 4, S)
        base = Q.now(*ALL)
        for h in range(4):
            for i, n in enumerate(("w_mq_2", "w_mk_2")):
                self.gemm(n, 1, self.HH, self.HL,
                          lambda j, ps, t, ev, h=h, i=i: [Q.op("act", self.act(MQK[:, i, h, :], ps), [t, *base], sem=ev)],
                          deps=base, x0=2 * h)
        HM = self.arena(9248 + 24, 1024)
        E_ = self.arena(14408, S)
        P_ = self.arena(14920, 4, S)
        after, done = Q.now(*ALL), []
        HMT = self.HH
        s_ = self.arena(16968, 32)
        SM = self.SC
        ob = [(self.g + t) % 4 for t in range(NT)]
        og = [(self.g + t) // 4 for t in range(NT)]
        O = [self.PS[b] for b in ob]
        for h in range(4):
            for s in range(NT):
                w = 512 - 128 * s
                t0 = 128 * s
                Q.op("pe", self.mm(self.PS[4][:, 0:w], self.C("ident")[:, 64 + h:65 + h].to_broadcast([128, 128]),
                                 M_[:, t0:512], True, False), after, inc=False)
                done += [Q.op("pe", self.mm(self.PS[4][:, 0:128], self.IDB[:], self.TRB[:, 1, :], False, True), after)]
                done += [Q.op("pe", self.mm(self.PS[5][:, 0:w], MQK[:, 1, h, t0:t0 + 128], MQK[:, 0, h, t0:512]), after)]
                after, done = done, []
                done += [Q.op("act", self.act(E_[:, 0:w], self.PS[4][:, 0:w], ACT.Exp, scale=-1.0, bias=COL[:, 0, s, h:h + 1]), after)]
                after, done = done, []
                done += [Q.op("dve", self.stt(P_[:, s, t0:512], self.PS[5][:, 0:w], 128.0 ** -0.5, E_[:, 0:w], MUL, MUL), after)]
                after, done = done, []
            for t in range(NT):
                for s in range(t + 1):
                    d = Q.op("pe", self.mm(O[t][:, 0:257], P_[:, s, 128 * t:128 * t + 128], V4[:, s, h, :], s == 0, s == t),
                             [*after, (f"ev{ob[t]}", og[t])], inc=s == t)
                done.append(d)
            after, done = done, []
            dn, ri = s_[:, 0:4], s_[:, 4:8]
            for t in range(NT):
                done += [Q.op("act", self.act(dn[:, t:t + 1], O[t][:, 256:257], ACT.Abs), after)]
            after, done = done, []
            done += [Q.op("dve", self.tt(dn, dn, COL[:, 1, :, h], MAX), after)]
            after, done = done, []
            done += [Q.op("dve", lambda: nc.vector.reciprocal(ri, dn), after)]
            after, done = done, []
            for t in range(NT):
                done += [Q.op("dve", self.ts(V4[:, t, h, 0:256], O[t][:, 0:256], ri[:, t:t + 1]), after,
                              sem=f"ev{ob[t]}" if h == 3 else None)]
            after, done = done, []
            bs = SM[:, 8:32].rearrange("p (t x) -> p t x", t=4)
            mv = SM[:, 32:40].rearrange("p (t x) -> p t x", t=4)
            for t in range(NT):
                done += [Q.op("dve", lambda t=t, h=h, bs=bs: nc.vector.bn_stats(bs[:, t, :], V4[:, t, h, 0:256]), after)]
            after, done = done, []
            for t in range(NT):
                done += [Q.op("dve", lambda t=t, bs=bs, mv=mv: nc.vector.bn_aggr(mv[:, t, :], bs[:, t, :]), after)]
            after, done = done, []
            rs = SM[:, 40:44]
            after = self.rstd(after, rs, mv[:, :, 1], 1.0, 1e-5)
            for t in range(NT):
                done += [Q.op("dve", self.ts(V4[:, t, h, 0:256], V4[:, t, h, 0:256], mv[:, t, 0:1], rs[:, t:t + 1], SUB, MUL), after)]
            after, done = done, []
        self.g += NT
        HT = self.arena(5152, 8, S)
        SG = self.arena(14408, 2, S)
        base = Q.now(*ALL)
        tt_ = {}

        def evh(j, ps, tok, ev):
            tt_[j] = Q.op("dve", self.ts(HT[:, j, :], ps, self.V("mh_norm_g_2", j)), [tok, *base], sem=ev)
            return [tt_[j]]

        self.transpose_to(lambda t, j: V4[:, t, j // 2, 128 * (j % 2):128 * (j % 2) + 128], 8, evh)
        base = Q.now(*ALL)
        hold = [[], []]

        def evo(j, ps, t, ev):
            a = Q.op("act", self.act(SG[:, j % 2, :], ps, ACT.Sigmoid, bias=self.V("b_mo", j)), [t, *base, *hold[-2]], sem=ev)
            d = Q.op("dve", self.tt(HT[:, j, :], HT[:, j, :], SG[:, j % 2, :], MUL), [a])
            hold.append([d])
            return [a]

        self.gemm("w_in_2", 8, self.AH, self.AL, evo, deps=at)
        Y = self.arena(9272, 8, S)
        base = Q.now(*ALL)
        for j in range(4):
            tk = self.split(AT2[:, j, :], self.HH[:, j, :], self.HL[:, j, :], base)
        hold = [[], []]
        box = {}
        for j in range(8):
            def e1(_, ps, t, ev, j=j):
                box["g"] = Q.op("act", self.act(SG[:, j % 2, :], ps, ACT.Sigmoid, bias=self.V("b_ga", j)),
                                [t, *base, *hold[-2]], sem=ev)
                return [box["g"]]

            def e2(_, ps, t, ev, j=j):
                d = Q.op("dve", self.tt(Y[:, j, :], ps, SG[:, j % 2, :], MUL), [t, box["g"]], sem=ev)
                hold.append([d])
                return [d]

            self.gemm("w_in_2", 1, self.AH, self.AL, e1, deps=at)
            self.gemm("w_pa_2", 1, self.HH, self.HL, e2, deps=tk)
        base = Q.now(*ALL)
        for j in range(8):
            tk = self.split(HT[:, j, :], self.HH[:, j, :], self.HL[:, j, :], base)
        hold = [[], []]
        for j in range(8):
            def e3(_, ps, t, ev, j=j):
                box["g"] = Q.op("act", self.act(SG[:, j % 2, :], ps, ACT.Sigmoid, bias=self.V("b_gb", j)),
                                [t, *base, *hold[-2]], sem=ev)
                return [box["g"]]

            def e4(_, ps, t, ev, j=j):
                a = Q.op("dve", self.tt(SG[:, j % 2, :], ps, SG[:, j % 2, :], MUL), [t, box["g"]], sem=ev)
                d = Q.op("dve", self.tt(Y[:, j, :], Y[:, j, :], SG[:, j % 2, :], ADD), [a])
                hold.append([d])
                return [a]

            self.gemm("w_in_2", 1, self.AH, self.AL, e3, deps=at)
            self.gemm("w_pb_2", 1, self.HH, self.HL, e4, deps=tk)
        base = Q.now(*ALL)
        for j in range(8):
            tk = self.split(Y[:, j, :], self.AH[:, j, :], self.AL[:, j, :], base)
            Q.op("act" if j % 2 else "dve", self.act(self.XT[:, j, :], self.XT[:, j, :], ACT.Copy, scale=ALPHA) if j % 2
                 else self.ts(self.XT[:, j, :], self.XT[:, j, :], ALPHA), base)
        self.gemm("w_out_2", 8, self.AH, self.AL, self.residual_evac(lambda j: M[:, 16 + j:17 + j]),
                  deps=Q.now(*ALL))
        self.ln_x("ln1_g_2", "ln1_b_2")
        self.ln_mod(4, 3)
        at = Q.now(*ALL)
        for j in range(8):
            Q.op("act" if j % 2 else "dve", self.act(self.XT[:, j, :], self.XT[:, j, :], ACT.Copy, scale=ALPHA) if j % 2
                 else self.ts(self.XT[:, j, :], self.XT[:, j, :], ALPHA), at)
        self.swiglu("w_ffn_in_2", "w_ffn_in_2", "w_ffn_down_2", lambda j: M[:, 40 + j:41 + j], 0, Q.now(*ALL))
        self.ln_x("ln2_g_2", "ln2_b_2")

    def ln_mod(self, sc, sh):
        M = self.MOD
        self.scaled(None, sc)
        after = self.Q.now(*ALL)
        XC, tmp, rs, v = self.arena(0, 8, S), self.arena(4096, 2, S), self.arena(5120, S), self.arena(5632, 2, S)
        after = self.ln_center(after, self.XT, 8, 1024, XC, tmp, rs, 1e-5)
        self.affine(after, XC, 8, rs, lambda t: self.SC[:, t:t + 1], lambda t: M[:, 8 * sh + t:8 * sh + t + 1],
                    self.AH, self.AL, 0, tmp, v)

    def ln_x(self, g, b):
        Q = self.Q
        after, done = Q.now(*ALL), []
        tmp, rs = self.arena(4096, 2, S), self.arena(5120, S)
        after = self.ln_center(after, self.XT, 8, 1024, self.XT, tmp, rs, 1e-5)
        for t in range(8):
            done += [Q.op("dve", self.tt(self.XT[:, t, :], self.XT[:, t, :], rs, MUL), after)]
        after, done = done, []
        for t in range(8):
            done += [Q.op("act", self.act(self.XT[:, t, :], self.XT[:, t, :], ACT.Identity, scale=self.V(g, t), bias=self.V(b, t)), after)]
        after, done = done, []

    def block3(self):
        nc, Q = self.nc, self.Q
        one = 1.0
        at = self.rms(self.XT, 8, 1024, 1e-6, 0, lambda t: self.V("ffn1_norm_3", t), None, self.AH, self.AL)
        self.swiglu("ffn1_w_gate_3", "ffn1_w_up_3", "ffn1_w_down_3", 0.5, 0, Q.now(*ALL))
        self.rms(self.XT, 8, 1024, 1e-6, 0, lambda t: self.V("mix_norm_3", t), None, self.AH, self.AL)
        at = Q.now(*ALL)
        xs = self.xs.rearrange("(k p) t -> p k t", p=128)
        sp = Q.dma("spill", lambda: nc.sync.dma_start(xs, self.XT[:]), at)
        CU = self.arena(0, 4, 514)
        T_ = self.arena(2056, 4, S)
        z = Q.op("pool", lambda: nc.gpsimd.memset(CU[:, :, 0:2], 0.0), at)
        ct, cv = {}, {}

        def ec(j, ps, t, ev):
            if j < 4:
                ct[j] = Q.op("act", self.act(T_[:, j, :], ps), [t, *at], sem=ev)
                return [ct[j]]
            j -= 4
            u = Q.op("dve", self.tt(CU[:, j, 2:514], ps, T_[:, j, :], MUL), [t, ct[j]], sem=ev)
            d = Q.op("dve", self.ts(T_[:, j, :], CU[:, j, 0:512], self.V("conv_w_3", 3 * j)), [u, z])
            for k in (1, 2):
                d = Q.op("dve", self.stt(T_[:, j, :], CU[:, j, k:k + 512], self.V("conv_w_3", 3 * j + k), T_[:, j, :], MUL, ADD), [d])
            cv[j] = d
            return [u]

        self.gemm("w_in_3", 8, self.AH, self.AL, ec, deps=at)

        def eb(j, ps, t, ev):
            d = Q.op("dve", self.tt(T_[:, j, :], ps, T_[:, j, :], MUL), [t, cv[j]], sem=ev)
            self.split(T_[:, j, :], self.HH[:, j, :], self.HL[:, j, :], [d, *at])
            return [d]

        self.gemm("w_in_3", 4, self.AH, self.AL, eb, deps=at)
        W = [self.arena(2048 * i, 4, S) for i in range(7)]
        R_, K_, V_, A_, B_, C_, G_ = W
        LO = self.XT[:, 0:2, :]
        PB = self.XT[:, 2:6, :].rearrange("p a b -> p (a b)")
        base = Q.now(*ALL) + [sp]
        z = Q.op("pool", lambda: nc.gpsimd.memset(PB[:, 0:1540], 0.0), base)
        hold = [[], []]

        def es(j, ps, t, ev):
            pb = PB[:, 514 * (j % 2):514 * (j % 2) + 513]
            tmp = PB[:, 1028:1540]
            a = Q.op("act", self.act(pb[:, 1:513], ps), [t, z, *base, *hold[-2]], sem=ev)
            d = Q.op("dve", self.tt(tmp, pb[:, 0:512], pb[:, 1:513], SUB), [a, z, *hold[-1]])
            dst = W[j // 4][:, j % 4, :] if j < 12 else LO[:, j - 12, :]
            d = Q.op("dve", self.stt(dst, tmp, self.V("mu_b_3", j), pb[:, 1:513], MUL, ADD), [d])
            hold.append([d])
            return [a]

        self.gemm("w_in_3", 14, self.AH, self.AL, es, deps=at)
        after, done = Q.now(*ALL), []
        done += [Q.op("act", self.act(LO[0:64, 0, :], LO[0:64, 0, :], ACT.Tanh), after)]
        done += [Q.op("act", self.act(LO[:, 1, :], LO[:, 1, :], ACT.Sigmoid), after)]
        after, done = done, []
        wl, _, wt = self.next_block("w_lora_3")
        wg, _, wt2 = self.next_block("w_gate_up_3")
        for j in range(4):
            c = slice(128 * j, 128 * j + 128)
            done += [Q.op("pe", self.mm(self.PS[4][:], wl[0:64, 0, c], LO[0:64, 0, :]), [*after, *wt])]
            last = "blk" if j == 3 else None
            done += [Q.op("pe", self.mm(self.PS[5][:], wl[64:128, 0, c], LO[64:128, 0, :]), [*after, *wt], sem=last)]
            done += [Q.op("pe", self.mm(self.PS[6][:], wg[:, 0, c], LO[:, 1, :]), [*after, *wt2], sem=last)]
            after, done = done, []
            done += [Q.op("act", self.act(C_[:, j, :], self.PS[4][:], ACT.Sigmoid, bias=self.V("w0_3", j)), after)]
            done += [Q.op("act", self.act(B_[:, j, :], self.PS[5][:], ACT.Sigmoid, bias=self.V("a0_3", j)), after)]
            done += [Q.op("dve", self.cp(G_[:, j, :], self.PS[6][:]), after)]
            after, done = done, []
        RST = self.CST[:, 128 * len(CONSTS) + 64:128 * len(CONSTS) + 576]
        EM = float(-np.exp(np.float32(-0.5)))
        SQ = self.XT[:, 2:4, :]
        N1 = self.XT[:, 4, :]
        for j in range(4):
            done += [Q.op("dve", self.ts(C_[:, j, :], C_[:, j, :], EM), after)]
            done += [Q.op("dve", self.ts(A_[:, j, :], K_[:, j, :], self.V("k_k_3", j)), after)]
            after, done = done, []
            done += [Q.op("dve", lambda j=j: nc.vector.tensor_tensor_scan(C_[:, j, :], RST, C_[:, j, :], 0.0, MUL, ADD), after)]
            done += [Q.op("act", self.act(SQ[:, 0, :], A_[:, j, :], ACT.Square), after)]
            after, done = done, []
            done += [Q.op("pe", self.mm(self.PS[4][:], self.C("bd"), SQ[:, 0, :]), after)]
            done += [Q.op("dve", self.ts(SQ[:, 1, :], B_[:, j, :], -1.0, self.V("k_a_3", j), ADD, MUL), after)]
            after, done = done, []
            done += [Q.op("act", self.act(N1, self.PS[4][:], ACT.Sqrt), after)]
            done += [Q.op("dve", self.stt(K_[:, j, :], SQ[:, 1, :], 1.0, K_[:, j, :], ADD, MUL), after)]
            after, done = done, []
            done += [Q.op("dve", self.ts(N1, N1, 1e-12, None, MAX), after)]
            after, done = done, []
            done += [Q.op("dve", lambda: nc.vector.reciprocal(N1, N1), after)]
            after, done = done, []
            done += [Q.op("dve", self.stt(A_[:, j, :], A_[:, j, :], -1.0, N1, MUL, MUL), after)]
            after, done = done, []
            done += [Q.op("dve", self.stt(B_[:, j, :], A_[:, j, :], -1.0, B_[:, j, :], MUL, MUL), after)]
            after, done = done, []
        self.rwkv(W)
        after, done = Q.now(*ALL), []
        Y = A_
        for j in range(4):
            T1, T2, T3 = self.XT[:, 0, :], self.XT[:, 1, :], self.XT[:, 2, :]
            done += [Q.op("pe", self.mm(self.PS[4][:], self.C("bd"), Y[:, j, :]), after)]
            done += [Q.op("dve", self.tt(T3, R_[:, j, :], K_[:, j, :], MUL), after)]
            after, done = done, []
            done += [Q.op("dve", self.stt(Y[:, j, :], self.PS[4][:], -1.0 / 64, Y[:, j, :], MUL, ADD), after)]
            done += [Q.op("act", self.act(T3, T3, ACT.Copy, scale=self.V("r_k_3", j)), after)]
            after, done = done, []
            done += [Q.op("act", self.act(T1, Y[:, j, :], ACT.Square), after)]
            done += [Q.op("pe", self.mm(self.PS[6][:], self.C("bd"), T3), after)]
            after, done = done, []
            done += [Q.op("pe", self.mm(self.PS[5][:], self.C("bd"), T1), after)]
            done += [Q.op("dve", self.tt(T3, self.PS[6][:], V_[:, j, :], MUL), after)]
            after, done = done, []
            after = self.rstd(after, T2, self.PS[5][:], 1.0 / 64, 64e-5)
            done += [Q.op("dve", self.tt(Y[:, j, :], Y[:, j, :], T2, MUL), after)]
            after, done = done, []
            done += [Q.op("dve", self.ts(Y[:, j, :], Y[:, j, :], self.V("ln_x_w_3", j), self.V("ln_x_b_3", j), MUL, ADD), after)]
            after, done = done, []
            done += [Q.op("dve", self.tt(Y[:, j, :], Y[:, j, :], T3, ADD), after)]
            after, done = done, []
            done += [Q.op("dve", self.tt(Y[:, j, :], Y[:, j, :], G_[:, j, :], MUL), after)]
            after, done = done, []
            self.split(Y[:, j, :], self.HH[:, 4 + j, :], self.HL[:, 4 + j, :], after)
        xr = Q.dma("spill", lambda: nc.sync.dma_start(self.XT[:], xs), Q.now(*ALL))
        Y = self.arena(0, 8, S)
        SG = self.arena(4096, 2, S)
        base = Q.now(*ALL)
        hold, box = [[], []], {}
        for j in range(8):
            def e1(_, ps, t, ev, j=j):
                box["g"] = Q.op("act", self.act(SG[:, j % 2, :], ps, ACT.Sigmoid), [t, *base, *hold[-2]], sem=ev)
                return [box["g"]]

            def e2(_, ps, t, ev, j=j):
                d = Q.op("dve", self.tt(Y[:, j, :], ps, SG[:, j % 2, :], MUL), [t, box["g"]], sem=ev)
                hold.append([d])
                return [d]

            self.gemm("w_in_3", 1, self.AH, self.AL, e1, deps=at)
            self.gemm("w_out_a_3", 1, self.HH, self.HL, e2, deps=base)
        hold = [[], []]
        base = Q.now(*ALL)
        for j in range(8):
            def e3(_, ps, t, ev, j=j):
                box["g"] = Q.op("act", self.act(SG[:, j % 2, :], ps, ACT.Sigmoid), [t, *base, *hold[-2]], sem=ev)
                return [box["g"]]

            def e4(_, ps, t, ev, j=j):
                a = Q.op("dve", self.tt(SG[:, j % 2, :], ps, SG[:, j % 2, :], MUL), [t, box["g"]], sem=ev)
                d = Q.op("dve", self.tt(Y[:, j, :], Y[:, j, :], SG[:, j % 2, :], ADD), [a])
                hold.append([d])
                return [a]

            self.gemm("w_in_3", 1, self.AH, self.AL, e3, deps=at)
            self.gemm("w_out_b_3", 1, self.HH, self.HL, e4, deps=base, x0=4)
        base = Q.now(*ALL) + [xr]
        for j in range(8):
            self.split(Y[:, j, :], self.AH[:, j, :], self.AL[:, j, :], base)
        self.gemm("w_o_3", 8, self.AH, self.AL, self.residual_evac(one), deps=Q.now(*ALL))
        self.rms(self.XT, 8, 1024, 1e-6, 0, lambda t: self.V("ffn2_norm_3", t), None, self.AH, self.AL)
        self.swiglu("ffn2_w_gate_3", "ffn2_w_up_3", "ffn2_w_down_3", 0.5, 0, Q.now(*ALL))
        after, done = Q.now(*ALL), []
        tmp, rs = self.arena(0, 2, S), self.arena(1024, S)
        ps, after = self.stat(after, self.XT, 8, self.C("ones"), 4, True, tmp)
        after = self.rstd(after, rs, ps[:], 1.0 / 1024, 1e-6)
        for t in range(8):
            done += [Q.op("dve", self.stt(self.XT[:, t, :], self.XT[:, t, :], self.V("final_norm_3", t), rs, MUL, MUL), after)]
        after, done = done, []

    def rwkv(self, W):
        base = self.Q.now(*ALL)
        ZB = self.XT[:, 0, :].rearrange("p (a b) -> p a b", a=4)
        z = self.Q.op("dve", lambda: self.nc.vector.memset(ZB, 0.0), base)
        jobs = [(t, p) for t in range(NT) for p in range(4)]
        ends = [[], [], [], [], [], []]
        live = []
        free = [0, 1]
        while jobs or live:
            while free and jobs:
                s = free.pop(0)
                t, p = jobs.pop(0)
                live.append((s, p, self.rwkv_pair(W, t, p, s, ZB, ends, base + [z])))
            nxt = []
            for s, p, g in live:
                try:
                    next(g)
                    nxt.append((s, p, g))
                except StopIteration:
                    free.append(s)
            live = nxt

    def rwkv_pair(self, W, tt_, p, s, ZB, ends, base):
        nc, Q, C = self.nc, self.Q, self.C
        R_, K_, V_, A_, B_, C_, G_ = W
        t0 = 128 * tt_
        sl = slice(t0, t0 + 128)
        after, done = base + ends[4 + s], []
        xf = self.XT[:].rearrange("p a b -> p (a b)")
        area = xf[:, 512 + 1792 * s:512 + 1792 * s + 1792]
        pos = [0]
        more = self.arena(14336 + 1536 * s, 1536)

        def alloc(*shape):
            n = int(np.prod(shape))
            o = pos[0]
            if o < 1792 and o + n > 1792:
                o = 1792
            src, oo = (area, o) if o < 1792 else (more, o - 1792)
            assert oo + n <= (1792 if o < 1792 else 1536), (o, n)
            pos[0] = o + n
            ap = src[:, oo:oo + n]
            if len(shape) == 2:
                return ap.rearrange("p (a b) -> p a b", a=shape[0])
            if len(shape) == 3:
                return ap.rearrange("p (a b c) -> p a b c", a=shape[0], b=shape[1])
            return ap

        PB = [self.PS[4 * s + i] for i in range(4)]
        MT4 = alloc(2, 4, 128)
        PP = alloc(2, 128)
        TT = alloc(2, 128)
        ARt = alloc(2, 128)
        BK = alloc(2, 128)
        BKh = alloc(2, 128)
        EX = alloc(2, 65)
        TK = alloc(4, 128)
        p16 = [BK, BKh, alloc(2, 128)]
        E2 = p16[2][:, 0, :]
        c2 = C_[:, p, sl].rearrange("p (c t) -> p c t", c=2)
        c1 = C_[:, p, sl]
        done += [Q.op("dve", lambda: nc.vector.memset(EX[:, :, 0:1], 1.0), after)]
        done += [Q.op("act", self.act(EX[:, :, 1:65], c2, ACT.Exp), after)]
        done += [Q.op("act", self.act(E2, c1, ACT.Exp, scale=-1.0), after)]
        after, done = done, []
        yield
        eh = p16[2][:, 1, :]
        done += [Q.op("dve", self.tt(ARt[:, 0, :].rearrange("p (c t) -> p c t", c=2), A_[:, p, sl].rearrange("p (c t) -> p c t", c=2),
                          EX[:, :, 0:64], MUL), after)]
        done += [Q.op("dve", self.tt(ARt[:, 1, :].rearrange("p (c t) -> p c t", c=2), R_[:, p, sl].rearrange("p (c t) -> p c t", c=2),
                          EX[:, :, 1:65], MUL), after)]
        done += [Q.op("dve", self.tt(BK[:, 0, :], B_[:, p, sl], E2, MUL), after)]
        done += [Q.op("dve", self.tt(BK[:, 1, :], K_[:, p, sl], E2, MUL), after)]
        for c in range(2):
            done += [Q.op("act", self.act(eh[:, 64 * c:64 * c + 64], c2[:, c, :], ACT.Exp, scale=-1.0,
                               bias=C_[:, p, t0 + 64 * c + 63:t0 + 64 * c + 64]), after)]
        after, done = done, []
        yield
        done += [Q.op("dve", self.tt(BKh[:, 0, :], B_[:, p, sl], eh, MUL), after)]
        done += [Q.op("dve", self.tt(BKh[:, 1, :], K_[:, p, sl], eh, MUL), after)]
        for h in range(2):
            q = slice(64 * h, 64 * h + 64)
            for i in range(2):
                done += [Q.op("pe", self.mm(PB[h][:, 256 * i:256 * i + 256], BK[q, i, :], ARt[q, :, :].rearrange("p a b -> p (a b)")), after)]
            done += [Q.op("pe", self.mm(PB[2 + h][:, 0:128], ARt[q, 0, :], BK[q, 0, :]), after)]
        after, done = done, []
        yield
        mk = self.CST[:, 128 * CONSTS.index("SLT"):128 * CONSTS.index("SLT") + 256].unsqueeze(1).to_broadcast([128, 2, 256])
        for h in range(2):
            done += [Q.op("dve", self.tt(MT4[:, h].rearrange("p a b -> p (a b)").rearrange("p (a b) -> p a b", a=2),
                              PB[h][:].rearrange("p (a b) -> p a b", a=2), mk, MUL), after)]
            done += [Q.op("dve", self.tt(PP[:, h, :], PB[2 + h][:, 0:128], C("SL"), MUL), after)]
        after, done = done, []
        yield
        for i, x in enumerate((ARt[:, 0, :], BKh[:, 0, :], BKh[:, 1, :], V_[:, p, sl])):
            done += [Q.op("pe", self.tr(PB[0][:, 128 * i:128 * i + 128], x), after)]
        after, done = done, []
        yield
        done += [Q.op("act", self.act(TK.rearrange("p a b -> p (a b)"), PB[0][:]), after)]
        bc = lambda m: C(m).unsqueeze(1).to_broadcast([128, 2, 128])
        x, xt, y = p16
        done += [Q.op("dve", self.tt(x, PP, bc("m16"), MUL), after)]
        done += [Q.op("dve", self.tt(xt, MT4[:, :, 0, :], bc("m16T"), MUL), after)]
        after, done = done, []
        done += [Q.op("dve", self.tt(TT, xt, bc("ident"), ADD), after)]
        X, XT_ = x, xt
        for lev in range(3):
            for h in range(2):
                done += [Q.op("pe", self.mm(PB[1][:, 128 * h:128 * h + 128], XT_[:, h, :], X[:, h, :]), after)]
                if lev < 2:
                    done += [Q.op("pe", self.mm(PB[2][:, 128 * h:128 * h + 128], X[:, h, :], XT_[:, h, :]), after)]
            after, done = done, []
            yield
            pv = lambda b: PB[b][:, 0:256].rearrange("p (a b) -> p a b", a=2)
            done += [Q.op("act", self.act(X, pv(1)), after)]
            if lev < 2:
                done += [Q.op("dve", self.cp(XT_, pv(2)), after)]
            after, done = done, []
            yield
            for h in range(2):
                done += [Q.op("pe", self.mm(PB[3][:, 128 * h:128 * h + 128], X[:, h, :], TT[:, h, :]), after)]
            after, done = done, []
            yield
            done += [Q.op("dve", self.tt(TT, pv(3), TT, ADD), after)]
            after, done = done, []
            yield
        L, Xx, D = x, xt, y
        for name in ("L32", "L64"):
            done += [Q.op("dve", self.tt(L, PP, bc(name), MUL), after)]
            for h in range(2):
                done += [Q.op("pe", self.tr(PB[1][:, 128 * h:128 * h + 128], TT[:, h, :]), after)]
            after, done = done, []
            yield
            done += [Q.op("act", self.act(D, pv(1)), after)]
            for h in range(2):
                done += [Q.op("pe", self.mm(PB[2][:, 128 * h:128 * h + 128], L[:, h, :], TT[:, h, :]), after)]
            after, done = done, []
            yield
            done += [Q.op("dve", self.cp(Xx, pv(2)), after)]
            after, done = done, []
            yield
            for h in range(2):
                done += [Q.op("pe", self.mm(PB[3][:, 128 * h:128 * h + 128], D[:, h, :], Xx[:, h, :]), after)]
            after, done = done, []
            yield
            done += [Q.op("dve", self.tt(TT, pv(3), TT, ADD), after)]
            after, done = done, []
            yield
        U, AS = x, xt
        hs = lambda h: slice(64 * h, 64 * h + 64)
        for h in range(2):
            done += [Q.op("pe", self.mm(PB[1][:, hs(h)], MT4[:, h, 2, :], TK[:, 3, hs(h)]), after)]
        after, done = done, []
        yield
        done += [Q.op("act", self.act(U[:, 0, :], PB[1][:, 0:128]), after)]
        after, done = done, []
        for h in range(2):
            done += [Q.op("pe", self.mm(PB[2][:, hs(h)], TT[:, h, :], TK[:, 0, hs(h)]), after)]
            done += [Q.op("pe", self.mm(PB[2][:, 128 + 64 * h:192 + 64 * h], TT[:, h, :], U[:, 0, hs(h)]), after)]
        after, done = done, []
        yield
        done += [Q.op("dve", self.cp(AS, PB[2][:, 0:256].rearrange("p (a b) -> p a b", a=2)), after)]
        after, done = done, []
        yield
        MG = MT4[:, 0]
        for c in range(2):
            q = slice(64 * c, 64 * c + 64)
            done += [Q.op("pe", self.mm(PB[c][:, 0:128], AS[q, 0, :], TK[q, 1, :]), after)]
            Q.op("pe", self.mm(PB[c][:, 128:256], TK[q, 1, :], AS[q, 1, :], True, False), after, inc=False)
            done += [Q.op("pe", self.mm(PB[c][:, 128:256], TK[q, 2, :], TK[q, 3, :], False, True), after)]
        for h in range(2):
            o = hs(h)
            done += [Q.op("pe", self.mm(PB[2][o, 0:128], AS[:, 0, hs(h)], MT4[:, h, 1, :]), after)]
            Q.op("pe", self.mm(PB[2][o, 128:256], AS[:, 1, hs(h)], MT4[:, h, 1, :], True, False), after, inc=False)
            done += [Q.op("pe", self.mm(PB[2][o, 128:256], TK[:, 3, hs(h)], MT4[:, h, 3, :], False, True), after)]
        after, done = done, []
        yield
        mg = MT4.rearrange("p h a b -> p (h a) b")[:, 0:4, :]
        bd2 = C("bd").unsqueeze(1).to_broadcast([128, 2, 128])
        for c in range(2):
            done += [Q.op("dve", self.tt(mg[:, 2 * c:2 * c + 2, :], PB[c][:, 0:256].rearrange("p (a b) -> p a b", a=2), bd2, MUL), after)]
        qt, y0 = y[:, 0, :], y[:, 1, :]
        done += [Q.op("dve", self.tt(qt, PB[2][:, 0:128], ARt[:, 1, :], ADD), after)]
        done += [Q.op("dve", self.cp(y0, PB[2][:, 128:256]), after)]
        after, done = done, []
        yield
        for c in range(2):
            done += [Q.op("dve", self.stt(mg[:, 2 * c, :], C("ident"), EX[:, c, 64:65], mg[:, 2 * c, :], MUL, ADD), after)]
        after, done = done, []
        yield
        ze = ends[p]
        for c in range(2):
            done += [Q.op("pe", self.mm(PB[3][:, 128 * c:128 * c + 64], ZB[:, p, :], qt[:, 64 * c:64 * c + 64]), [*after, *ze])]
            done += [Q.op("pe", self.mm(PB[1][:, 0:128], mg[:, 2 * c, :], ZB[:, p, :]), [*after, *ze])]
            after, done = done, []
            yield
            done += [Q.op("dve", self.tt(ZB[:, p, :], PB[1][:, 0:128], mg[:, 2 * c + 1, :], ADD), after)]
            done += [Q.op("dve", self.tt(A_[:, p, t0 + 64 * c:t0 + 64 * c + 64], PB[3][:, 128 * c:128 * c + 64],
                              y0[:, 64 * c:64 * c + 64], ADD), after)]
            after, done = done, []
            yield
        ends[p] = ends[4 + s] = after


ARENA = 17408
STOP = 3
START = 1
ALPHA = 2.0 ** 0.25


def bass_program(nc, xin, wst, vec, cst, fvb, out):
    with ExitStack() as ctx:
        K = Program(nc, ctx, xin, wst, vec, cst, fvb, out)
        K.build()
        names = set(K.Q.n) | {"pe", "act", "dve", "pool", "sp"}
        sems = {n: ctx.enter_context(nc.semaphore("s_" + n)) for n in sorted(names)}
        block = ctx.enter_context(nc.Block())

        @block.sync
        def _(eng):
            K.Q.play("sp", eng, sems)

        @block.tensor
        def _(eng):
            K.Q.play("pe", eng, sems)

        @block.scalar
        def _(eng):
            K.Q.play("act", eng, sems)

        @block.vector
        def _(eng):
            K.Q.play("dve", eng, sems)

        @block.gpsimd
        def _(eng):
            K.Q.play("pool", eng, sems)


def lay_out(inp):
    x = {k: np.asarray(v) for k, v in inp.items()}
    w = {k: (v[0] if v.ndim >= 3 else v) for k, v in x.items()}
    g = np.zeros((1024, 256), np.float32)
    g[:, 0:8] = w["w_in_2"][:, 1536:1544]
    g[:, 64:68] = w["w_in_2"][:, 3596:3600]
    g[:, 192:196] = w["w_in_2"][:, 3592:3596]
    w["w_gates_2"] = g
    w["w_lora_3"] = np.concatenate([w["w_decay_up_3"], w["w_iclr_up_3"]], 0)
    slots = plan()
    ws = np.zeros((len(slots), 128, SLOT), np.float32)
    for i, (kind, blocks) in enumerate(slots):
        o = 0
        for name, r0, nk, c0, nc_ in blocks:
            if name in ("w_mq_2", "w_mk_2"):
                a = w[name][r0]
            else:
                a = w[name][r0:r0 + 128 * nk, c0:c0 + nc_]
            ws[i, :, o:o + nk * nc_] = a.reshape(nk, 128, nc_).transpose(1, 0, 2).reshape(128, nk * nc_)
            o += nk * nc_
    b2 = x["b_in_2"][0]
    bg = np.zeros(256, np.float32)
    bg[0:8], bg[64:68], bg[192:196] = b2[1536:1544], b2[3596:3600], b2[3592:3596]
    extra = {"b_fq": b2[0:512], "b_fk": b2[512:1024], "b_mu": b2[1544:2568], "b_mo": b2[3600:4624],
             "b_ga": b2[4624:5648], "b_gb": b2[5648:6672], "b_gates": bg}
    cols = []
    for n, k in VECS:
        if n in ("g_q", "g_k"):
            cols.append(np.broadcast_to(x[n].reshape(1, 64), (128, 64)))
        elif n in ("w_dw", "conv_w_2", "conv_w_3"):
            a = x[n][0]
            cols.append(a.reshape(a.shape[0], -1, 128).transpose(2, 1, 0).reshape(128, k))
        else:
            a = extra[n] if n in extra else x[n]
            cols.append(a.reshape(k, 128).T)
    vec = np.ascontiguousarray(np.concatenate(cols, 1))
    fvb = np.ascontiguousarray(np.broadcast_to(np.concatenate([b2[1024:1536], b2[2568:3592]])[None], (128, 1536)))
    xin = np.ascontiguousarray(x["x"][0].T)
    return {"xin": xin, "wst": ws, "vec": vec, "cst": const_array(), "fvb": fvb}


def kernel(**inputs):
    import concourse.bacc as _bacc
    from concourse.bass_utils import run_bass_kernel_spmd as _run

    nc = _bacc.Bacc("TRN2", target_bir_lowering=False, num_devices=1)
    arrays, args = {}, []
    for name, a in lay_out(inputs).items():
        arrays[f"in_{name}_dram"] = a
        args.append(nc.dram_tensor(f"in_{name}_dram", a.shape, mybir.dt.from_np(a.dtype), kind="ExternalInput").ap())
    args.append(nc.dram_tensor("out_0_dram", (1024, S), F32, kind="ExternalOutput").ap())
    bass_program(nc, *args)
    r = _run(nc, [arrays], core_ids=[0])
    return np.ascontiguousarray(r.results[0]["out_0_dram"].T)[None]
```

```python
from contextlib import ExitStack

import numpy as np

import concourse.bass as bass
from concourse import mybir

ALU = mybir.AluOpType
ACT = mybir.ActivationFunctionType
F32 = mybir.dt.float32
F32R = mybir.dt.float32r
BF16 = mybir.dt.bfloat16
AX = mybir.AxisListType.X
MUL, ADD, SUB, MAX, MIN = ALU.mult, ALU.add, ALU.subtract, ALU.max, ALU.min

S = 512
NT = 4
SLOT = 2048
RAW = 2
RING = 2
NEG = -3.0e38
ALL = ("pe", "blk", "act", "dve", "pool", "ev0", "ev1", "ev2", "ev3")
BIG = 2.0 ** 100


def plan():
    slots = []

    def put(kind, blocks):
        cur, used = [], 0
        for b in blocks:
            n = b[2] * b[4]
            if used + n > SLOT:
                slots.append((kind, cur))
                cur, used = [], 0
            cur.append(b)
            used += n
        if cur:
            slots.append((kind, cur))

    def fm(name, nk, col0, ntiles, row0=0):
        return [(name, row0, nk, col0 + 128 * j, 128) for j in range(ntiles)]

    def tm(name, col0, ncol=512):
        return [(name, 0, 4, col0, ncol), (name, 512, 4, col0, ncol)]

    def riding(start, ada):
        rest, slots[start:] = slots[start:], []
        for i, x in enumerate(rest):
            slots.append(x)
            if i < len(ada):
                slots.append(ada[i])
        assert len(ada) <= len(rest)

    def ada(name):
        return [("ada", fm(name, 8, 256 * i, 2)) for i in range(24)]

    ada1, ada2 = ada("w_ada"), ada("w_ada_2")
    put("raw", fm("w_ada", 8, 0, 16))
    start = len(slots)
    put("mm", fm("w_in", 8, 2120, 4) + fm("w_in", 8, 2632, 4))
    put("mm", tm("w_in", 0) + tm("w_in", 512) + tm("w_in", 1536) + tm("w_in", 1024))
    riding(start, ada1[8:20])
    put("mm", [("w_in", 0, 8, 2048, 72)])
    start = len(slots)
    put("mm", fm("w_out", 8, 0, 8))
    riding(start, ada1[20:])
    start = len(slots)
    for q in range(4):
        put("mm", fm("w_ff1", 8, q * 1024, 8))
        put("mm", fm("w_ff2", 8, 0, 8, row0=q * 1024))
    riding(start, ada2)
    if START == 2:
        slots = list(ada2)
    put("mm", fm("w_gates_2", 8, 0, 2))
    put("mm", fm("w_in_2", 8, 0, 8))
    put("mm", tm("w_in_2", 1024))
    put("mm", fm("w_in_2", 8, 1544, 8))
    put("mm", tm("w_in_2", 2568) + tm("w_in_2", 3080))
    put("mm", [(n, h, 2, 0, 128) for h in range(4) for n in ("w_mq_2", "w_mk_2")])
    put("mm", fm("w_in_2", 8, 3600, 8))
    blocks = []
    for j in range(8):
        blocks += [("w_in_2", 0, 8, 4624 + 128 * j, 128), ("w_pa_2", 0, 4, 128 * j, 128)]
    put("mm", blocks)
    blocks = []
    for j in range(8):
        blocks += [("w_in_2", 0, 8, 5648 + 128 * j, 128), ("w_pb_2", 0, 8, 128 * j, 128)]
    put("mm", blocks)
    put("mm", fm("w_out_2", 8, 0, 8))

    def ffn(gate, gcol, up, ucol, down):
        j0 = 0
        for n in (8, 7, 7):
            blocks = []
            for j in range(j0, j0 + n):
                blocks += [(gate, 0, 8, gcol + 128 * j, 128), (up, 0, 8, ucol + 128 * j, 128)]
            put("mm", blocks)
            put("mm", fm(down, n, 0, 8, row0=128 * j0))
            j0 += n

    ffn("w_ffn_in_2", 0, "w_ffn_in_2", 2816, "w_ffn_down_2")
    ffn("ffn1_w_gate_3", 0, "ffn1_w_up_3", 0, "ffn1_w_down_3")
    put("mm", fm("w_in_3", 8, 512, 8))
    put("mm", fm("w_in_3", 8, 0, 4))
    put("mm", fm("w_in_3", 8, 1536, 14))
    put("raw", [("w_lora_3", 0, 1, 0, 512), ("w_gate_up_3", 0, 1, 0, 512)])
    blocks = []
    for j in range(8):
        blocks += [("w_in_3", 0, 8, 3328 + 128 * j, 128), ("w_out_a_3", 0, 4, 128 * j, 128)]
    put("mm", blocks)
    blocks = []
    for j in range(8):
        blocks += [("w_in_3", 0, 8, 4352 + 128 * j, 128), ("w_out_b_3", 0, 4, 128 * j, 128)]
    put("mm", blocks)
    put("mm", fm("w_o_3", 8, 0, 8))
    ffn("ffn2_w_gate_3", 0, "ffn2_w_up_3", 0, "ffn2_w_down_3")
    return slots


def counted(block):
    _, row0, _, _, ncol = block
    return 4 if (ncol == 512 and row0 == 512) or ncol == 72 else 1


VECS = [
    ("c", 8), ("b_ada", 48), ("g_norm1", 8), ("w_dw", 124), ("b_dw", 4), ("g_conv_ln", 4), ("b_conv_ln", 4),
    ("g_out_attn", 4), ("g_out_conv", 4), ("g_norm2", 8), ("c_2", 8), ("b_ada_2", 48), ("b_fq", 4), ("b_fk", 4),
    ("b_mu", 8), ("b_mo", 8), ("b_ga", 8), ("b_gb", 8), ("b_gates", 2), ("conv_w_2", 32), ("conv_b_2", 8),
    ("mh_norm_g_2", 8), ("ln1_g_2", 8), ("ln1_b_2", 8), ("ln2_g_2", 8), ("ln2_b_2", 8), ("ffn1_norm_3", 8),
    ("mix_norm_3", 8), ("conv_w_3", 12), ("mu_b_3", 14), ("w0_3", 4), ("a0_3", 4), ("k_k_3", 4), ("k_a_3", 4),
    ("r_k_3", 4), ("ln_x_w_3", 4), ("ln_x_b_3", 4), ("ffn2_norm_3", 8), ("final_norm_3", 8), ("g_q", 64), ("g_k", 64),
]
VOFF = {}
_o = 0
for _n, _k in VECS:
    VOFF[_n] = (_o, _k)
    _o += _k
NVEC = _o

CONSTS = ["ident", "ones", "bd", "SLT", "LET", "SL", "m16", "m16T", "L32", "L64", "tri", "triT"]
NCONST = 128 * len(CONSTS) + 64 + 512


def const_array():
    i = np.arange(128)
    r, c = i[:, None], i[None, :]
    c64, c32, c16 = (r // 64 == c // 64), (r // 32 == c // 32), (r // 16 == c // 16)
    m = {
        "ident": r == c, "ones": r + c >= 0, "bd": c64, "SLT": (r < c) & c64, "LET": (r <= c) & c64,
        "SL": (r > c) & c64, "m16": (r > c) & c16, "m16T": (r < c) & c16, "L32": (r > c) & c32 & ~c16,
        "L64": (r > c) & c64 & ~c32,
    }
    m = {k: v.astype(np.float32) for k, v in m.items()}
    m["tri"] = np.where(c > r, np.float32(-BIG), np.float32(0))
    m["triT"] = np.where(r > c, np.float32(BIG), np.float32(0))
    pos = np.arange(S, dtype=np.float32)
    inv = np.float32(500000.0) ** (-np.arange(0, 16, 2, dtype=np.float32) / np.float32(16))
    ang = (pos[:, None] * inv[None, :]).astype(np.float32)
    rope = np.concatenate([np.cos(ang).reshape(4, 128, 8), np.sin(ang).reshape(4, 128, 8)], 0)
    rope = rope.transpose(1, 0, 2).reshape(128, 64).astype(np.float32)
    reset = np.ones((128, S), np.float32)
    reset[:, ::64] = 0
    return np.ascontiguousarray(np.concatenate([m[k] for k in CONSTS] + [rope, reset], 1).astype(np.float32))


class Queues:

    def __init__(self):
        self.q = {e: [] for e in ("pe", "act", "dve", "pool", "sp")}
        self.n = {}

    def op(self, e, fn, waits=(), sem=None, inc=True, by=1):
        sem = (sem or e) if inc else None
        self.q[e].append((list(waits), fn, sem, by))
        if inc:
            self.n[sem] = self.n.get(sem, 0) + by
            return (sem, self.n[sem])

    def dma(self, sem, fn, waits=()):
        return self.op("sp", fn, waits, sem, by=16)

    def now(self, *sems):
        return [(s, self.n[s]) for s in sems if s in self.n]

    def play(self, e, eng, sems):
        seen = {}
        for waits, fn, sem, by in self.q[e]:
            for s, v in waits:
                if v > seen.get(s, 0):
                    eng.wait_ge(sems[s], v)
                    seen[s] = v
            if fn:
                ins = fn()
                if sem:
                    ins.then_inc(sems[sem], by)


class Instructions:

    def act(self, out, in_, f=ACT.Copy, **kw):
        return lambda: self.nc.scalar.activation(out, in_, f, **kw)

    def tt(self, out, a, b, o, e="vector"):
        eng = self.nc.vector if e == "vector" else self.nc.gpsimd
        return lambda: eng.tensor_tensor(out, a, b, o)

    def ts(self, out, a, s1, s2=None, o0=MUL, o1=None):
        if o1 is None:
            return lambda: self.nc.vector.tensor_scalar(out, a, s1, None, o0)
        return lambda: self.nc.vector.tensor_scalar(out, a, s1, s2, o0, o1)

    def stt(self, out, a, s, b, o0, o1):
        return lambda: self.nc.vector.scalar_tensor_tensor(out=out, in0=a, scalar=s, in1=b, op0=o0, op1=o1)

    def cp(self, out, a):
        return lambda: self.nc.vector.tensor_copy(out, a)

    def mm(self, out, l, r, start=True, stop=True):
        return lambda: self.nc.tensor.matmul(out, l, r, start=start, stop=stop)

    def tr(self, out, in_):
        return lambda: self.nc.tensor.transpose(out, in_, self.C("ident"))


class Program(Instructions):

    def __init__(self, nc, ctx, xin, wst, vec, cst, fvb, cbd, out):
        self.xs = nc.dram_tensor("x_spill", (1024, S), F32, kind="Internal").ap()
        self.ys = nc.dram_tensor("y_spill", (1024, S), F32, kind="Internal").ap()
        self.nc, self.Q = nc, Queues()
        self.xin, self.wst, self.vec_d, self.cst_d, self.fvb, self.cbd, self.out = xin, wst, vec, cst, fvb, cbd, out
        self.slots = plan()
        sb = lambda n, s, d=F32: ctx.enter_context(nc.sbuf_tensor(n, s, d))
        self.RAWT = sb("wraw", [128, RAW, SLOT])
        self.WH = sb("wh", [128, RING, SLOT], F32R)
        self.WL = sb("wl", [128, RING, SLOT], F32R)
        self.AH = sb("ah", [128, 8, S], F32R)
        self.AL = sb("al", [128, 8, S], F32R)
        self.HH = sb("hh", [128, 8, S], F32R)
        self.HL = sb("hl", [128, 8, S], F32R)
        self.VEC = sb("vecs", [128, NVEC])
        self.CST = sb("csts", [128, NCONST])
        self.MOD = sb("mod", [128, 48])
        self.SC = sb("scr", [128, 64])
        self.IDB = sb("identb", [128, 128], BF16)
        self.TRB = sb("trib", [128, 2, 128], BF16)
        self.XT = sb("xt", [128, 8, S])
        self.AR = sb("arena", [128, ARENA])
        self.PS = [ctx.enter_context(nc.psum_tensor(f"ps{i}", [128, 512], F32)) for i in range(8)]
        self.slot = -1
        if START > 1:
            pre = {2: "w_ada_2", 3: "ffn1_w_gate_3"}[START]
            self.slot = [i for i, x in enumerate(self.slots) if x[1][0][0] == pre][0] - 1
        self.slot0 = self.slot + 1
        self.blk = 0
        self.mm_slots = [i for i, x in enumerate(self.slots) if x[0] == "mm" and i >= self.slot0]
        self.mth = {n: m for m, n in enumerate(self.mm_slots)}
        self.through, c = {}, 0
        for i in range(self.slot0, len(self.slots)):
            c += sum(counted(b) for b in self.slots[i][1]) if self.slots[i][0] != "ada" else 0
            self.through[i] = c
        self.g, self.passed = 0, [0, 0, 0, 0]
        self.nsplit = 0
        self.adat = None
        self.side = iter(())

    def C(self, name):
        i = CONSTS.index(name)
        return self.CST[:, 128 * i:128 * i + 128]

    def V(self, name, j=0, n=1):
        o = VOFF[name][0]
        return self.VEC[:, o + j:o + j + n]

    def arena(self, off, *shape):
        n = 1
        for s in shape:
            n *= s
        assert off + n <= ARENA, (off, n)
        ap = self.AR[:, off:off + n]
        if len(shape) == 2:
            ap = ap.rearrange("p (a b) -> p a b", a=shape[0])
        if len(shape) == 3:
            ap = ap.rearrange("p (a b c) -> p a b c", a=shape[0], b=shape[1])
        return ap

    def load(self, n):
        if n >= len(self.slots):
            return
        waits = []
        o = n - RAW
        if o >= self.slot0:
            if self.slots[o][0] == "mm":
                waits = [("hi", self.mth[o] + 1), ("lo", self.mth[o] + 1)]
            elif self.slots[o][0] == "ada":
                waits = [("ada", 2 * sum(x[0] == "ada" for x in self.slots[self.slot0:o + 1]))]
            else:
                waits = [("blk", self.through[o])]
        w = sum(b[2] * b[4] for b in self.slots[n][1])
        dst, src = self.RAWT[:, n % RAW, 0:w], self.wst[n][:, 0:w]
        self.Q.dma(f"w{n % RAW}", lambda: self.nc.sync.dma_start(dst, src), waits)

    def arrived(self, n):
        return (f"w{n % RAW}", 16 * ((n - self.slot0) // RAW + 1))

    def split_slot(self, n):
        m = self.mth[n]
        w = sum(b[2] * b[4] for b in self.slots[n][1])
        src = self.RAWT[:, n % RAW, 0:w]
        hi, lo = self.WH[:, m % RING, 0:w], self.WL[:, m % RING, 0:w]
        waits = [self.arrived(n)]
        if m >= RING:
            waits.append(("blk", self.through[self.mm_slots[m - RING]]))
        self.Q.op("act", self.act(hi, src), waits, sem="hi")
        self.Q.op("dve", self.tt(lo, src, hi.bitcast(F32), SUB), [*waits, ("hi", m + 1)], sem="lo")
        self.load(n + RAW)

    def enter(self, n):
        if n > self.slot0 and self.slots[n - 1][0] != "mm":
            self.load(n - 1 + RAW)
        self.slot, self.blk = n, 0
        mm = self.slots[n][0] == "mm"
        reach = n + 2 if mm else n + 1
        while self.nsplit < len(self.mm_slots) and self.mm_slots[self.nsplit] <= reach and \
                sum(x < n or (mm and x == n) for x in self.mm_slots) + 1 > self.nsplit:
            self.split_slot(self.mm_slots[self.nsplit])
            self.nsplit += 1

    def next_block(self, name):
        while self.slot < self.slot0 or self.blk == len(self.slots[self.slot][1]):
            self.ride()
            self.enter(self.slot + 1)
        kind, blocks = self.slots[self.slot]
        b = blocks[self.blk]
        assert b[0] == name, (b, name)
        off = sum(x[2] * x[4] for x in blocks[:self.blk])
        self.blk += 1
        view = lambda t, i: t[:, i, off:off + b[2] * b[4]].rearrange("p (k c) -> p k c", k=b[2])
        if kind == "raw":
            return view(self.RAWT, self.slot % RAW), None, [self.arrived(self.slot)]
        m = self.mth[self.slot]
        return view(self.WH, m % RING), view(self.WL, m % RING), [("hi", m + 1), ("lo", m + 1)]

    def triple(self, out, wh, wl, xh, xl, first, last, waits, moving_w=False, count=False):
        Q = self.Q
        if moving_w:
            pairs = [(xh, wh), (xh, wl), (xl, wh)]
        else:
            pairs = [(wh, xh), (wh, xl), (wl, xh)]
        for i, (l, r) in enumerate(pairs):
            t = Q.op("pe", self.mm(out, l, r, first and i == 0, last and i == 2), waits if i == 0 else (),
                     sem="blk", inc=i == 2 and (last or count))
        return t

    def emptied(self, g):
        return (f"ev{g % 4}", g // 4 - self.passed[g % 4])

    def gemm(self, *args, **kw):
        for _ in self.gemm_steps(*args, **kw):
            pass

    def gemm_steps(self, name, ntiles, xh, xl, evac, deps=(), x0=0, xk=None, banks=(0, 1, 2, 3)):
        for j in range(ntiles):
            wh, wl, wt = self.next_block(name)
            while self.g % 4 not in banks:
                self.passed[self.g % 4] += 1
                self.g += 1
            bank, empty = self.g % 4, self.emptied(self.g)
            ps = self.PS[bank]
            nk = wh.shape[1]
            for k in range(nk):
                t = self.triple(ps[:], wh[:, k, :], wl[:, k, :], xh[:, x0 + k, :], xl[:, x0 + k, :], k == 0,
                                k == nk - 1, ([*wt, empty, *deps] if k == 0 else []) + (xk[k] if xk and j == 0 else []))
                if k < nk - 1:
                    yield
            evac(j, ps[:], t, f"ev{bank}")
            self.g += 1
            next(self.side, None)
            yield

    def gemm_tm(self, name, ncol, evac, deps=()):
        rows = 0
        toks = []
        while rows < 8:
            wh, wl, wt = self.next_block(name)
            nk = wh.shape[1]
            for t4 in range(NT):
                bank, empty = (self.g + t4) % 4, self.emptied(self.g + t4)
                for k in range(nk):
                    kk = rows + k
                    c = slice(t4 * 128, t4 * 128 + 128)
                    t = self.triple(self.PS[bank][:, 0:ncol], wh[:, k, :], wl[:, k, :], self.AH[:, kk, c],
                                    self.AL[:, kk, c], kk == 0, kk == 7,
                                    [*wt, empty, *deps] if k == 0 else (), moving_w=True,
                                    count=t4 == 3 and k == nk - 1)
                toks.append(t)
                next(self.side, None)
            rows += nk
        for t4 in range(NT):
            bank = (self.g + t4) % 4
            evac(t4, self.PS[bank][:, 0:ncol], toks[t4 - 4], f"ev{bank}")
        self.g += 4

    def split(self, v, hi, lo, deps):
        a = self.Q.op("act", self.act(hi, v), deps)
        d = self.Q.op("dve", self.tt(lo, v, hi.bitcast(F32), SUB), [*deps, a])
        return [a, d]

    def stat(self, after, src, n, bank, square, tmp, each=None):
        Q, ps = self.Q, self.PS[bank]
        read = [[], []]
        for t in range(n):
            r, w = src[:, t, :], each[t] if each else []
            if square:
                r = tmp[:, t % 2, :]
                w = [Q.op("act", self.act(r, src[:, t, :], ACT.Square), [*after, *w, *read[-2]])]
            read.append([Q.op("pe", self.mm(ps[:], self.C("ones"), r, t == 0, t == n - 1), [*after, *w])])
        return ps, read[-1]

    def rstd(self, after, out, ps, inv, eps, refine=None):
        Q, v = self.Q, out if refine is None else refine[0]
        t = Q.op("dve", self.ts(v, ps, inv, eps, MUL, ADD), after)
        t = Q.op("dve", lambda: self.nc.vector.reciprocal(out, v), [t])
        t = Q.op("act", self.act(out, out, ACT.Sqrt), [t])
        if refine is not None:
            w = refine[1]
            t = Q.op("dve", self.tt(w, v, out, MUL), [t])
            t = Q.op("dve", self.tt(w, w, out, MUL), [t])
            t = Q.op("dve", self.ts(w, w, -0.5, 1.5, MUL, ADD), [t])
            t = Q.op("dve", self.tt(out, out, w, MUL), [t])
        return [t]

    def rms(self, src, n, width, eps, off, scale, bias, hi, lo, dst0=0, summed=None, refine=False):
        after = self.Q.now(*ALL)
        tmp, rs, v = self.arena(off, 2, S), self.arena(off + 1024, S), self.arena(off + 1536, 2, S)
        if summed is None:
            _, summed = self.stat(after, src, n, 4, True, tmp)
        after = self.rstd([*after, *summed], rs, self.PS[4][:], 1.0 / width, eps, (v[:, 0, :], v[:, 1, :]) if refine else None)
        return self.affine(after, src, n, rs, scale, bias, hi, lo, dst0, tmp, v, refine)

    def affine(self, after, src, n, rs, scale, bias, hi, lo, dst0, tmp, v, on_dve=False):
        Q = self.Q
        parts = [[], []]
        for t in range(n):
            y = tmp[:, t % 2, :]
            z = v[:, t % 2, :]
            if bias is None:
                b = Q.op("dve", self.stt(z, src[:, t, :], scale(t), rs, MUL, MUL), [*after, *parts[-2]])
            else:
                a = Q.op("dve", self.tt(y, src[:, t, :], rs, MUL), [*after, *parts[-2]])
                if on_dve:
                    b = Q.op("dve", self.ts(z, y, scale(t), bias(t), MUL, ADD), [a])
                else:
                    b = Q.op("act", self.act(z, y, ACT.Identity, scale=scale(t), bias=bias(t)), [a])
            parts.append(self.split(z, hi[:, dst0 + t, :], lo[:, dst0 + t, :], [b]))
        return parts[2:]

    def ln_center(self, after, src, n, width, dst, tmp, rs, eps, summed=None):
        Q = self.Q
        if summed is None:
            _, summed = self.stat(after, src, n, 4, False, None)
        mean = Q.op("act", self.act(rs, self.PS[4][:], ACT.Copy, scale=1.0 / width), [*after, *summed])
        centred = [[Q.op("dve", self.tt(dst[:, t, :], src[:, t, :], rs, SUB), [mean])] for t in range(n)]
        ps, summed = self.stat([mean], dst, n, 5, True, tmp, centred)
        return self.rstd([*summed, *centred[-1]], rs, ps[:], 1.0 / width, eps)

    def summing(self, square, off, evac):
        Q, tmp, read, ready = self.Q, self.arena(off, 2, S), [[], []], []
        first = Q.now(*ALL)

        def add(j):
            r = tmp[:, j % 2, :] if square else self.XT[:, j, :]
            read.append([Q.op("pe", self.mm(self.PS[4][:], self.C("ones"), r, j == 0, j == 7), [*first, ready[j]])])

        def ev(j, ps, t, ev):
            x = evac(j, ps, t, ev)[0]
            if square:
                x = Q.op("act", self.act(tmp[:, j % 2, :], self.XT[:, j, :], ACT.Square), [*first, x, *read[-1]])
            ready.append(x)
            if j:
                add(j - 1)
            if j == 7:
                add(7)
                done.extend(read[-1])

        done = []
        return ev, done

    def ada_begin(self, c, off, dst, start):
        Q = self.Q
        self.cb, self.dump, self.adst = self.arena(off, 1024), self.arena(off + 1024, 1024), dst
        cb = self.cb
        t = Q.dma("cb", lambda: self.nc.sync.dma_start(cb, self.cbd[c]), start)
        th = Q.op("act", self.act(self.dump, self.cb, ACT.Tanh, scale=0.5), [t])
        self.cbt = Q.op("dve", self.stt(self.cb, self.dump, 1.0, self.cb, ADD, MUL), [th])

    def ride(self):
        while self.slot + 1 < len(self.slots) and self.slots[self.slot + 1][0] == "ada":
            self.enter(self.slot + 1)
            self.ada_slot()

    def ada_slot(self):
        n = self.slot
        for i, b in enumerate(self.slots[n][1]):
            j = b[3] // 128
            src = self.RAWT[:, n % RAW, 1024 * i:1024 * i + 1024]
            self.Q.op("dve", lambda src=src, j=j, cb=self.cb, dump=self.dump, dst=self.adst:
                      self.nc.vector.scalar_tensor_tensor(out=dump, in0=src, scalar=0.5, in1=cb, op0=MUL, op1=MUL,
                                                          accum_out=dst[:, j:j + 1]),
                      [self.arrived(n), self.cbt, *([self.adat] if self.adat else [])], sem="ada")
            self.adat = ("ada", self.Q.n["ada"])
        self.blk = len(self.slots[n][1])

    def ada_bias(self, src, bvec, j0, j1):
        self.Q.op("dve", self.tt(self.MOD[:, j0:j1], src[:, j0:j1], self.V(bvec, j0, j1 - j0), ADD),
                  self.Q.now(*ALL, "ada"))

    def shift_scale(self):
        Q = self.Q
        half, ca, c = self.SC[:, 44:52], self.SC[:, 52:60], self.V("c", 0, 8)
        start = [self.vtok]
        th = Q.op("act", self.act(ca, c, ACT.Tanh, scale=0.5), start)
        hf = Q.op("dve", self.ts(half, c, 0.5), start)
        silu = Q.op("dve", self.stt(ca, ca, 1.0, half, ADD, MUL), [th, hf])
        ps = self.PS[5]
        for j in range(16):
            w, _, wt = self.next_block("w_ada")
            for k in range(8):
                t = Q.op("pe", self.mm(ps[:, j:j + 1], w[:, k, :], ca[:, k:k + 1], k == 0, k == 7),
                         [*wt, silu] if k == 0 else (), sem="blk", inc=k == 7)
        Q.op("dve", self.tt(self.MOD[:, 0:16], ps[:, 0:16], self.V("b_ada", 0, 16), ADD), [t])

    def scaled(self, g, part):
        start = self.Q.now(*ALL)
        m = self.MOD[:, 8 * part:8 * part + 8]
        if g is None:
            self.Q.op("dve", self.ts(self.SC[:, 0:8], m, 1.0, None, ADD), start)
        else:
            self.Q.op("dve", self.stt(self.SC[:, 0:8], m, 1.0, self.V(g, 0, 8), ADD, MUL), start)

    def attention(self, qT, kT, v, add, out, p, pT, st, deps, scale, before=None):
        Q, PS = self.Q, self.PS
        N = [(i, h) for i in range(NT) for h in range(8)]
        tmax, texp, ttr, tcp, tpv = {}, {}, {}, {}, {}
        for n in range(len(N) + 2):
            if n < len(N):
                i, h = N[n]
                if before:
                    before(i, h)
                w = 128 * (i + 1)
                ps = PS[4 + n % 2]
                q0 = 64 * (h % 2)
                Q.op("pe", self.mm(ps[:, 0:w], qT[q0:q0 + 64, h // 2, 128 * i:128 * i + 128],
                                   kT[q0:q0 + 64, h // 2, 0:w], True, False),
                     [*deps, *([texp[n - 2]] if n >= 2 else [])], inc=False)
                tl = add(i, h, ps, w)
                mx, nb, rs = st[:, 0, n:n + 1], st[:, 1, n:n + 1], st[:, 2, n:n + 1]
                psw = ps[:, 0:w]
                tm_ = Q.op("dve", lambda mx=mx, psw=psw: self.nc.vector.reduce_max(mx, psw, AX), [tl])
                tmax[n] = Q.op("dve", self.ts(nb, mx, -scale), [tm_])
                texp[n] = Q.op("act", self.act(p[:, n % 2, 0:w], psw, ACT.Exp, bias=nb, scale=scale, accum_out=rs),
                               [tmax[n], *([ttr[n - 2]] if n >= 2 else [])])
            m = n - 1
            if 0 <= m < len(N):
                i, h = N[m]
                ps = PS[6 + m % 2]
                for j in range(i + 1):
                    t = Q.op("pe", self.tr(ps[:, 128 * j:128 * j + 128], p[:, m % 2, 128 * j:128 * j + 128]),
                             [texp[m], *([tcp[m - 2]] if m >= 2 else [])], inc=j == i)
                ttr[m] = t
                w = 128 * (i + 1)
                dst, src = pT[:, m % 2, 0:w], ps[:, 0:w]
                wt = [t, *([tpv[m - 2]] if m >= 2 else [])]
                tcp[m] = Q.op("act", self.act(dst, src), wt) if m % 2 else Q.op("dve", self.cp(dst, src), wt)
            m = n - 2
            if 0 <= m < len(N):
                i, h = N[m]
                bank, empty = (self.g + i) % 4, self.emptied(self.g + i)
                ob = PS[bank]
                for j in range(i + 1):
                    t = Q.op("pe", self.mm(ob[:, 64 * h:64 * h + 64], pT[:, m % 2, 128 * j:128 * j + 128],
                                           v(j, h), j == 0, j == i),
                             [tcp[m], empty], inc=j == i)
                tpv[m] = t
                if h == 7:
                    rs8 = st[:, 2, 8 * i:8 * i + 8]
                    ri8 = st[:, 3, 8 * i:8 * i + 8]
                    a = Q.op("dve", lambda ri8=ri8, rs8=rs8: self.nc.vector.reciprocal(ri8, rs8), [texp[m]])
                    o3 = out[:, i, :].rearrange("p (h d) -> p h d", h=8)
                    s3 = ob[:].rearrange("p (h d) -> p h d", h=8)
                    Q.op("dve", self.tt(o3, s3, ri8.unsqueeze(2).to_broadcast([128, 8, 64]), MUL), [a, t], sem=f"ev{bank}")
        self.g += NT

    def transpose_to(self, src, ntiles, evac):
        base = self.Q.now(*ALL)
        emptied = [[], [], [], []]
        for j in range(ntiles):
            b = 4 + j % 4
            for t in range(NT):
                tok = self.Q.op("pe", self.tr(self.PS[b][:, 128 * t:128 * t + 128], src(t, j)),
                                [*base, *emptied[j]], inc=t == 3)
            emptied.append(evac(j, self.PS[b][:], tok, None))

    def residual_evac(self, gate, extra=None):
        def ev(j, ps, t, ev):
            x = self.XT[:, j, :]
            g = gate if isinstance(gate, float) else gate(j)
            return [self.Q.op("dve", self.stt(x, ps, g, x, MUL, ADD), [t, *self.Q.now("dve", "ev0", "ev1", "ev2", "ev3")], sem=ev)]
        return ev

    def swiglu(self, gname, uname, dname, gate, off, atok, xk=None, square=True):
        Q = self.Q
        v = self.arena(off, 2, 2, S)
        act, parts = [], [[], []]
        read = []
        for n in (8, 7, 7):
            for j in range(n):
                g, z = v[:, j % 2, 0, :], v[:, j % 2, 1, :]

                def evg(_, ps, t, ev, g=g):
                    act.append(Q.op("act", self.act(g, ps, ACT.Silu), [t, *parts[-2]], sem=ev))

                def evu(_, ps, t, ev, j=j, g=g, z=z):
                    b = Q.op("dve", self.tt(z, ps, g, MUL), [t, act[-1], *parts[-2]], sem=ev)
                    parts.append(self.split(z, self.HH[:, j, :], self.HL[:, j, :], [b, *read]))

                self.gemm(gname, 1, self.AH, self.AL, evg, deps=atok, xk=xk)
                self.gemm(uname, 1, self.AH, self.AL, evu, deps=atok)
            evd, done = self.residual_evac(gate), []
            if len(parts) == 24:
                evd, done = self.summing(square, off + 2048, evd)
            self.gemm(dname, 8, self.HH, self.HL, evd, xk=parts[-n:])
            read = Q.now("blk")
        return done

    def build(self):
        nc, Q = self.nc, self.Q
        t1 = Q.dma("v", lambda: nc.sync.dma_start(self.VEC[:], self.vec_d))
        t2 = Q.dma("c", lambda: nc.sync.dma_start(self.CST[:], self.cst_d))
        t3 = Q.dma("x", lambda: nc.sync.dma_start(self.XT[:], self.xin.rearrange("(k p) t -> p k t", p=128)))
        for i in range(RAW):
            self.load(self.slot0 + i)
        self.vtok, self.xtok = t1, t3
        a = Q.op("dve", self.cp(self.IDB[:], self.C("ident")), [t1, t2])
        Q.op("dve", self.cp(self.TRB[:, 0, :], self.C("tri")), [a])
        Q.op("act", self.act(self.TRB[:, 1, :], self.C("triT")), [t2, t3, t1])
        Q.op("pool", lambda: nc.gpsimd.memset(self.SC[:, 0:44], 0.0))
        Q.op("pe", self.tr(self.PS[7][:, 0:128], self.C("ident")), [t1, t2, t3])
        summed = None
        if START <= 1:
            summed = self.block1()
        if STOP == 1:
            return self.finish([Q.now(*ALL)] * 8)
        if START <= 2:
            summed = self.block2(summed)
        if STOP == 2:
            return self.finish([Q.now(*ALL)] * 8)
        self.finish(self.block3(summed))

    def finish(self, each):
        o = self.out.rearrange("(k p) t -> p k t", p=128)
        for k in range(8):
            t = self.Q.dma("out", lambda k=k: self.nc.sync.dma_start(o[:, k, :], self.XT[:, k, :]), each[k])
        self.Q.op("sp", None, [t], inc=False)

    def block1(self):
        nc, Q, M = self.nc, self.Q, self.MOD
        _, summed = self.stat([self.xtok, *Q.now(*ALL)], self.XT, 8, 4, True, self.arena(0, 2, S))
        self.shift_scale()
        self.ada_begin(0, 14848, M, [])
        self.scaled("g_norm1", 1)
        xk = self.rms(self.XT, 8, 1024, 1e-6, 0, lambda t: self.SC[:, t:t + 1], lambda t: M[:, t:t + 1], self.AH, self.AL,
                      summed=summed, refine=True)
        at = xk[-1]
        U = self.arena(8480, 4, 542)
        Y = self.arena(8480 + 2168, 4, S)
        z = Q.op("pool", lambda: nc.gpsimd.memset(U[:, :, 0:30], 0.0))
        ut, ya = {}, []
        self.gemm("w_in", 4, self.AH, self.AL,
                  lambda j, ps, t, ev: ya.append(Q.op("act", self.act(Y[:, j, :], ps), [t], sem=ev)), xk=xk)
        SG = self.arena(12800, 4, S)

        def evg(j, ps, t, ev):
            a = Q.op("act", self.act(SG[:, j, :], ps, ACT.Sigmoid), [t], sem=ev)
            ut[j] = Q.op("dve", self.tt(U[:, j, 30:542], Y[:, j, :], SG[:, j, :], MUL), [a, ya[j]])
            return [a]

        self.gemm("w_in", 4, self.AH, self.AL, evg, deps=at)
        conv = {}

        def taps():
            for k in range(31):
                for t in range(4):
                    y, u, w = Y[:, t, :], U[:, t, k:k + 512], self.V("w_dw", 31 * t + k)
                    if k == 0:
                        conv[t] = Q.op("dve", self.ts(y, u, w, self.V("b_dw", t), MUL, ADD), [ut[t], z])
                    else:
                        conv[t] = Q.op("dve", self.stt(y, u, w, y, MUL, ADD), [conv[t]])
                yield

        TM = self.arena(0, 4, 2120)
        base = xk[-1]
        self.side = taps()
        for c in range(4):
            def ev(t, ps, tok, ev, c=c):
                dst = TM[:, t, 512 * c:512 * c + 512]
                return [Q.op("act", self.act(dst, ps), [tok, *base], sem=ev)]
            self.gemm_tm("w_in", 512, ev, deps=at)
        self.gemm_tm("w_in", 72, lambda t, ps, tok, ev: [Q.op("act", self.act(TM[:, t, 2048:2120], ps), [tok, *base], sem=ev)], deps=at)
        for _ in self.side:
            pass
        start = Q.now(*ALL)

        def conv_norm(_):
            tmp, rs, v = self.arena(12800, 2, S), self.arena(13824, S), self.arena(14336, 2, S)
            _, summed = self.stat(start, Y, 4, 4, False, None)
            mean = Q.op("act", self.act(rs, self.PS[4][:], ACT.Copy, scale=1.0 / 512), summed)
            yield
            each = [[Q.op("dve", self.tt(Y[:, t, :], Y[:, t, :], rs, SUB), [mean])] for t in range(4)]
            yield
            _, summed = self.stat([mean], Y, 4, 5, True, tmp, each)
            yield
            after = self.rstd([*summed, *each[-1]], rs, self.PS[5][:], 1.0 / 512, 1e-6)
            yield
            each = []
            for t in range(4):
                a = Q.op("dve", self.tt(Y[:, t, :], Y[:, t, :], rs, MUL), after)
                a = Q.op("act", self.act(Y[:, t, :], Y[:, t, :], ACT.Silu, scale=self.V("g_conv_ln", t),
                                         bias=self.V("b_conv_ln", t)), [a])
                each.append([a])
            yield
            _, summed = self.stat([], Y, 4, 4, True, tmp, each)
            yield
            after = self.rstd(summed, rs, self.PS[4][:], 1.0 / 512, 1e-6)
            yield
            self.affine(after, Y, 4, rs, lambda t: self.V("g_out_conv", t), None, self.HH, self.HL, 4, tmp, v)

        ST = self.arena(8480 + 2048, 64)
        R4 = self.arena(8480, 4, 24 * 8)

        def query_key(_):
            SQ = self.arena(8480, 2, 1024)
            after, done = start, []
            for i in (0, 2):
                for t in (0, 1):
                    done += [Q.op("act", self.act(SQ[:, t, :], TM[:, i + t, 0:1024], ACT.Square), after)]
                after, done = done, []
                yield
                done += [Q.op("dve", lambda i=i: nc.vector.reduce_sum(ST[:, 16 * i:16 * i + 32], SQ.rearrange("p t (h d) -> p (t h) d", d=64), AX), after)]
                after, done = done, []
                yield
            done += [Q.op("dve", self.ts(ST, ST, 1.0 / 64, 1e-6, MUL, ADD), after)]
            after, done = done, []
            done += [Q.op("dve", lambda: nc.vector.reciprocal(ST, ST), after)]
            after, done = done, []
            done += [Q.op("act", self.act(ST, ST, ACT.Sqrt), after)]
            after, done = done, []
            yield
            for t in range(4):
                qk = TM[:, t, 0:1024].rearrange("p (h d) -> p h d", d=64)
                done += [Q.op("dve", self.tt(qk, qk, ST[:, 16 * t:16 * t + 16].unsqueeze(2).to_broadcast([128, 16, 64]), MUL), after)]
                if t % 2:
                    yield
            after, done = done, []
            for g, o in (("g_q", 0), ("g_k", 512)):
                for t in range(4):
                    x = TM[:, t, o:o + 512].rearrange("p (h d) -> p h d", d=64)
                    done += [Q.op("dve", self.tt(x, x, self.V(g, 0, 64).unsqueeze(1).to_broadcast([128, 8, 64]), MUL), after)]
                yield
            after, done = done, []
            RO = self.CST[:, 128 * len(CONSTS):128 * len(CONSTS) + 64].rearrange("p (s t f) -> p s t f", s=2, t=4)
            for t in range(4):
                for x, nh in ((TM[:, t, 0:1536].rearrange("p (h d) -> p h d", d=64), 24),
                              (TM[:, t, 2048:2112].rearrange("p (h d) -> p h d", d=64), 1)):
                    x1, x2 = x[:, :, 0:8], x[:, :, 8:16]
                    c = RO[:, 0, t, :].unsqueeze(1).to_broadcast([128, nh, 8])
                    s = RO[:, 1, t, :].unsqueeze(1).to_broadcast([128, nh, 8])
                    r = [R4[:, i, 0:nh * 8].rearrange("p (h f) -> p h f", h=nh) for i in range(4)]
                    done += [Q.op("dve", self.tt(r[0], x1, c, MUL), after)]
                    done += [Q.op("dve", self.tt(r[1], x2, s, MUL), after)]
                    done += [Q.op("dve", self.tt(r[2], x2, c, MUL), after)]
                    done += [Q.op("dve", self.tt(r[3], x1, s, MUL), after)]
                    after, done = done, []
                    done += [Q.op("dve", self.tt(x1, r[0], r[1], SUB), after)]
                    done += [Q.op("dve", self.tt(x2, r[2], r[3], ADD), after)]
                    after, done = done, []
                yield

        self.abreast([conv_norm, query_key], 2)
        after, done = Q.now(*ALL), []
        IK2 = self.arena(8480, 4, 128)
        for t in range(4):
            for r in range(2):
                done += [Q.op("dve", self.cp(IK2[:, t, 64 * r:64 * r + 64], TM[:, t, 2048:2112]), after)]
        IW = self.arena(8480 + 512, 32)
        done += [Q.op("dve", self.ts(IW.rearrange("p (t h) -> p t h", t=4), TM[:, :, 2112:2120], 8.0 ** -0.5), after)]
        after, done = done, []
        QKT = self.arena(8480 + 544, 13, S)

        def evt(j, ps, tok, ev):
            return [Q.op("act", self.act(QKT[:, j, :], ps), [tok], sem=ev)] if j % 2 else [Q.op("dve", self.cp(QKT[:, j, :], ps), [tok], sem=ev)]

        self.transpose_to(lambda t, j: TM[:, t, 128 * j:128 * j + 128] if j < 12 else IK2[:, t, :], 13, evt)
        qT, kT, iqT, ikT = QKT[:, 0:4, :], QKT[:, 4:8, :], QKT[:, 8:12, :], QKT[:, 12, :]
        NM = self.arena(15680, 1024).bitcast(BF16).rearrange("p (i s) -> p i s", i=4)
        SCR = self.arena(0, 4, 2120)
        f = Q.now(*ALL)
        acc_, rel_ = SCR[:, 0, 1024:1536], [SCR[:, 1, 1024:1536], SCR[:, 2, 1024:1536]]
        eq_, gt_, cum_ = SCR[:, 3, 1024:1536], self.arena(8480, 512), self.arena(16832, 512)
        m8, cnt = self.arena(17344, 8), self.arena(17352, 1)
        known = {}

        def select():
            a = Q.op("dve", lambda: nc.vector.memset(NM[:, 0, 0:128], 0.0), f)
            known[0] = Q.op("dve", lambda: nc.vector.memset(NM[0:64, 0, 64:128], -BIG), [a])
            relu, mac = [], [known[0], known[0]]
            for i in range(1, NT):
                w = 128 * (i + 1)
                acc, eq, gt, cum = acc_[:, 0:w], eq_[:, 0:w], gt_[:, 0:w], cum_[:, 0:w]
                for h in range(8):
                    g = self.g + i + h % 2 if i + h % 2 < NT else self.g
                    bank, free = self.PS[g % 4], (f"ev{g % 4}", g // 4 + (i + h % 2 == NT))
                    q0 = 64 * (h % 2)
                    t = Q.op("pe", self.mm(bank[:, 0:w], iqT[q0:q0 + 64, h // 2, 128 * i:128 * i + 128],
                                           ikT[q0:q0 + 64, 0:w]), [*f, free, *relu[-1 if h == 0 else -2:][:1]])
                    rel = rel_[h % 2][:, 0:w]
                    relu.append(Q.op("act", self.act(rel, bank[:, 0:w], ACT.Relu, scale=0.125), [t, mac[-2]]))
                    iw = IW[:, 8 * i + h:8 * i + h + 1]
                    if h == 0:
                        mac.append(Q.op("dve", self.ts(acc, rel, iw), [relu[-1], mac[-1]]))
                    else:
                        mac.append(Q.op("dve", self.stt(acc, rel, iw, acc, MUL, ADD), [relu[-1], mac[-1]]))
                    yield
                a = Q.op("dve", lambda acc=acc, i=i: nc.vector.memset(acc[0:64, 128 * i + 64:128 * i + 128], NEG), [mac[-1]])
                src = acc
                for r in range(16):
                    a = Q.op("dve", lambda src=src: nc.vector.max(m8, src), [a])
                    if r < 15:
                        a = Q.op("dve", lambda src=src, eq=eq: nc.vector.match_replace(eq, m8, src, NEG), [a])
                    src = eq
                    yield
                th = m8[:, 7:8]
                b = Q.op("dve", self.ts(gt, acc, th, None, ALU.is_gt), [a])
                a = Q.op("dve", self.ts(eq, acc, th, None, ALU.is_equal), [a])
                b = Q.op("dve", lambda gt=gt: nc.vector.reduce_sum(cnt, gt, AX), [b])
                ones = rel_[0][:, 0:w]
                a = Q.op("dve", lambda ones=ones: nc.vector.memset(ones, 1.0), [a])
                a = Q.op("dve", lambda ones=ones, eq=eq, cum=cum: nc.vector.tensor_tensor_scan(cum, ones, eq, 0.0, MUL, ADD), [a])
                mac += [a, a]
                b = Q.op("dve", self.ts(cnt, cnt, -1.0, 128.0, MUL, ADD), [b])
                yield
                a = Q.op("dve", self.stt(eq, cum, cnt, eq, ALU.is_le, MUL), [a, b])
                a = Q.op("dve", self.tt(eq, eq, gt, ADD), [a])
                known[i] = Q.op("dve", self.ts(NM[:, i, 0:w], eq, -1.0, BIG, ADD, MUL), [a])
                yield

        steps = select()
        AT = SCR[:, :, 0:512]
        PP = SCR[:, 0:2, 512:1024]
        PT = SCR[:, 2:4, 512:1024]
        ST4 = self.arena(16704, 4, 32)

        def add(i, h, ps, w):
            return Q.op("pe", self.mm(ps[:, 0:w], self.IDB[:], NM[:, i, 0:w], False, True), [known[i]])

        def before(i, h):
            while i not in known:
                next(steps)
            if h and i:
                for _ in range(4):
                    next(steps, None)

        self.attention(qT, kT, lambda j, h: TM[:, j, 1536 + 64 * h:1600 + 64 * h], add, AT, PP, PT, ST4, f, 0.125, before)
        after, done = Q.now(*ALL), []
        ss = SCR[:, 0, 1024:1028]
        for t in range(4):
            done += [Q.op("act", self.act(SCR[:, t, 512:1024], AT[:, t, :], ACT.Square, accum_out=ss[:, t:t + 1]), after)]
        after, done = done, []
        after = self.rstd(after, ss, ss, 1.0 / 512, 1e-6)
        for t in range(4):
            done += [Q.op("dve", self.ts(AT[:, t, :], AT[:, t, :], ss[:, t:t + 1]), after)]
        after, done = done, []
        YT = QKT

        def evo(j, ps, tok, ev):
            a = Q.op("dve", self.ts(YT[:, j, :], ps, self.V("g_out_attn", j)), [tok], sem=ev)
            self.split(YT[:, j, :], self.HH[:, j, :], self.HL[:, j, :], [a])
            return [a]

        self.transpose_to(lambda t, j: AT[:, t, 128 * j:128 * j + 128], 4, evo)
        self.ada_begin(0, 6144, M, Q.now(*ALL))
        self.ada_bias(M, "b_ada", 16, 40)
        evd, summed = self.summing(True, 4096, self.residual_evac(lambda j: M[:, 16 + j:17 + j]))
        self.gemm("w_out", 8, self.HH, self.HL, evd, deps=Q.now(*ALL))
        self.scaled("g_norm2", 4)
        xk = self.rms(self.XT, 8, 1024, 1e-6, 2048, lambda t: self.SC[:, t:t + 1], lambda t: M[:, 24 + t:25 + t],
                      self.AH, self.AL, summed=summed)
        self.ride()
        self.ada_bias(M, "b_ada", 40, 48)
        self.sums2 = self.arena(8192, 48)
        self.ada_begin(1, 6144, self.sums2, Q.now(*ALL, "ada"))
        R = self.arena(0, 2, 2, S)
        parts = [[], []]
        for q in range(4):
            read = Q.now("blk")

            def evr(j, ps, t, ev):
                r, z = R[:, j % 2, 0, :], R[:, j % 2, 1, :]
                a = Q.op("act", self.act(r, ps, ACT.Relu), [t, *parts[-2]], sem=ev)
                b = Q.op("dve", self.tt(z, r, r, MUL), [a, *parts[-2]])
                parts.append(self.split(z, self.HH[:, j, :], self.HL[:, j, :], [b, *read]))

            self.gemm("w_ff1", 8, self.AH, self.AL, evr, xk=xk)
            evd = self.residual_evac(lambda j: M[:, 40 + j:41 + j])
            if q == 3:
                evd, summed = self.summing(False, 4096, evd)
            self.gemm("w_ff2", 8, self.HH, self.HL, evd, xk=parts[-8:])
        return summed

    def block2(self, summed):
        nc, Q, M = self.nc, self.Q, self.MOD
        if START == 2:
            self.sums2 = self.arena(8192, 48)
            self.ada_begin(1, 6144, self.sums2, self.Q.now(*ALL))
            self.ride()
        self.ada_bias(self.sums2, "b_ada_2", 0, 48)
        xk = self.ln_mod(1, 0, summed)
        at = xk[-1]
        GA = self.arena(0, 6, S)
        self.gemm("w_gates_2", 2, self.AH, self.AL,
                  lambda j, ps, t, ev: [Q.op("act", self.act(GA[:, j, :], ps, ACT.Identity, bias=self.V("b_gates", j)), [t], sem=ev)],
                  xk=xk)
        COL = self.arena(3072, 2, 4, 4)
        B_, A_, M_, F8 = GA[:, 0, :], GA[:, 1, :], GA[:, 2, :], GA[:, 5, :]

        def decays():
            after, done = Q.now(*ALL), []
            done += [Q.op("act", self.act(GA[:, 2, :], GA[:, 0, :], ACT.Abs), after)]
            done += [Q.op("dve", self.ts(GA[:, 3, :], GA[:, 0, :], 0.0, None, MIN), after)]
            done += [Q.op("pool", lambda: nc.gpsimd.memset(GA[:, 4, :], 1.0), after)]
            after, done = done, []
            yield
            done += [Q.op("act", self.act(GA[:, 2, :], GA[:, 2, :], ACT.Exp, scale=-1.0), after)]
            after, done = done, []
            yield
            done += [Q.op("act", self.act(GA[:, 2, :], GA[:, 2, :], ACT.Ln, bias=1.0), after)]
            after, done = done, []
            yield
            done += [Q.op("dve", self.tt(GA[:, 3, :], GA[:, 3, :], GA[:, 2, :], SUB), after)]
            after, done = done, []
            yield
            done += [Q.op("dve", lambda: nc.vector.tensor_tensor_scan(B_, GA[:, 4, :], GA[:, 3, :], 0.0, MUL, ADD), after)]
            after, done = done, []
            yield
            done += [Q.op("dve", self.tt(A_, A_, B_, SUB), after)]
            done += [Q.op("act", self.act(F8, B_, ACT.Copy, scale=-8.0), after)]
            after, done = done, []
            yield
            done += [Q.op("dve", lambda: nc.vector.tensor_tensor_scan(M_, A_, A_, 0.0, MAX, MAX), after)]
            after, done = done, []
            yield
            done += [Q.op("dve", self.tt(GA[:, 3, :], B_, M_, ADD), after)]
            after, done = done, []
            yield
            for t in range(NT):
                done += [Q.op("pe", self.tr(self.PS[4][:, 128 * t:128 * t + 128], A_[:, 128 * t:128 * t + 128]), after)]
                done += [Q.op("pe", self.tr(self.PS[5][:, 128 * t:128 * t + 128], GA[:, 3, 128 * t:128 * t + 128]), after)]
            after, done = done, []
            yield
            p4 = self.PS[4][:].rearrange("p (t r) -> p t r", t=4)[:, :, 64:68]
            p5 = self.PS[5][:].rearrange("p (t r) -> p t r", t=4)[:, :, 64:68]
            done += [Q.op("dve", self.cp(COL[:, 0], p4), after)]
            done += [Q.op("act", self.act(COL[:, 1], p5, ACT.Exp, scale=-1.0), after)]
            after, done = done, []
            yield

        self.side = decays()
        QT, VF = self.arena(3104, 8, S), self.arena(7200, 4, S)
        VB = self.arena(9248, 512)
        vb = Q.dma("b", lambda: nc.sync.dma_start(VB, self.fvb[:, 0:512]), Q.now(*ALL))
        base = at

        def evq(j, ps, t, ev):
            b = self.V("b_fq", j) if j < 4 else self.V("b_fk", j - 4)
            return [Q.op("act", self.act(QT[:, j, :], ps, ACT.Identity, bias=b), [t, *base], sem=ev)]

        self.gemm("w_in_2", 8, self.AH, self.AL, evq, deps=at)
        self.gemm_tm("w_in_2", 512, lambda t, ps, tok, ev: [Q.op("dve", self.tt(VF[:, t, :], ps, VB, ADD), [tok, *base, vb], sem=ev)],
                     deps=at)
        for _ in self.side:
            pass
        ATT, PP, PT = self.arena(9760, 4, S), self.arena(11808, 2, S), self.arena(12832, 2, S)
        ST4 = self.arena(13856, 4, 32)

        def add(i, h, ps, w):
            Q.op("pe", self.mm(ps[:, 0:w], self.C("ident")[:, h:h + 1].to_broadcast([128, 128]), F8[:, 0:w], False, False),
                 inc=False)
            return Q.op("pe", self.mm(ps[:, 128 * i:w], self.IDB[:], self.TRB[:, 0, :], False, True))

        self.attention(QT[:, 0:4, :], QT[:, 4:8, :], lambda j, h: VF[:, j, 64 * h:64 * h + 64], add, ATT, PP, PT, ST4,
                       Q.now(*ALL), 0.125)
        f = Q.now(*ALL)
        AT2 = self.arena(3104, 4, S)

        def eva(j, ps, tok, ev):
            return [Q.op("act", self.act(AT2[:, j, :], ps), [tok, *f], sem=ev)]

        self.transpose_to(lambda t, j: ATT[:, t, 128 * j:128 * j + 128], 4, eva)
        base = Q.now(*ALL)
        MU = self.arena(5152, 8, 515)
        U = self.arena(9272, 2, S)
        z = Q.op("pool", lambda: nc.gpsimd.memset(MU[:, :, 0:3], 0.0), base)
        ut = [[], []]
        prevs = {}

        def evm(j, ps, t, ev):
            a = Q.op("act", self.act(MU[:, j, 3:515], ps, ACT.Identity, bias=self.V("b_mu", j)), [t, *base], sem=ev)
            u = U[:, j % 2, :]
            for k in range(4):
                src, w = MU[:, j, k:k + 512], self.V("conv_w_2", 4 * j + k)
                if k == 0:
                    d = Q.op("dve", self.ts(u, src, w, self.V("conv_b_2", j), MUL, ADD), [a, z, *ut[-2]])
                else:
                    d = Q.op("dve", self.stt(u, src, w, u, MUL, ADD), [d])
            d = Q.op("act", self.act(u, u, ACT.Silu), [d])
            ut.append(self.split(u, self.HH[:, j, :], self.HL[:, j, :], [d, *base]))
            return [a]

        self.gemm("w_in_2", 8, self.AH, self.AL, evm, deps=at)
        VM = self.arena(9272 + 1024, 4, 4 * 257)
        VB2 = self.arena(9272, 1024)
        base = Q.now(*ALL)
        vb = Q.dma("b", lambda: nc.sync.dma_start(VB2, self.fvb[:, 512:1536]), base)
        V4 = VM.rearrange("p t (h e) -> p t h e", h=4)
        on = Q.op("dve", lambda: nc.vector.memset(V4[:, :, :, 256:257], 1.0), base)
        for c in range(2):
            def evv(t, ps, tok, ev, c=c):
                dst = V4[:, t, 2 * c:2 * c + 2, 0:256]
                vv = VB2[:, 512 * c:512 * c + 512].rearrange("p (h e) -> p h e", h=2)
                return [Q.op("dve", self.tt(dst, ps.rearrange("p (h e) -> p h e", h=2), vv, ADD), [tok, *base, vb, on], sem=ev)]
            self.gemm_tm("w_in_2", 512, evv, deps=at)
        MQK = self.arena(5152, 2, 4, S)
        base = Q.now(*ALL)
        for h in range(4):
            for i, n in enumerate(("w_mq_2", "w_mk_2")):
                self.gemm(n, 1, self.HH, self.HL,
                          lambda j, ps, t, ev, h=h, i=i: [Q.op("act", self.act(MQK[:, i, h, :], ps), [t, *base], sem=ev)],
                          deps=base, x0=2 * h)
        E_ = [self.arena(14408, S), self.arena(9272, S)]
        PK = [self.arena(14920, 1280), self.arena(1536, 1280)]
        at_s = [0, 512, 896, 1152]
        s_ = self.arena(16968, 32)
        SM = self.SC
        ob = [(self.g + t) % 4 for t in range(NT)]
        og = [(self.g + t) // 4 for t in range(NT)]
        O = [self.PS[b] for b in ob]
        start = Q.now(*ALL)
        used = [[start, start], [start, start]]
        parts, summed, emptied, ended = {}, {-2: start, -1: start}, start, start

        def scores(h):
            parts[h] = []
            for s in range(NT):
                w, t0, i = 512 - 128 * s, 128 * s, s % 2
                pa, pb = self.PS[4 + 2 * i], self.PS[5 + 2 * i]
                Q.op("pe", self.mm(pa[:, 0:w], self.C("ident")[:, 64 + h:65 + h].to_broadcast([128, 128]),
                                   M_[:, t0:512], True, False), used[i][0], inc=False)
                a = Q.op("pe", self.mm(pa[:, 0:128], self.IDB[:], self.TRB[:, 1, :], False, True))
                b = Q.op("pe", self.mm(pb[:, 0:w], MQK[:, 1, h, t0:t0 + 128], MQK[:, 0, h, t0:512]), used[i][1])
                a = Q.op("act", self.act(E_[i][:, 0:w], pa[:, 0:w], ACT.Exp, scale=-1.0, bias=COL[:, 0, s, h:h + 1]),
                         [a, *used[i][1]])
                b = Q.op("dve", self.stt(PK[h % 2][:, at_s[s]:at_s[s] + w], pb[:, 0:w], 128.0 ** -0.5, E_[i][:, 0:w], MUL, MUL),
                         [a, b, *summed[h - 2]])
                used[i] = [[a], [b]]
                parts[h].append(b)

        scores(0)
        for h in range(4):
            if h < 3:
                scores(h + 1)
            summed[h] = []
            for t in range(NT):
                for s in range(t + 1):
                    o = at_s[s] + 128 * (t - s)
                    d = Q.op("pe", self.mm(O[t][:, 0:257], PK[h % 2][:, o:o + 128], V4[:, s, h, :], s == 0, s == t),
                             [parts[h][s], *emptied, (f"ev{ob[t]}", og[t])], inc=s == t)
                summed[h].append(d)
            after, done = [*summed[h], *ended], []
            dn, ri = s_[:, 0:4], s_[:, 4:8]
            for t in range(NT):
                done += [Q.op("act", self.act(dn[:, t:t + 1], O[t][:, 256:257], ACT.Abs), after)]
            after, done = done, []
            done += [Q.op("dve", self.tt(dn, dn, COL[:, 1, :, h], MAX), after)]
            after, done = done, []
            done += [Q.op("dve", lambda: nc.vector.reciprocal(ri, dn), after)]
            after, done = done, []
            for t in range(NT):
                done += [Q.op("dve", self.ts(V4[:, t, h, 0:256], O[t][:, 0:256], ri[:, t:t + 1]), after,
                              sem=f"ev{ob[t]}" if h == 3 else None)]
            after, done, emptied = done, [], done
            bs = SM[:, 8:32].rearrange("p (t x) -> p t x", t=4)
            mv = SM[:, 32:40].rearrange("p (t x) -> p t x", t=4)
            for t in range(NT):
                done += [Q.op("dve", lambda t=t, h=h, bs=bs: nc.vector.bn_stats(bs[:, t, :], V4[:, t, h, 0:256]), after)]
            after, done = done, []
            for t in range(NT):
                done += [Q.op("dve", lambda t=t, bs=bs, mv=mv: nc.vector.bn_aggr(mv[:, t, :], bs[:, t, :]), after)]
            after, done = done, []
            rs = SM[:, 40:44]
            after = self.rstd(after, rs, mv[:, :, 1], 1.0, 1e-5)
            for t in range(NT):
                done += [Q.op("dve", self.ts(V4[:, t, h, 0:256], V4[:, t, h, 0:256], mv[:, t, 0:1], rs[:, t:t + 1], SUB, MUL), after)]
            ended = done
        self.g += NT
        HT = self.arena(5152, 8, S)
        SG = self.arena(14408, 2, S)
        base = Q.now(*ALL)
        tt_ = {}

        def evh(j, ps, tok, ev):
            tt_[j] = Q.op("dve", self.ts(HT[:, j, :], ps, self.V("mh_norm_g_2", j)), [tok, *base], sem=ev)
            return [tt_[j]]

        self.transpose_to(lambda t, j: V4[:, t, j // 2, 128 * (j % 2):128 * (j % 2) + 128], 8, evh)
        for j in range(8):
            Q.op("act" if j % 2 else "dve", self.act(self.XT[:, j, :], self.XT[:, j, :], ACT.Copy, scale=ALPHA) if j % 2
                 else self.ts(self.XT[:, j, :], self.XT[:, j, :], ALPHA), base)
        base = Q.now(*ALL)
        hold = [[], []]

        def evo(j, ps, t, ev):
            a = Q.op("act", self.act(SG[:, j % 2, :], ps, ACT.Sigmoid, bias=self.V("b_mo", j)), [t, *base, *hold[-2]], sem=ev)
            d = Q.op("dve", self.tt(HT[:, j, :], HT[:, j, :], SG[:, j % 2, :], MUL), [a])
            hold.append([d])
            return [a]

        self.gemm("w_in_2", 8, self.AH, self.AL, evo, deps=at)
        Y = self.arena(9272, 8, S)
        base = Q.now(*ALL)
        ak = [self.split(AT2[:, j, :], self.HH[:, j, :], self.HL[:, j, :], base) for j in range(4)]
        hold = [[], []]
        box = {}
        for j in range(8):
            def e1(_, ps, t, ev, j=j):
                box["g"] = Q.op("act", self.act(SG[:, j % 2, :], ps, ACT.Sigmoid, bias=self.V("b_ga", j)),
                                [t, *base, *hold[-2]], sem=ev)
                return [box["g"]]

            def e2(_, ps, t, ev, j=j):
                d = Q.op("dve", self.tt(Y[:, j, :], ps, SG[:, j % 2, :], MUL), [t, box["g"]], sem=ev)
                hold.append([d])
                return [d]

            self.gemm("w_in_2", 1, self.AH, self.AL, e1, deps=at)
            self.gemm("w_pa_2", 1, self.HH, self.HL, e2, xk=ak)
        base = Q.now(*ALL)
        hk = [self.split(HT[:, j, :], self.HH[:, j, :], self.HL[:, j, :], base) for j in range(8)]
        hold = [[], []]
        for j in range(8):
            def e3(_, ps, t, ev, j=j):
                box["g"] = Q.op("act", self.act(SG[:, j % 2, :], ps, ACT.Sigmoid, bias=self.V("b_gb", j)),
                                [t, *base, *hold[-2]], sem=ev)
                return [box["g"]]

            def e4(_, ps, t, ev, j=j):
                a = Q.op("dve", self.tt(SG[:, j % 2, :], ps, SG[:, j % 2, :], MUL), [t, box["g"]], sem=ev)
                d = Q.op("dve", self.tt(Y[:, j, :], Y[:, j, :], SG[:, j % 2, :], ADD), [a])
                hold.append([d])
                return [a]

            self.gemm("w_in_2", 1, self.AH, self.AL, e3, deps=at)
            self.gemm("w_pb_2", 1, self.HH, self.HL, e4, xk=hk)
        base = Q.now(*ALL)
        xk = [self.split(Y[:, j, :], self.AH[:, j, :], self.AL[:, j, :], base) for j in range(8)]
        evd, summed = self.summing(False, 0, self.residual_evac(lambda j: M[:, 16 + j:17 + j]))
        self.gemm("w_out_2", 8, self.AH, self.AL, evd, xk=xk)
        _, summed = self.stat([], self.XT, 8, 4, False, None, self.ln_x("ln1_g_2", "ln1_b_2", summed))
        xk = self.ln_mod(4, 3, summed)
        at = Q.now("pe", "act", "dve")
        for j in range(8):
            Q.op("act" if j % 2 else "dve", self.act(self.XT[:, j, :], self.XT[:, j, :], ACT.Copy, scale=ALPHA) if j % 2
                 else self.ts(self.XT[:, j, :], self.XT[:, j, :], ALPHA), at)
        summed = self.swiglu("w_ffn_in_2", "w_ffn_in_2", "w_ffn_down_2", lambda j: M[:, 40 + j:41 + j], 8192, [], xk, False)
        tmp = self.arena(6144, 2, S)
        _, summed = self.stat([], self.XT, 8, 4, True, tmp, self.ln_x("ln2_g_2", "ln2_b_2", summed))
        return summed

    def ln_mod(self, sc, sh, summed=None):
        M = self.MOD
        self.scaled(None, sc)
        after = self.Q.now(*ALL)
        XC, tmp, rs, v = self.arena(8192, 8, S), self.arena(12288, 2, S), self.arena(13312, S), self.arena(13824, 2, S)
        after = self.ln_center(after, self.XT, 8, 1024, XC, tmp, rs, 1e-5, summed)
        return self.affine(after, XC, 8, rs, lambda t: self.SC[:, t:t + 1], lambda t: M[:, 8 * sh + t:8 * sh + t + 1],
                           self.AH, self.AL, 0, tmp, v)

    def ln_x(self, g, b, summed):
        Q = self.Q
        after, each = Q.now(*ALL), []
        tmp, rs = self.arena(4096, 2, S), self.arena(5120, S)
        after = self.ln_center(after, self.XT, 8, 1024, self.XT, tmp, rs, 1e-5, summed)
        for t in range(8):
            a = Q.op("dve", self.tt(self.XT[:, t, :], self.XT[:, t, :], rs, MUL), after)
            each.append([Q.op("act", self.act(self.XT[:, t, :], self.XT[:, t, :], ACT.Identity, scale=self.V(g, t), bias=self.V(b, t)), [a])])
        return each

    def block3(self, summed):
        nc, Q = self.nc, self.Q
        one = 1.0
        xk = self.rms(self.XT, 8, 1024, 1e-6, 4096, lambda t: self.V("ffn1_norm_3", t), None, self.AH, self.AL, summed=summed)
        summed = self.swiglu("ffn1_w_gate_3", "ffn1_w_up_3", "ffn1_w_down_3", 0.5, 0, [], xk)
        xk = self.rms(self.XT, 8, 1024, 1e-6, 4096, lambda t: self.V("mix_norm_3", t), None, self.AH, self.AL, summed=summed)
        at = Q.now(*ALL)
        xs = self.xs.rearrange("(k p) t -> p k t", p=128)
        sp = Q.dma("spill", lambda: nc.sync.dma_start(xs, self.XT[:]), at)
        CU = self.arena(0, 4, 514)
        T_ = self.arena(2056, 4, S)
        z = Q.op("pool", lambda: nc.gpsimd.memset(CU[:, :, 0:2], 0.0), at)
        ct, cv = {}, {}

        def ec(j, ps, t, ev):
            if j < 4:
                ct[j] = Q.op("act", self.act(T_[:, j, :], ps), [t, *at], sem=ev)
                return [ct[j]]
            j -= 4
            u = Q.op("dve", self.tt(CU[:, j, 2:514], ps, T_[:, j, :], MUL), [t, ct[j]], sem=ev)
            d = Q.op("dve", self.ts(T_[:, j, :], CU[:, j, 0:512], self.V("conv_w_3", 3 * j)), [u, z])
            for k in (1, 2):
                d = Q.op("dve", self.stt(T_[:, j, :], CU[:, j, k:k + 512], self.V("conv_w_3", 3 * j + k), T_[:, j, :], MUL, ADD), [d])
            cv[j] = d
            return [u]

        self.gemm("w_in_3", 8, self.AH, self.AL, ec, xk=xk)

        def eb(j, ps, t, ev):
            d = Q.op("dve", self.tt(T_[:, j, :], ps, T_[:, j, :], MUL), [t, cv[j]], sem=ev)
            self.split(T_[:, j, :], self.HH[:, j, :], self.HL[:, j, :], [d, *at])
            return [d]

        self.gemm("w_in_3", 4, self.AH, self.AL, eb, deps=at)
        W = [self.arena(2048 * i, 4, S) for i in range(7)]
        R_, K_, V_, A_, B_, C_, G_ = W
        LO = self.XT[:, 0:2, :]
        PB = self.XT[:, 2:6, :].rearrange("p a b -> p (a b)")
        base = Q.now(*ALL) + [sp]
        z = Q.op("pool", lambda: nc.gpsimd.memset(PB[:, 0:1540], 0.0), base)
        hold = [[], []]

        def es(j, ps, t, ev):
            pb = PB[:, 514 * (j % 2):514 * (j % 2) + 513]
            tmp = PB[:, 1028:1540]
            a = Q.op("act", self.act(pb[:, 1:513], ps), [t, z, *base, *hold[-2]], sem=ev)
            d = Q.op("dve", self.tt(tmp, pb[:, 0:512], pb[:, 1:513], SUB), [a, z, *hold[-1]])
            dst = W[j // 4][:, j % 4, :] if j < 12 else LO[:, j - 12, :]
            d = Q.op("dve", self.stt(dst, tmp, self.V("mu_b_3", j), pb[:, 1:513], MUL, ADD), [d])
            hold.append([d])
            return [a]

        self.gemm("w_in_3", 14, self.AH, self.AL, es, deps=at)
        after, done = Q.now(*ALL), []
        done += [Q.op("act", self.act(LO[0:64, 0, :], LO[0:64, 0, :], ACT.Tanh), after)]
        done += [Q.op("act", self.act(LO[:, 1, :], LO[:, 1, :], ACT.Sigmoid), after)]
        after, done = done, []
        wl, _, wt = self.next_block("w_lora_3")
        wg, _, wt2 = self.next_block("w_gate_up_3")
        RST = self.CST[:, 128 * len(CONSTS) + 64:128 * len(CONSTS) + 576]
        EM = float(-np.exp(np.float32(-0.5)))
        start, left = [*after, *Q.now(*ALL)], [[], []]

        def prepare(j, p):
            SQ, N1 = self.XT[:, 2 + 3 * p:4 + 3 * p, :], self.XT[:, 4 + 3 * p, :]
            bank, b1, b2 = (self.PS[4 * p + i] for i in range(3))
            after, done = [*start, *left[p]], []
            c = slice(128 * j, 128 * j + 128)
            last = "blk" if j == 3 else None
            ta = Q.op("pe", self.mm(bank[:], wl[0:64, 0, c], LO[0:64, 0, :]), [*after, *wt])
            tb = Q.op("pe", self.mm(b1[:], wl[64:128, 0, c], LO[64:128, 0, :]), [*after, *wt], sem=last)
            tg = Q.op("pe", self.mm(b2[:], wg[:, 0, c], LO[:, 1, :]), [*after, *wt2], sem=last)
            done += [Q.op("act", self.act(C_[:, j, :], bank[:], ACT.Sigmoid, bias=self.V("w0_3", j)), [*after, ta])]
            done += [Q.op("act", self.act(B_[:, j, :], b1[:], ACT.Sigmoid, bias=self.V("a0_3", j)), [*after, tb])]
            done += [Q.op("dve", self.cp(G_[:, j, :], b2[:]), [*after, tg])]
            after, done = done, []
            yield
            done += [Q.op("dve", self.ts(C_[:, j, :], C_[:, j, :], EM), after)]
            done += [Q.op("dve", self.ts(A_[:, j, :], K_[:, j, :], self.V("k_k_3", j)), after)]
            after, done = done, []
            yield
            done += [Q.op("dve", lambda j=j: nc.vector.tensor_tensor_scan(C_[:, j, :], RST, C_[:, j, :], 0.0, MUL, ADD), after)]
            done += [Q.op("act", self.act(SQ[:, 0, :], A_[:, j, :], ACT.Square), after)]
            after, done = done, []
            yield
            done += [Q.op("pe", self.mm(bank[:], self.C("bd"), SQ[:, 0, :]), after)]
            done += [Q.op("dve", self.ts(SQ[:, 1, :], B_[:, j, :], -1.0, self.V("k_a_3", j), ADD, MUL), after)]
            after, done = done, []
            yield
            done += [Q.op("act", self.act(N1, bank[:], ACT.Sqrt), after)]
            done += [Q.op("dve", self.stt(K_[:, j, :], SQ[:, 1, :], 1.0, K_[:, j, :], ADD, MUL), after)]
            after, done = done, []
            yield
            done += [Q.op("dve", self.ts(N1, N1, 1e-12, None, MAX), after)]
            after, done = done, []
            yield
            done += [Q.op("dve", lambda: nc.vector.reciprocal(N1, N1), after)]
            after, done = done, []
            yield
            done += [Q.op("dve", self.stt(A_[:, j, :], A_[:, j, :], -1.0, N1, MUL, MUL), after)]
            after, done = done, []
            yield
            done += [Q.op("dve", self.stt(B_[:, j, :], A_[:, j, :], -1.0, B_[:, j, :], MUL, MUL), after)]
            after, done = done, []
            yield
            left[p] = after

        self.abreast([lambda p, j=j: prepare(j, p) for j in range(4)], 2)
        ys = self.ys.rearrange("(k p) t -> p k t", p=128)

        def conv_half():
            gate, base = {}, Q.now(*ALL)
            sent = [[]]
            for j in range(8):
                def e1(_, ps, t, ev, j=j):
                    gate[j] = Q.op("act", self.act(RST, ps, ACT.Sigmoid), [t, *base, *sent[-1]], sem=ev)

                def e2(_, ps, t, ev, j=j):
                    a = Q.op("dve", self.tt(RST, ps, RST, MUL), [t, gate[j]], sem=ev)
                    sent.append([Q.dma("ys", lambda: nc.sync.dma_start(ys[:, j, :], RST), [a])])

                yield from self.gemm_steps("w_in_3", 1, self.AH, self.AL, e1, deps=base, banks=(2, 3))
                yield from self.gemm_steps("w_out_a_3", 1, self.HH, self.HL, e2, deps=base, banks=(2, 3))

        beside = conv_half()
        self.rwkv(W, beside)
        for _ in beside:
            pass
        start, left, Y = Q.now(*ALL), [[], []], A_
        merged = self.arena(8192, 8, S)
        Q.dma("ym", lambda: nc.sync.dma_start(merged, ys), [*start, *Q.now("ys")])

        def normed(j, p):
            T1, T2, T3 = (self.XT[:, 4 * p + i, :] for i in range(3))
            b0, b1, b2 = (self.PS[4 * p + i] for i in range(3))
            after, done = [*start, *left[p]], []
            done += [Q.op("pe", self.mm(b0[:], self.C("bd"), Y[:, j, :]), after)]
            done += [Q.op("dve", self.tt(T3, R_[:, j, :], K_[:, j, :], MUL), after)]
            after, done = done, []
            yield
            done += [Q.op("dve", self.stt(Y[:, j, :], b0[:], -1.0 / 64, Y[:, j, :], MUL, ADD), after)]
            done += [Q.op("act", self.act(T3, T3, ACT.Copy, scale=self.V("r_k_3", j)), after)]
            after, done = done, []
            yield
            done += [Q.op("act", self.act(T1, Y[:, j, :], ACT.Square), after)]
            done += [Q.op("pe", self.mm(b2[:], self.C("bd"), T3), after)]
            after, done = done, []
            yield
            done += [Q.op("pe", self.mm(b1[:], self.C("bd"), T1), after)]
            done += [Q.op("dve", self.tt(T3, b2[:], V_[:, j, :], MUL), after)]
            after, done = done, []
            yield
            after = self.rstd(after, T2, b1[:], 1.0 / 64, 64e-5)
            yield
            done += [Q.op("dve", self.tt(Y[:, j, :], Y[:, j, :], T2, MUL), after)]
            after, done = done, []
            yield
            done += [Q.op("dve", self.ts(Y[:, j, :], Y[:, j, :], self.V("ln_x_w_3", j), self.V("ln_x_b_3", j), MUL, ADD), after)]
            after, done = done, []
            yield
            done += [Q.op("dve", self.tt(Y[:, j, :], Y[:, j, :], T3, ADD), after)]
            after, done = done, []
            yield
            done += [Q.op("dve", self.tt(Y[:, j, :], Y[:, j, :], G_[:, j, :], MUL), after)]
            after, done = done, []
            yield
            left[p] = self.split(Y[:, j, :], self.HH[:, 4 + j, :], self.HL[:, 4 + j, :], after)

        self.abreast([lambda p, j=j: normed(j, p) for j in range(4)], 2)
        xr = Q.dma("spill", lambda: nc.sync.dma_start(self.XT[:], xs), Q.now(*ALL))
        Y = merged
        SG = self.arena(4096, 2, S)
        box = {}
        hold = [[], []]
        base = Q.now(*ALL, "ym")
        for j in range(8):
            def e3(_, ps, t, ev, j=j):
                box["g"] = Q.op("act", self.act(SG[:, j % 2, :], ps, ACT.Sigmoid), [t, *base, *hold[-2]], sem=ev)
                return [box["g"]]

            def e4(_, ps, t, ev, j=j):
                a = Q.op("dve", self.tt(SG[:, j % 2, :], ps, SG[:, j % 2, :], MUL), [t, box["g"]], sem=ev)
                d = Q.op("dve", self.tt(Y[:, j, :], Y[:, j, :], SG[:, j % 2, :], ADD), [a])
                hold.append([d])
                return [a]

            self.gemm("w_in_3", 1, self.AH, self.AL, e3, deps=base)
            self.gemm("w_out_b_3", 1, self.HH, self.HL, e4, deps=base, x0=4)
        base = Q.now(*ALL) + [xr]
        xk = [self.split(Y[:, j, :], self.AH[:, j, :], self.AL[:, j, :], base) for j in range(8)]
        evd, summed = self.summing(True, 6144, self.residual_evac(one))
        self.gemm("w_o_3", 8, self.AH, self.AL, evd, xk=xk)
        xk = self.rms(self.XT, 8, 1024, 1e-6, 4096, lambda t: self.V("ffn2_norm_3", t), None, self.AH, self.AL, summed=summed)
        after = self.swiglu("ffn2_w_gate_3", "ffn2_w_up_3", "ffn2_w_down_3", 0.5, 0, [], xk)
        rs, done = self.arena(4096, S), []
        after = self.rstd([*after, *Q.now(*ALL)], rs, self.PS[4][:], 1.0 / 1024, 1e-6)
        for t in range(8):
            done += [[Q.op("dve", self.stt(self.XT[:, t, :], self.XT[:, t, :], self.V("final_norm_3", t), rs, MUL, MUL), after)]]
        return done

    def abreast(self, jobs, places):
        live, n = {}, 0
        while n < len(jobs) or live:
            for p in range(places):
                if p not in live and n < len(jobs):
                    live[p] = jobs[n](p)
                    n += 1
                if p in live and next(live[p], "end") == "end":
                    del live[p]

    def rwkv(self, W, beside):
        base = self.Q.now(*ALL)
        ZB = self.XT[:, 0, :].rearrange("p (a b) -> p a b", a=4)
        z = self.Q.op("dve", lambda: self.nc.vector.memset(ZB, 0.0), base)
        jobs = [(t, p) for t in range(NT) for p in range(4)]
        ends = [[], [], [], [], [], []]
        live = []
        free = [0, 1]
        turn = 0
        while jobs or live:
            while free and jobs:
                s = free.pop(0)
                t, p = jobs.pop(0)
                live.append((s, p, self.rwkv_pair(W, t, p, s, ZB, ends, base + [z])))
            nxt = []
            for s, p, g in live:
                try:
                    next(g)
                    nxt.append((s, p, g))
                    turn += 1
                    if turn % 5 == 0:
                        next(beside, None)
                except StopIteration:
                    free.append(s)
            live = nxt

    def rwkv_pair(self, W, tt_, p, s, ZB, ends, base):
        nc, Q, C = self.nc, self.Q, self.C
        R_, K_, V_, A_, B_, C_, G_ = W
        t0 = 128 * tt_
        sl = slice(t0, t0 + 128)
        after, done = base + ends[4 + s], []
        xf = self.XT[:].rearrange("p a b -> p (a b)")
        area = xf[:, 512 + 1792 * s:512 + 1792 * s + 1792]
        pos = [0]
        more = self.arena(14336 + 1536 * s, 1536)

        def alloc(*shape):
            n = int(np.prod(shape))
            o = pos[0]
            if o < 1792 and o + n > 1792:
                o = 1792
            src, oo = (area, o) if o < 1792 else (more, o - 1792)
            assert oo + n <= (1792 if o < 1792 else 1536), (o, n)
            pos[0] = o + n
            ap = src[:, oo:oo + n]
            if len(shape) == 2:
                return ap.rearrange("p (a b) -> p a b", a=shape[0])
            if len(shape) == 3:
                return ap.rearrange("p (a b c) -> p a b c", a=shape[0], b=shape[1])
            return ap

        PB = [self.PS[b] for b in ((0, 1, 4), (5, 6, 7))[s]]
        MT4 = alloc(2, 4, 128)
        PP = alloc(2, 128)
        TT = alloc(2, 128)
        ARt = alloc(2, 128)
        BK = alloc(2, 128)
        BKh = alloc(2, 128)
        EX = alloc(2, 65)
        TK = alloc(4, 128)
        p16 = [BK, BKh, alloc(2, 128)]
        E2 = p16[2][:, 0, :]
        c2 = C_[:, p, sl].rearrange("p (c t) -> p c t", c=2)
        c1 = C_[:, p, sl]
        done += [Q.op("dve", lambda: nc.vector.memset(EX[:, :, 0:1], 1.0), after)]
        done += [Q.op("act", self.act(EX[:, :, 1:65], c2, ACT.Exp), after)]
        done += [Q.op("act", self.act(E2, c1, ACT.Exp, scale=-1.0), after)]
        after, done = done, []
        yield
        eh = p16[2][:, 1, :]
        done += [Q.op("dve", self.tt(ARt[:, 0, :].rearrange("p (c t) -> p c t", c=2), A_[:, p, sl].rearrange("p (c t) -> p c t", c=2),
                          EX[:, :, 0:64], MUL), after)]
        done += [Q.op("dve", self.tt(ARt[:, 1, :].rearrange("p (c t) -> p c t", c=2), R_[:, p, sl].rearrange("p (c t) -> p c t", c=2),
                          EX[:, :, 1:65], MUL), after)]
        done += [Q.op("dve", self.tt(BK[:, 0, :], B_[:, p, sl], E2, MUL), after)]
        done += [Q.op("dve", self.tt(BK[:, 1, :], K_[:, p, sl], E2, MUL), after)]
        for c in range(2):
            done += [Q.op("act", self.act(eh[:, 64 * c:64 * c + 64], c2[:, c, :], ACT.Exp, scale=-1.0,
                               bias=C_[:, p, t0 + 64 * c + 63:t0 + 64 * c + 64]), after)]
        after, done = done, []
        yield
        done += [Q.op("dve", self.tt(BKh[:, 0, :], B_[:, p, sl], eh, MUL), after)]
        done += [Q.op("dve", self.tt(BKh[:, 1, :], K_[:, p, sl], eh, MUL), after)]
        for h in range(2):
            q = slice(64 * h, 64 * h + 64)
            for i in range(2):
                done += [Q.op("pe", self.mm(PB[h][:, 256 * i:256 * i + 256], BK[q, i, :], ARt[q, :, :].rearrange("p a b -> p (a b)")), after)]
            if h == 0:
                done += [Q.op("pe", self.mm(PB[2][:, 0:128], ARt[q, 0, :], BK[q, 0, :]), after)]
        after, done = done, []
        yield
        mk = self.CST[:, 128 * CONSTS.index("SLT"):128 * CONSTS.index("SLT") + 256].unsqueeze(1).to_broadcast([128, 2, 256])
        for h in range(2):
            done += [Q.op("dve", self.tt(MT4[:, h].rearrange("p a b -> p (a b)").rearrange("p (a b) -> p a b", a=2),
                              PB[h][:].rearrange("p (a b) -> p a b", a=2), mk, MUL), after)]
        a = Q.op("dve", self.tt(PP[:, 0, :], PB[2][:, 0:128], C("SL"), MUL), after)
        second = Q.op("pe", self.mm(PB[2][:, 128:256], ARt[64:128, 0, :], BK[64:128, 0, :]), [*after, a])
        after, done = [*done, a], []
        yield
        for i, x in enumerate((ARt[:, 0, :], BKh[:, 0, :], BKh[:, 1, :], V_[:, p, sl])):
            done += [Q.op("pe", self.tr(PB[0][:, 128 * i:128 * i + 128], x), after)]
        after, done = done, []
        yield
        done += [Q.op("act", self.act(TK.rearrange("p a b -> p (a b)"), PB[0][:]), after)]
        after.append(Q.op("dve", self.tt(PP[:, 1, :], PB[2][:, 128:256], C("SL"), MUL), [*after, second]))
        bc = lambda m: C(m).unsqueeze(1).to_broadcast([128, 2, 128])
        x, xt, y = p16
        done += [Q.op("dve", self.tt(x, PP, bc("m16"), MUL), after)]
        done += [Q.op("dve", self.tt(xt, MT4[:, :, 0, :], bc("m16T"), MUL), after)]
        after, done = done, []
        done += [Q.op("dve", self.tt(TT, xt, bc("ident"), ADD), after)]
        X, XT_ = x, xt
        for lev in range(3):
            for h in range(2):
                done += [Q.op("pe", self.mm(PB[1][:, 128 * h:128 * h + 128], XT_[:, h, :], X[:, h, :]), after)]
                if lev < 2:
                    done += [Q.op("pe", self.mm(PB[2][:, 128 * h:128 * h + 128], X[:, h, :], XT_[:, h, :]), after)]
            after, done = done, []
            yield
            pv = lambda b: PB[b][:, 0:256].rearrange("p (a b) -> p a b", a=2)
            done += [Q.op("act", self.act(X, pv(1)), after)]
            if lev < 2:
                done += [Q.op("dve", self.cp(XT_, pv(2)), after)]
            after, done = done, []
            yield
            for h in range(2):
                done += [Q.op("pe", self.mm(PB[0][:, 128 * h:128 * h + 128], X[:, h, :], TT[:, h, :]), after)]
            after, done = done, []
            yield
            done += [Q.op("dve", self.tt(TT, pv(0), TT, ADD), after)]
            after, done = done, []
            yield
        L, Xx, D = x, xt, y
        for name in ("L32", "L64"):
            done += [Q.op("dve", self.tt(L, PP, bc(name), MUL), after)]
            for h in range(2):
                done += [Q.op("pe", self.tr(PB[1][:, 128 * h:128 * h + 128], TT[:, h, :]), after)]
            after, done = done, []
            yield
            done += [Q.op("act", self.act(D, pv(1)), after)]
            for h in range(2):
                done += [Q.op("pe", self.mm(PB[2][:, 128 * h:128 * h + 128], L[:, h, :], TT[:, h, :]), after)]
            after, done = done, []
            yield
            done += [Q.op("dve", self.cp(Xx, pv(2)), after)]
            after, done = done, []
            yield
            for h in range(2):
                done += [Q.op("pe", self.mm(PB[0][:, 128 * h:128 * h + 128], D[:, h, :], Xx[:, h, :]), after)]
            after, done = done, []
            yield
            done += [Q.op("dve", self.tt(TT, pv(0), TT, ADD), after)]
            after, done = done, []
            yield
        U, AS = x, xt
        hs = lambda h: slice(64 * h, 64 * h + 64)
        for h in range(2):
            done += [Q.op("pe", self.mm(PB[1][:, hs(h)], MT4[:, h, 2, :], TK[:, 3, hs(h)]), after)]
        after, done = done, []
        yield
        done += [Q.op("act", self.act(U[:, 0, :], PB[1][:, 0:128]), after)]
        after, done = done, []
        for h in range(2):
            done += [Q.op("pe", self.mm(PB[2][:, hs(h)], TT[:, h, :], TK[:, 0, hs(h)]), after)]
            done += [Q.op("pe", self.mm(PB[2][:, 128 + 64 * h:192 + 64 * h], TT[:, h, :], U[:, 0, hs(h)]), after)]
        after, done = done, []
        yield
        done += [Q.op("dve", self.cp(AS, PB[2][:, 0:256].rearrange("p (a b) -> p a b", a=2)), after)]
        after, done = done, []
        yield
        MG = MT4[:, 0]
        for c in range(2):
            q = slice(64 * c, 64 * c + 64)
            done += [Q.op("pe", self.mm(PB[c][:, 0:128], AS[q, 0, :], TK[q, 1, :]), after)]
            Q.op("pe", self.mm(PB[c][:, 128:256], TK[q, 1, :], AS[q, 1, :], True, False), after, inc=False)
            done += [Q.op("pe", self.mm(PB[c][:, 128:256], TK[q, 2, :], TK[q, 3, :], False, True), after)]
        for h in range(2):
            o = hs(h)
            done += [Q.op("pe", self.mm(PB[2][o, 0:128], AS[:, 0, hs(h)], MT4[:, h, 1, :]), after)]
            Q.op("pe", self.mm(PB[2][o, 128:256], AS[:, 1, hs(h)], MT4[:, h, 1, :], True, False), after, inc=False)
            done += [Q.op("pe", self.mm(PB[2][o, 128:256], TK[:, 3, hs(h)], MT4[:, h, 3, :], False, True), after)]
        after, done = done, []
        yield
        mg = MT4.rearrange("p h a b -> p (h a) b")[:, 0:4, :]
        bd2 = C("bd").unsqueeze(1).to_broadcast([128, 2, 128])
        for c in range(2):
            done += [Q.op("dve", self.tt(mg[:, 2 * c:2 * c + 2, :], PB[c][:, 0:256].rearrange("p (a b) -> p a b", a=2), bd2, MUL), after)]
        qt, y0 = y[:, 0, :], y[:, 1, :]
        done += [Q.op("dve", self.tt(qt, PB[2][:, 0:128], ARt[:, 1, :], ADD), after)]
        done += [Q.op("dve", self.cp(y0, PB[2][:, 128:256]), after)]
        after, done = done, []
        yield
        for c in range(2):
            done += [Q.op("dve", self.stt(mg[:, 2 * c, :], C("ident"), EX[:, c, 64:65], mg[:, 2 * c, :], MUL, ADD), after)]
        after, done = done, []
        yield
        ze = ends[p]
        for c in range(2):
            done += [Q.op("pe", self.mm(PB[2][:, 256 + 128 * c:320 + 128 * c], ZB[:, p, :], qt[:, 64 * c:64 * c + 64]), [*after, *ze])]
            done += [Q.op("pe", self.mm(PB[1][:, 0:128], mg[:, 2 * c, :], ZB[:, p, :]), [*after, *ze])]
            after, done = done, []
            yield
            done += [Q.op("dve", self.tt(ZB[:, p, :], PB[1][:, 0:128], mg[:, 2 * c + 1, :], ADD), after)]
            done += [Q.op("dve", self.tt(A_[:, p, t0 + 64 * c:t0 + 64 * c + 64], PB[2][:, 256 + 128 * c:320 + 128 * c],
                              y0[:, 64 * c:64 * c + 64], ADD), after)]
            after, done = done, []
            yield
        ends[p] = ends[4 + s] = after


ARENA = 17408
STOP = 3
START = 1
ALPHA = 2.0 ** 0.25


def bass_program(nc, xin, wst, vec, cst, fvb, cbd, out):
    with ExitStack() as ctx:
        K = Program(nc, ctx, xin, wst, vec, cst, fvb, cbd, out)
        K.build()
        names = set(K.Q.n) | {"pe", "act", "dve", "pool", "sp"}
        sems = {n: ctx.enter_context(nc.semaphore("s_" + n)) for n in sorted(names)}
        block = ctx.enter_context(nc.Block())

        @block.sync
        def _(eng):
            K.Q.play("sp", eng, sems)

        @block.tensor
        def _(eng):
            K.Q.play("pe", eng, sems)

        @block.scalar
        def _(eng):
            K.Q.play("act", eng, sems)

        @block.vector
        def _(eng):
            K.Q.play("dve", eng, sems)

        @block.gpsimd
        def _(eng):
            K.Q.play("pool", eng, sems)


def lay_out(inp):
    x = {k: np.asarray(v) for k, v in inp.items()}
    w = {k: (v[0] if v.ndim >= 3 else v) for k, v in x.items()}
    g = np.zeros((1024, 256), np.float32)
    g[:, 0:8] = w["w_in_2"][:, 1536:1544]
    g[:, 64:68] = w["w_in_2"][:, 3596:3600]
    g[:, 192:196] = w["w_in_2"][:, 3592:3596]
    w["w_gates_2"] = g
    w["w_lora_3"] = np.concatenate([w["w_decay_up_3"], w["w_iclr_up_3"]], 0)
    slots = plan()
    ws = np.zeros((len(slots), 128, SLOT), np.float32)
    for i, (kind, blocks) in enumerate(slots):
        o = 0
        for name, r0, nk, c0, nc_ in blocks:
            if kind == "ada":
                ws[i, :, o:o + 1024] = w[name][:, c0:c0 + 128].T
                o += 1024
                continue
            if name in ("w_mq_2", "w_mk_2"):
                a = w[name][r0]
            else:
                a = w[name][r0:r0 + 128 * nk, c0:c0 + nc_]
            ws[i, :, o:o + nk * nc_] = a.reshape(nk, 128, nc_).transpose(1, 0, 2).reshape(128, nk * nc_)
            o += nk * nc_
    b2 = x["b_in_2"][0]
    bg = np.zeros(256, np.float32)
    bg[0:8], bg[64:68], bg[192:196] = b2[1536:1544], b2[3596:3600], b2[3592:3596]
    extra = {"b_fq": b2[0:512], "b_fk": b2[512:1024], "b_mu": b2[1544:2568], "b_mo": b2[3600:4624],
             "b_ga": b2[4624:5648], "b_gb": b2[5648:6672], "b_gates": bg}
    cols = []
    for n, k in VECS:
        if n in ("g_q", "g_k"):
            cols.append(np.broadcast_to(x[n].reshape(1, 64), (128, 64)))
        elif n in ("w_dw", "conv_w_2", "conv_w_3"):
            a = x[n][0]
            cols.append(a.reshape(a.shape[0], -1, 128).transpose(2, 1, 0).reshape(128, k))
        else:
            a = extra[n] if n in extra else x[n]
            cols.append(a.reshape(k, 128).T)
    vec = np.ascontiguousarray(np.concatenate(cols, 1))
    fvb = np.ascontiguousarray(np.broadcast_to(np.concatenate([b2[1024:1536], b2[2568:3592]])[None], (128, 1536)))
    xin = np.ascontiguousarray(x["x"][0].T)
    cbd = np.ascontiguousarray(np.stack([np.broadcast_to(x[n].reshape(1, 1024), (128, 1024)) for n in ("c", "c_2")]))
    return {"xin": xin, "wst": ws, "vec": vec, "cst": const_array(), "fvb": fvb, "cbd": cbd}


def kernel(**inputs):
    import concourse.bacc as _bacc
    from concourse.bass_utils import run_bass_kernel_spmd as _run

    nc = _bacc.Bacc("TRN2", target_bir_lowering=False, num_devices=1)
    arrays, args = {}, []
    for name, a in lay_out(inputs).items():
        arrays[f"in_{name}_dram"] = a
        args.append(nc.dram_tensor(f"in_{name}_dram", a.shape, mybir.dt.from_np(a.dtype), kind="ExternalInput").ap())
    args.append(nc.dram_tensor("out_0_dram", (1024, S), F32, kind="ExternalOutput").ap())
    bass_program(nc, *args)
    r = _run(nc, [arrays], core_ids=[0])
    return np.ascontiguousarray(r.results[0]["out_0_dram"].T)[None]
```
